# Optimizing a Trainium2 kernel written in Bass

```python
import math
import jax, jax.numpy as jnp
from jax import lax
import numpy as np

D_MODEL = 1024
BATCH = 1
SEQ = 256
DEPTH = 1

CTX_LEN = 256
GRID_W = 64
A_HEADS = 4
A_DK = 128
A_DV = 128
A_KW = A_HEADS * A_DK
A_VW = A_HEADS * A_DV
A_CHUNK = 64
B_WIDTH = 512
HYENA_ORDER = 2
HYENA_SHORT = 3
HYENA_EMB = 33
HYENA_BANDS = (HYENA_EMB - 1) // 2
HYENA_FFN = 64
HYENA_FAST_DECAY = 0.3
HYENA_SLOW_DECAY = 1.5
HYENA_TARGET = 1e-2
HYENA_SHIFT = 0.05
HYENA_L1_EPS = 1e-6
D_FF = 2816
N_MOD = 9
RMS_EPS = 1e-6
COL_V = 0
COL_FFW = COL_V + A_VW
COL_FBW = COL_FFW + A_KW
COL_Q = COL_FBW + A_KW
COL_G = COL_Q + A_KW
COL_HY = COL_G + A_VW
COL_MERGE = COL_HY + 3 * B_WIDTH
IN_COLS = COL_MERGE + 2 * D_MODEL


def rms_norm(x):
    xf = x.astype(jnp.float32)
    return (xf * lax.rsqrt(jnp.mean(xf * xf, axis=-1, keepdims=True) + RMS_EPS)).astype(x.dtype)

def modulate(x, shift, scale):
    return x * (1.0 + scale) + shift

def swiglu(x, wg, wu, wd):
    return (jax.nn.silu(x @ wg) * (x @ wu)) @ wd

def half_ffn(h, shift, scale, gate, wg, wu, wd):
    return h + 0.5 * gate * swiglu(modulate(rms_norm(h), shift, scale), wg, wu, wd)

def grid_pos_embed(n_tokens):
    rows = n_tokens // GRID_W
    quarter = D_MODEL // 4
    omega = 1.0 / (10000.0 ** (jnp.arange(quarter, dtype=jnp.float32) / quarter))
    ar = jnp.arange(rows, dtype=jnp.float32)[:, None] * omega
    ac = jnp.arange(GRID_W, dtype=jnp.float32)[:, None] * omega
    er = jnp.concatenate([jnp.sin(ar), jnp.cos(ar)], axis=-1)
    ec = jnp.concatenate([jnp.sin(ac), jnp.cos(ac)], axis=-1)
    emb = jnp.concatenate([jnp.broadcast_to(er[:, None, :], (rows, GRID_W, D_MODEL // 2)),
                           jnp.broadcast_to(ec[None, :, :], (rows, GRID_W, D_MODEL // 2))], axis=-1)
    return emb.reshape(rows * GRID_W, D_MODEL)

def to_heads(a):
    b, l, w = a.shape
    return a.reshape(b, l, A_HEADS, w // A_HEADS).transpose(0, 2, 1, 3)

def hgrn2_forget(z, lb):
    f = lb + (1.0 - lb) * jax.nn.sigmoid(z.astype(jnp.float32))
    return to_heads(jnp.log(f)), to_heads(1.0 - f)

def hgrn2_chunk_scan(q, k, v, logf, s0):
    b, h, l, dk = q.shape
    n_chunks = l // A_CHUNK

    def to_chunks(a):
        return a.reshape(b, h, n_chunks, A_CHUNK, a.shape[-1]).transpose(2, 0, 1, 3, 4)

    within_scan = jnp.tril(jnp.ones((A_CHUNK, A_CHUNK), dtype=bool))[:, :, None]

    def step(s, inp):
        qb, kb, vb, gb = inp
        cum = jnp.cumsum(gb, axis=2)
        diff = cum[:, :, :, None, :] - cum[:, :, None, :, :]
        decay = jnp.exp(jnp.where(within_scan, diff, -jnp.inf))
        scores = jnp.einsum('bhtsd,bhsd->bhts', qb[:, :, :, None, :] * decay, kb)
        o = scores @ vb + (qb * jnp.exp(cum)) @ s
        last = cum[:, :, -1:, :]
        s_new = jnp.exp(last[:, :, 0, :])[..., None] * s + jnp.einsum('bhsd,bhse->bhde', kb * jnp.exp(last - cum), vb)
        return s_new, o

    s_final, oc = lax.scan(step, s0, (to_chunks(q), to_chunks(k), to_chunks(v), to_chunks(logf)))
    o = oc.transpose(1, 2, 0, 3, 4).reshape(b, h, l, v.shape[-1])
    return o, s_final

def hgrn2_final_state(k, v, logf):
    cum = jnp.cumsum(logf, axis=2)
    return jnp.einsum('bhld,bhle->bhde', k * jnp.exp(cum[:, :, -1:, :] - cum), v)

def flip_seq(a):
    return jnp.flip(a, axis=2)

def hgrn2_bidir(q, v, logf_fw, k_fw, logf_bw, k_bw, s0_fw, s0_bw):
    o_fw, s_fw = hgrn2_chunk_scan(q, k_fw, v, logf_fw, s0_fw)
    o_bw, s_bw = hgrn2_chunk_scan(flip_seq(q), flip_seq(k_bw), flip_seq(v), flip_seq(logf_bw), s0_bw)
    return o_fw + flip_seq(o_bw), s_fw, s_bw

def context_states(nc, w_in, lb):
    p = nc @ w_in[:, :COL_Q]
    v = to_heads(p[..., COL_V:COL_FFW]).astype(jnp.float32)
    logf_fw, k_fw = hgrn2_forget(p[..., COL_FFW:COL_FBW], lb[0])
    logf_bw, k_bw = hgrn2_forget(p[..., COL_FBW:COL_Q], lb[1])
    s_fw = hgrn2_final_state(k_fw, v, logf_fw)
    s_bw = hgrn2_final_state(flip_seq(k_bw), flip_seq(v), flip_seq(logf_bw))
    return s_fw, s_bw

def short_conv(u, w, bias):
    l = u.shape[1]
    pad = HYENA_SHORT // 2
    up = jnp.pad(u, ((0, 0), (pad, pad), (0, 0)))
    out = bias
    for j in range(HYENA_SHORT):
        out = out + up[:, j:j + l] * w[j]
    return out

def hyena_pos_features(l):
    p = jnp.arange(l, dtype=jnp.float32)
    t = p / (l - 1)
    w = 2.0 * math.pi * p / l
    f = jnp.linspace(1e-4, HYENA_BANDS - 1, HYENA_BANDS, dtype=jnp.float32)
    ang = w[:, None] * f[None, :]
    z = jnp.concatenate([t[:, None], jnp.cos(ang), -jnp.sin(ang)], axis=-1)
    return t, z

def hyena_kernels(l, w1, b1, fr1, w2, b2, fr2, w3):
    t, z = hyena_pos_features(l)
    h = jnp.sin(fr1 * (z @ w1 + b1))
    h = jnp.sin(fr2 * (h @ w2 + b2))
    h = (h @ w3).astype(jnp.float32).reshape(l, HYENA_ORDER, 2, B_WIDTH)
    max_decay = math.log(HYENA_TARGET) / HYENA_FAST_DECAY
    min_decay = math.log(HYENA_TARGET) / HYENA_SLOW_DECAY
    deltas = jnp.abs(jnp.linspace(min_decay, max_decay, B_WIDTH, dtype=jnp.float32))
    window = jnp.exp(-t[:, None] * deltas[None, :]) + HYENA_SHIFT
    h = h * window[:, None, None, :]
    kern = jnp.concatenate([h[:, :, 0], jnp.flip(h[:, :, 1], axis=0)], axis=0)
    return kern / (jnp.sum(jnp.abs(kern), axis=0, keepdims=True) + HYENA_L1_EPS)

def fft_conv(u, kern):
    l = u.shape[1]
    uf = jnp.fft.rfft(u.astype(jnp.float32), n=2 * l, axis=1)
    kf = jnp.fft.rfft(kern, n=2 * l, axis=0)
    return jnp.fft.irfft(uf * kf[None], n=2 * l, axis=1)[:, :l]

def hyena(u3, kern, hy_bias):
    v, x1, x2 = jnp.split(u3, 3, axis=-1)
    z = v
    for o, gate in enumerate((x1, x2)):
        z = gate * (fft_conv(z, kern[:, o]).astype(z.dtype) + hy_bias[o] * z)
    return z

def token_mixers(n, s0_fw, s0_bw, kern, w_in, lb, a_norm_w, conv_w, conv_b, hy_bias, w_pa, w_pb, w_out):
    b, l, _ = n.shape
    p = n @ w_in
    v = to_heads(p[..., COL_V:COL_FFW]).astype(jnp.float32)
    logf_fw, k_fw = hgrn2_forget(p[..., COL_FFW:COL_FBW], lb[0])
    logf_bw, k_bw = hgrn2_forget(p[..., COL_FBW:COL_Q], lb[1])
    q = to_heads(jax.nn.silu(p[..., COL_Q:COL_G])).astype(jnp.float32)
    o, s_fw, s_bw = hgrn2_bidir(q, v, logf_fw, k_fw, logf_bw, k_bw, s0_fw, s0_bw)
    o = rms_norm(o.transpose(0, 2, 1, 3)) * a_norm_w
    o_a = o.reshape(b, l, A_VW).astype(n.dtype) * jax.nn.silu(p[..., COL_G:COL_HY])
    u3 = short_conv(p[..., COL_HY:COL_MERGE], conv_w, conv_b)
    o_b = hyena(u3, kern, hy_bias)
    g_a, g_b = jnp.split(p[..., COL_MERGE:], 2, axis=-1)
    y = jax.nn.sigmoid(g_a) * (o_a @ w_pa) + jax.nn.sigmoid(g_b) * (o_b @ w_pb)
    return y @ w_out, s_fw, s_bw

def first_inputs(seed: int = 0) -> dict:
    key = jax.random.key(seed)
    ks = jax.random.split(key, 32)
    nrm = jax.random.normal
    f32 = jnp.float32
    d = D_MODEL
    return {
        'x': nrm(ks[0], (BATCH, SEQ, d), f32),
        'c': nrm(ks[1], (BATCH, d), f32),
        'ctx': nrm(ks[2], (BATCH, CTX_LEN, d), f32),
        'c_ctx': nrm(ks[3], (d,), f32),
        'mod_w': nrm(ks[4], (DEPTH, d, N_MOD * d), f32) * d ** -0.5,
        'mod_b': nrm(ks[5], (DEPTH, N_MOD * d), f32) * 0.01,
        'ffn_w_gate': nrm(ks[6], (DEPTH, 2, d, D_FF), f32) * d ** -0.5,
        'ffn_w_up': nrm(ks[7], (DEPTH, 2, d, D_FF), f32) * d ** -0.5,
        'ffn_w_down': nrm(ks[8], (DEPTH, 2, D_FF, d), f32) * D_FF ** -0.5,
        'w_in': nrm(ks[9], (DEPTH, d, IN_COLS), f32) * d ** -0.5,
        'hgrn_lb_logits': nrm(ks[10], (DEPTH + 1, 2, A_KW), f32) * 0.1,
        'hgrn_norm_w': 1.0 + 0.1 * nrm(ks[11], (DEPTH, A_DV), f32),
        'hyena_conv_w': nrm(ks[12], (DEPTH, HYENA_SHORT, 3 * B_WIDTH), f32) * HYENA_SHORT ** -0.5,
        'hyena_conv_b': nrm(ks[13], (DEPTH, 3 * B_WIDTH), f32) * 0.01,
        'hyena_w1': nrm(ks[14], (DEPTH, HYENA_EMB, HYENA_FFN), f32) * HYENA_EMB ** -0.5,
        'hyena_b1': nrm(ks[15], (DEPTH, HYENA_FFN), f32) * 0.1,
        'hyena_freq1': 1.0 + 0.1 * nrm(ks[16], (DEPTH, HYENA_FFN), f32),
        'hyena_w2': nrm(ks[17], (DEPTH, HYENA_FFN, HYENA_FFN), f32) * HYENA_FFN ** -0.5,
        'hyena_b2': nrm(ks[18], (DEPTH, HYENA_FFN), f32) * 0.1,
        'hyena_freq2': 1.0 + 0.1 * nrm(ks[19], (DEPTH, HYENA_FFN), f32),
        'hyena_w3': nrm(ks[20], (DEPTH, HYENA_FFN, HYENA_ORDER * 2 * B_WIDTH), f32) * HYENA_FFN ** -0.5,
        'hyena_bias': nrm(ks[21], (DEPTH, HYENA_ORDER, B_WIDTH), f32),
        'w_proj_a': nrm(ks[22], (DEPTH, A_VW, d), f32) * A_VW ** -0.5,
        'w_proj_b': nrm(ks[23], (DEPTH, B_WIDTH, d), f32) * B_WIDTH ** -0.5,
        'w_out': nrm(ks[24], (DEPTH, d, d), f32) * d ** -0.5,
        'final_norm_w': 1.0 + 0.1 * nrm(ks[25], (d,), f32),
    }

def first_block(x, c, ctx, c_ctx, mod_w, mod_b, ffn_w_gate, ffn_w_up, ffn_w_down, w_in, hgrn_lb_logits,
              hgrn_norm_w, hyena_conv_w, hyena_conv_b, hyena_w1, hyena_b1, hyena_freq1, hyena_w2, hyena_b2,
              hyena_freq2, hyena_w3, hyena_bias, w_proj_a, w_proj_b, w_out, final_norm_w):
    n_lat = x.shape[1]
    n_ctx = ctx.shape[1]
    h = x + grid_pos_embed(n_lat).astype(x.dtype)[None]
    hc = ctx
    lb_all = jnp.cumsum(jax.nn.softmax(hgrn_lb_logits.astype(jnp.float32), axis=0), axis=0)
    for l in range(DEPTH):
        last = l == DEPTH - 1
        m = jnp.split((jax.nn.silu(c) @ mod_w[l] + mod_b[l])[:, None, :], N_MOD, axis=-1)
        mc = jnp.split((jax.nn.silu(c_ctx) @ mod_w[l] + mod_b[l])[None, None, :], N_MOD, axis=-1)
        h = half_ffn(h, m[0], m[1], m[2], ffn_w_gate[l, 0], ffn_w_up[l, 0], ffn_w_down[l, 0])
        hc = half_ffn(hc, mc[0], mc[1], mc[2], ffn_w_gate[l, 0], ffn_w_up[l, 0], ffn_w_down[l, 0])
        n = modulate(rms_norm(h), m[3], m[4])
        nc = modulate(rms_norm(hc), mc[3], mc[4])
        mix_w = (w_in[l], lb_all[l], hgrn_norm_w[l], hyena_conv_w[l], hyena_conv_b[l], hyena_bias[l],
                 w_proj_a[l], w_proj_b[l], w_out[l])
        filt_w = (hyena_w1[l], hyena_b1[l], hyena_freq1[l], hyena_w2[l], hyena_b2[l], hyena_freq2[l], hyena_w3[l])
        if last:
            s_fw, s_bw = context_states(nc, w_in[l], lb_all[l])
        else:
            zeros = jnp.zeros((hc.shape[0], A_HEADS, A_DK, A_DV), jnp.float32)
            out_c, s_fw, s_bw = token_mixers(nc, zeros, zeros, hyena_kernels(n_ctx, *filt_w), *mix_w)
            hc = hc + mc[5] * out_c
            hc = half_ffn(hc, mc[6], mc[7], mc[8], ffn_w_gate[l, 1], ffn_w_up[l, 1], ffn_w_down[l, 1])
        out, _, _ = token_mixers(n, s_fw, s_bw, hyena_kernels(n_lat, *filt_w), *mix_w)
        h = h + m[5] * out
        h = half_ffn(h, m[6], m[7], m[8], ffn_w_gate[l, 1], ffn_w_up[l, 1], ffn_w_down[l, 1])
    return rms_norm(h) * final_norm_w


DEPTH_2 = 2

Q_BLOCK = 128
RET_CHUNK = 128
NORM_EPS = 1e-6

DIFF_HEADS = 4
DIFF_HEAD_DIM = 64
DIFF_V_DIM = 2 * DIFF_HEAD_DIM
DIFF_WIDTH = DIFF_HEADS * DIFF_V_DIM
PARTIAL_ROT_DIM = DIFF_HEAD_DIM // 4
PARTIAL_ROPE_THETA = 500000.0

RET_HEADS = 4
RET_KEY_DIM = 128
RET_VAL_DIM = 128
RET_WIDTH = RET_HEADS * RET_VAL_DIM
RET_ROPE_THETA = 10000.0

GQA_Q_HEADS = 8
GQA_KV_HEADS = 2
GQA_GROUP = GQA_Q_HEADS // GQA_KV_HEADS
GQA_HEAD_DIM = 64
GQA_WIDTH = GQA_Q_HEADS * GQA_HEAD_DIM
AXIAL_DIM = GQA_HEAD_DIM // 2
AXIAL_ROPE_THETA = 10000.0

N_BRANCHES = 3
BRANCH_WIDTH = 512
D_FF_2 = 4 * D_MODEL

IN_SPLITS = (
    DIFF_HEADS * 2 * DIFF_HEAD_DIM,
    DIFF_HEADS * 2 * DIFF_HEAD_DIM,
    DIFF_WIDTH,
    RET_HEADS * RET_KEY_DIM,
    RET_HEADS * RET_KEY_DIM,
    RET_WIDTH,
    RET_WIDTH,
    GQA_Q_HEADS * GQA_HEAD_DIM,
    GQA_KV_HEADS * GQA_HEAD_DIM,
    GQA_KV_HEADS * GQA_HEAD_DIM,
    N_BRANCHES * D_MODEL,
)
IN_COLS_2 = 7424


def rms_norm_2(x, gain, eps=NORM_EPS):
    xf = x.astype(jnp.float32)
    y = xf * lax.rsqrt(jnp.mean(xf * xf, axis=-1, keepdims=True) + eps)
    return (y * gain.astype(jnp.float32)).astype(x.dtype)

def rope_cos_sin(pos, dim, theta):
    inv_freq = theta ** (-jnp.arange(0, dim, 2, dtype=jnp.float32) / dim)
    ang = pos[:, None] * inv_freq[None, :]
    return jnp.cos(ang), jnp.sin(ang)

def apply_rope(x, cos_sin):
    cos, sin = cos_sin
    n = x.shape[-1] // 2
    shape = (1, cos.shape[0]) + (1,) * (x.ndim - 3) + (n,)
    c = cos.reshape(shape).astype(x.dtype)
    s = sin.reshape(shape).astype(x.dtype)
    x1, x2 = x[..., :n], x[..., n:]
    return jnp.concatenate([x1 * c - x2 * s, x2 * c + x1 * s], axis=-1)

def split_cols(y, sizes):
    out, start = [], 0
    for n in sizes:
        out.append(y[..., start:start + n])
        start += n
    return out

def sweep_query_blocks(fn, q):
    B, S = q.shape[:2]
    nb = S // Q_BLOCK
    qb = jnp.moveaxis(q.reshape((B, nb, Q_BLOCK) + q.shape[2:]), 1, 0)
    ob = lax.map(fn, qb)
    return jnp.moveaxis(ob, 0, 1).reshape((B, S) + ob.shape[3:])

def differential_attention(q, k, v, lam):
    scale = DIFF_HEAD_DIM ** -0.5

    def block(qb):
        s = jnp.einsum('bqhmd,bkhmd->bhmqk', qb, k).astype(jnp.float32) * scale
        p = jax.nn.softmax(s, axis=-1)
        w = (p[:, :, 0] - lam * p[:, :, 1]).astype(v.dtype)
        return jnp.einsum('bhqk,bkhe->bqhe', w, v)

    return sweep_query_blocks(block, q)

def grouped_query_attention(q, k, v):
    scale = GQA_HEAD_DIM ** -0.5

    def block(qb):
        s = jnp.einsum('bqgrd,bkgd->bgrqk', qb, k).astype(jnp.float32) * scale
        p = jax.nn.softmax(s, axis=-1).astype(v.dtype)
        return jnp.einsum('bgrqk,bkgd->bqgrd', p, v)

    return sweep_query_blocks(block, q)

def bidirectional_retention(q, k, v, log_fwd, log_bwd):
    B, S, H, dk = q.shape
    dv = v.shape[-1]
    C = RET_CHUNK
    N = S // C
    q = q.reshape(B, N, C, H, dk)
    k = k.reshape(B, N, C, H, dk)
    v = v.reshape(B, N, C, H, dv)
    i = jnp.arange(C, dtype=jnp.float32)
    diff = i[:, None] - i[None, :]
    decay_intra = jnp.where(
        diff[None] >= 0,
        jnp.exp(jnp.maximum(diff, 0.0)[None] * log_fwd[:, None, None]),
        jnp.exp(jnp.maximum(-diff, 0.0)[None] * log_bwd[:, None, None]))
    scores = jnp.einsum('bnihd,bnjhd->bnhij', q, k) * decay_intra
    out = jnp.einsum('bnhij,bnjhe->bnihe', scores, v)

    zeta_f = jnp.exp((C - 1 - i)[None] * log_fwd[:, None])
    xi_f = jnp.exp((i + 1)[None] * log_fwd[:, None])
    zeta_b = jnp.exp(i[None] * log_bwd[:, None])
    xi_b = jnp.exp((C - i)[None] * log_bwd[:, None])
    kv_f = jnp.einsum('bnjhd,bnjhe,hj->nbhde', k, v, zeta_f)
    kv_b = jnp.einsum('bnjhd,bnjhe,hj->nbhde', k, v, zeta_b)
    dec_f = jnp.exp(C * log_fwd)[None, :, None, None]
    dec_b = jnp.exp(C * log_bwd)[None, :, None, None]

    def chunk_states(kv, decay, reverse):
        def step(state, kv_n):
            return state * decay + kv_n, state
        _, states = lax.scan(step, jnp.zeros_like(kv[0]), kv, reverse=reverse)
        return states

    s_f = chunk_states(kv_f, dec_f, False)
    s_b = chunk_states(kv_b, dec_b, True)
    out = (out
           + jnp.einsum('bnihd,nbhde,hi->bnihe', q, s_f, xi_f)
           + jnp.einsum('bnihd,nbhde,hi->bnihe', q, s_b, xi_b))
    return out.reshape(B, S, H, dv)

def head_group_norm(x, gain, eps=1e-5):
    xf = x.astype(jnp.float32)
    mu = jnp.mean(xf, axis=-1, keepdims=True)
    var = jnp.mean(jnp.square(xf - mu), axis=-1, keepdims=True)
    y = ((xf - mu) * lax.rsqrt(var + eps)).reshape(x.shape[0], x.shape[1], -1)
    return y * gain.astype(jnp.float32)

def second_inputs(seed: int = 0) -> dict:
    key = jax.random.key(seed)
    ks = jax.random.split(key, 21)
    L, D = DEPTH_2, D_MODEL
    f32 = jnp.float32

    def normal(k, shape, scale):
        return jax.random.normal(k, shape, f32) * scale

    def gain(k, shape):
        return 1.0 + 0.02 * jax.random.normal(k, shape, f32)

    base_log_decay = jnp.log(-jnp.log1p(-(2.0 ** (-5.0 - jnp.arange(RET_HEADS, dtype=f32)))))
    return {
        "x": jax.random.normal(ks[0], (BATCH, SEQ, D), f32),
        "attn_norm": gain(ks[1], (L, D)),
        "w_in": normal(ks[2], (L, D, IN_COLS_2), D ** -0.5),
        "diff_q_norm": gain(ks[3], (L, DIFF_HEAD_DIM)),
        "diff_k_norm": gain(ks[4], (L, DIFF_HEAD_DIM)),
        "diff_lam_q1": normal(ks[5], (L, DIFF_HEAD_DIM), 0.1),
        "diff_lam_k1": normal(ks[6], (L, DIFF_HEAD_DIM), 0.1),
        "diff_lam_q2": normal(ks[7], (L, DIFF_HEAD_DIM), 0.1),
        "diff_lam_k2": normal(ks[8], (L, DIFF_HEAD_DIM), 0.1),
        "diff_subln": gain(ks[9], (L, DIFF_V_DIM)),
        "ret_decay_fwd": base_log_decay[None] + normal(ks[10], (L, RET_HEADS), 0.1),
        "ret_decay_bwd": base_log_decay[None] + normal(ks[11], (L, RET_HEADS), 0.1),
        "ret_group_norm": gain(ks[12], (L, RET_WIDTH)),
        "gqa_q_norm": gain(ks[13], (L, GQA_HEAD_DIM)),
        "gqa_k_norm": gain(ks[14], (L, GQA_HEAD_DIM)),
        "w_branch": normal(ks[15], (L, N_BRANCHES, BRANCH_WIDTH, D), BRANCH_WIDTH ** -0.5),
        "w_out": normal(ks[16], (L, D, D), D ** -0.5),
        "mlp_norm": gain(ks[17], (L, D)),
        "w_mlp_in": normal(ks[18], (L, D, D_FF_2), D ** -0.5),
        "w_mlp_out": normal(ks[19], (L, D_FF_2, D), D_FF_2 ** -0.5),
    }

def second_block(x, attn_norm, w_in, diff_q_norm, diff_k_norm, diff_lam_q1, diff_lam_k1,
              diff_lam_q2, diff_lam_k2, diff_subln, ret_decay_fwd, ret_decay_bwd,
              ret_group_norm, gqa_q_norm, gqa_k_norm, w_branch, w_out, mlp_norm,
              w_mlp_in, w_mlp_out):
    B, S, D = x.shape
    f32 = jnp.float32
    rows = S // GRID_W
    seq_pos = jnp.arange(S, dtype=f32)
    row_pos = jnp.repeat(jnp.arange(rows, dtype=f32), GRID_W)
    col_pos = jnp.tile(jnp.arange(GRID_W, dtype=f32), rows)
    rope_partial = rope_cos_sin(seq_pos, PARTIAL_ROT_DIM, PARTIAL_ROPE_THETA)
    rope_ret = rope_cos_sin(seq_pos, RET_KEY_DIM, RET_ROPE_THETA)
    rope_row = rope_cos_sin(row_pos, AXIAL_DIM, AXIAL_ROPE_THETA)
    rope_col = rope_cos_sin(col_pos, AXIAL_DIM, AXIAL_ROPE_THETA)

    def partial_rope(t):
        return jnp.concatenate([apply_rope(t[..., :PARTIAL_ROT_DIM], rope_partial),
                                t[..., PARTIAL_ROT_DIM:]], axis=-1)

    def axial_rope(t):
        return jnp.concatenate([apply_rope(t[..., :AXIAL_DIM], rope_row),
                                apply_rope(t[..., AXIAL_DIM:], rope_col)], axis=-1)

    h = x
    for l in range(DEPTH_2):
        u = rms_norm_2(h, attn_norm[l])
        proj = jnp.einsum('bsd,dc->bsc', u, w_in[l])
        (dq, dk, dv, rq, rk, rv, rg, gq, gk, gv, gate_logits) = split_cols(proj, IN_SPLITS)

        lambda_init = 0.8 - 0.6 * math.exp(-0.3 * l)
        lam = (jnp.exp(jnp.sum(diff_lam_q1[l].astype(f32) * diff_lam_k1[l].astype(f32)))
               - jnp.exp(jnp.sum(diff_lam_q2[l].astype(f32) * diff_lam_k2[l].astype(f32)))
               + lambda_init)
        dq = partial_rope(rms_norm_2(dq.reshape(B, S, DIFF_HEADS, 2, DIFF_HEAD_DIM), diff_q_norm[l]))
        dk = partial_rope(rms_norm_2(dk.reshape(B, S, DIFF_HEADS, 2, DIFF_HEAD_DIM), diff_k_norm[l]))
        dv = dv.reshape(B, S, DIFF_HEADS, DIFF_V_DIM)
        a = differential_attention(dq, dk, dv, lam)
        a = (rms_norm_2(a, diff_subln[l], eps=1e-5) * (1.0 - lambda_init)).reshape(B, S, DIFF_WIDTH)

        rq = apply_rope(rq.reshape(B, S, RET_HEADS, RET_KEY_DIM), rope_ret).astype(f32)
        rk = (apply_rope(rk.reshape(B, S, RET_HEADS, RET_KEY_DIM), rope_ret).astype(f32)
              * (RET_KEY_DIM ** -0.5))
        rv = rv.reshape(B, S, RET_HEADS, RET_VAL_DIM).astype(f32)
        log_fwd = -jnp.exp(ret_decay_fwd[l].astype(f32))
        log_bwd = -jnp.exp(ret_decay_bwd[l].astype(f32))
        r = bidirectional_retention(rq, rk, rv, log_fwd, log_bwd)
        r = (jax.nn.silu(rg.astype(f32)) * head_group_norm(r, ret_group_norm[l])).astype(h.dtype)

        gq = axial_rope(rms_norm_2(gq.reshape(B, S, GQA_KV_HEADS, GQA_GROUP, GQA_HEAD_DIM), gqa_q_norm[l]))
        gk = axial_rope(rms_norm_2(gk.reshape(B, S, GQA_KV_HEADS, GQA_HEAD_DIM), gqa_k_norm[l]))
        gv = gv.reshape(B, S, GQA_KV_HEADS, GQA_HEAD_DIM)
        c = grouped_query_attention(gq, gk, gv).reshape(B, S, GQA_WIDTH)

        branches = jnp.stack([a, r, c], axis=2)
        projected = jnp.einsum('bsnw,nwd->bsnd', branches, w_branch[l])
        gates = jax.nn.sigmoid(gate_logits.reshape(B, S, N_BRANCHES, D))
        merged = jnp.sum(gates * projected, axis=2)
        h = h + jnp.einsum('bsd,de->bse', merged, w_out[l])

        m = jnp.einsum('bsd,df->bsf', rms_norm_2(h, mlp_norm[l]), w_mlp_in[l])
        m = jnp.square(jax.nn.relu(m))
        h = h + jnp.einsum('bsf,fd->bsd', m, w_mlp_out[l])
    return h


def setup_inputs(seed=0):
    out = dict(first_inputs(seed))
    for name, value in second_inputs(seed + 1).items():
        if name != "x":
            out[name + "_2"] = value
    return out


def reference(
    x, c, ctx, c_ctx, mod_w, mod_b, ffn_w_gate, ffn_w_up, ffn_w_down, w_in, hgrn_lb_logits,
    hgrn_norm_w, hyena_conv_w, hyena_conv_b, hyena_w1, hyena_b1, hyena_freq1, hyena_w2,
    hyena_b2, hyena_freq2, hyena_w3, hyena_bias, w_proj_a, w_proj_b, w_out, final_norm_w,
    attn_norm_2, w_in_2, diff_q_norm_2, diff_k_norm_2, diff_lam_q1_2, diff_lam_k1_2,
    diff_lam_q2_2, diff_lam_k2_2, diff_subln_2, ret_decay_fwd_2, ret_decay_bwd_2,
    ret_group_norm_2, gqa_q_norm_2, gqa_k_norm_2, w_branch_2, w_out_2, mlp_norm_2, w_mlp_in_2,
    w_mlp_out_2,
):
    x = first_block(
        x, c, ctx, c_ctx, mod_w, mod_b, ffn_w_gate, ffn_w_up, ffn_w_down, w_in, hgrn_lb_logits,
        hgrn_norm_w, hyena_conv_w, hyena_conv_b, hyena_w1, hyena_b1, hyena_freq1, hyena_w2,
        hyena_b2, hyena_freq2, hyena_w3, hyena_bias, w_proj_a, w_proj_b, w_out, final_norm_w,
    )
    return second_block(
        x, attn_norm_2, w_in_2, diff_q_norm_2, diff_k_norm_2, diff_lam_q1_2, diff_lam_k1_2,
        diff_lam_q2_2, diff_lam_k2_2, diff_subln_2, ret_decay_fwd_2, ret_decay_bwd_2,
        ret_group_norm_2, gqa_q_norm_2, gqa_k_norm_2, w_branch_2, w_out_2, mlp_norm_2,
        w_mlp_in_2, w_mlp_out_2,
    )


_drawn_inputs = setup_inputs


def setup_inputs(seed=0):
    import zlib

    import numpy as np

    out = dict(_drawn_inputs(seed))
    spreads = {}
    factors = {'ctx': 7.348,
     'c_ctx': 5.254,
     'hgrn_lb_logits': 8.0,
     'hyena_conv_b': 5.967,
     'hyena_freq1': 4.463,
     'hyena_freq2': 6.006,
     'diff_q_norm_2': 8.0,
     'diff_k_norm_2': 8.0,
     'diff_lam_q2_2': 8.0,
     'diff_subln_2': 5.293,
     'ret_group_norm_2': 7.334,
     'gqa_q_norm_2': 8.0,
     'gqa_k_norm_2': 8.0}
    for name, (base, spread) in spreads.items():
        noise = np.random.default_rng([zlib.crc32(name.encode()), seed]).standard_normal(out[name].shape)
        drawn = base * np.exp(spread * noise) if base else spread * noise
        out[name] = __import__('jax').numpy.asarray(drawn.astype(out[name].dtype))
    for name, factor in factors.items():
        out[name] = (out[name] * factor).astype(out[name].dtype)
    return out
```

```python
import math
from contextlib import ExitStack

import numpy as np
import concourse.bass as bass
from concourse import mybir

F32 = mybir.dt.float32
F32R = mybir.dt.float32r
U8 = mybir.dt.uint8
ALU = mybir.AluOpType
ACT = mybir.ActivationFunctionType
AX = mybir.AxisListType.X
ds = bass.ds

P = 128
T = 256
TT = T // P
D = 1024
KD = D // P
DFF, MLP = 2816, 4096
KFF, KMLP = DFF // P, MLP // P
HEADS = 4
LAYERS = 2
PANEL = 2048
COLS = PANEL // KD
ROWK = PANEL // D
SLOTS = 4
UNROLL = 4
LEVELS = (64, 32, 16, 8, 4, 2, 1)
EPS = 1e-6
EPS2 = 1e-5
L1_EPS = 1e-6
TWO_PI_HI, TWO_PI_MID = 6.28125, 0.0019350051879882812
TWO_PI_LO = 2 * math.pi - TWO_PI_HI - TWO_PI_MID
ROUND = 1.5 * 2.0 ** 23
PI_SAFE = 3.1415925

N_MOD, N_WIN = 9 * D // COLS, 6144 // COLS
N_UP, N_DOWN, N_BR, N_OUT = DFF // P, DFF // (P * ROWK), 512 // (P * ROWK), D // (P * ROWK)
G_MOD = 0
G_UP1 = G_MOD + N_MOD
G_DOWN1 = G_UP1 + N_UP
G_WIN = G_DOWN1 + N_DOWN
G_PA = G_WIN + N_WIN
G_PB = G_PA + N_BR
G_OUT1 = G_PB + N_BR
G_UP2 = G_OUT1 + N_OUT
G_DOWN2 = G_UP2 + N_UP
G_LAYER = G_DOWN2 + N_DOWN
N_PROJ, N_MIN, N_MOUT = 30, MLP // COLS, MLP // (P * ROWK)
O_BR = N_PROJ
O_OUT = O_BR + 3 * N_BR
O_MIN = O_OUT + N_OUT
O_MOUT = O_MIN + N_MIN
PER_LAYER = O_MOUT + N_MOUT
PANELS = G_LAYER + LAYERS * PER_LAYER
DVE_LINKS, ACT_LINKS = 63, 8
R_DOWN1 = 0
R_PA = R_DOWN1 + N_DOWN
R_PB = R_PA + N_BR
R_OUT1 = R_PB + N_BR
R_DOWN2 = R_OUT1 + N_OUT
R_LAYER = R_DOWN2 + N_DOWN
RO_BR = 0
RO_OUT = RO_BR + 3 * N_BR
RO_MOUT = RO_OUT + N_OUT
R_PER_LAYER = RO_MOUT + N_MOUT
assert PER_LAYER % UNROLL == 0 and R_PER_LAYER % 2 == 0

def columns(*sizes):
    out, at = {}, 0
    for name, n in sizes:
        out[name] = (at, n)
        at += n
    return out, at

VEC1, NV1 = columns(("c", 2 * KD), ("mod_b", 72), ("logit0", 8), ("logit1", 8), ("a_norm", 1), ("conv_w", 36),
                    ("conv_b", 12), ("hy_bias", 8), ("final", 8), ("b1", 1), ("fr1", 1), ("b2", 1), ("fr2", 1))
VEC2, NV2 = columns(("attn_norm", 8), ("mlp_norm", 8), ("dq_norm", 1), ("dk_norm", 1), ("gq_norm", 1), ("gk_norm", 1),
                    ("subln", 1), ("ret_gain", 4), ("decay", 8), ("lam_q", 2), ("lam_k", 2), ("lam_init", 1),
                    ("one_less", 1))
MATS, NMATS = columns(("ident", P), ("block64", P), ("after", P), ("before", P), ("rot_part", P), ("rot_axial", P),
                      ("rot_ret", P))
TABS, NTABS = columns(("cos_part", T), ("sin_part", T), ("cos_axial", T), ("sin_axial", T), ("cos_ret", T),
                      ("sin_ret", T), ("ahead", TT * T), ("behind", TT * T))
HYC, NHYC = columns(("dft", TT * 512), ("dft_back", TT * 512), ("idft", 4 * T))


def shape_constants():
    f4 = np.float32
    p = np.arange(P)
    mats = {n: np.zeros((P, P), f4) for n in MATS}
    mats["ident"][:] = np.eye(P)
    mats["block64"][:] = (p[:, None] // 64 == p[None] // 64)
    mats["after"][:] = p[:, None] > p[None]
    mats["before"][:] = p[:, None] < p[None]

    def rotation(m, base, half):
        for i in range(half):
            m[base + half + i, base + i] = -1
            m[base + i, base + half + i] = 1

    for b in (0, 64):
        rotation(mats["rot_part"], b, 8)
        rotation(mats["rot_axial"], b, 16)
        rotation(mats["rot_axial"], b + 32, 16)
    rotation(mats["rot_ret"], 0, 64)

    pos = np.arange(T, dtype=f4)
    def angles(pos, dim, theta):
        inv = f4(theta) ** (-np.arange(0, dim, 2, dtype=f4) / f4(dim))
        return (pos[:, None] * inv[None, :]).astype(f4)

    tabs = {n: np.zeros((P, k), f4) for n, (_, k) in TABS.items()}
    a = angles(pos, 16, 500000.0)
    tabs["cos_part"][:] = 1
    for b in (0, 64):
        for h in (0, 8):
            tabs["cos_part"][b + h:b + h + 8] = np.cos(a).T
            tabs["sin_part"][b + h:b + h + 8] = np.sin(a).T
    for off, q in ((0, np.repeat(np.arange(T // 64), 64)), (32, np.tile(np.arange(64), T // 64))):
        a = angles(q.astype(f4), 32, 10000.0)
        for b in (0, 64):
            for h in (0, 16):
                tabs["cos_axial"][b + off + h:b + off + h + 16] = np.cos(a).T
                tabs["sin_axial"][b + off + h:b + off + h + 16] = np.sin(a).T
    a = angles(pos, 128, 10000.0)
    for h in (0, 64):
        tabs["cos_ret"][h:h + 64] = np.cos(a).T
        tabs["sin_ret"][h:h + 64] = np.sin(a).T
    j = (np.arange(TT)[None, :, None] * P + p[:, None, None])
    i = np.arange(T)[None, None, :]
    tabs["ahead"][:] = np.maximum(i - j, 0).reshape(P, -1)
    tabs["behind"][:] = np.maximum(j - i, 0).reshape(P, -1)

    masks = np.zeros((P, 2 * len(LEVELS) + 1, P), f4)
    for n, h in enumerate(LEVELS):
        same = (p[:, None] // (2 * h)) == (p[None] // (2 * h))
        first = (p // h) % 2 == 0
        masks[:, n] = same & first[:, None] & ~first[None]
        masks[:, len(LEVELS) + n] = same & ~first[:, None] & first[None]
    masks[:, -1] = np.eye(P)

    quarter = D // 4
    omega = (1.0 / (f4(10000.0) ** (np.arange(quarter, dtype=f4) / f4(quarter)))).astype(f4)
    rows = T // 64
    ar = np.arange(rows, dtype=f4)[:, None] * omega
    ac = np.arange(64, dtype=f4)[:, None] * omega
    er = np.concatenate([np.sin(ar), np.cos(ar)], -1)
    ec = np.concatenate([np.sin(ac), np.cos(ac)], -1)
    emb = np.concatenate([np.broadcast_to(er[:, None], (rows, 64, D // 2)),
                          np.broadcast_to(ec[None], (rows, 64, D // 2))], -1).reshape(T, D).astype(f4)
    posemb = emb.T.reshape(KD, P, T).transpose(1, 0, 2)

    n = 2 * T
    f = np.arange(T)
    def dft(t):
        w = 2 * np.pi * ((t[:, None] * f[None]) % n) / n
        im = -np.sin(w)
        im[:, 0] = np.cos(np.pi * t)
        return np.concatenate([np.cos(w), im], 1)
    t = np.arange(T)
    hyc = {}
    hyc["dft"] = dft(t).reshape(TT, P, n).transpose(1, 0, 2)
    hyc["dft_back"] = dft(n - 1 - t).reshape(TT, P, n).transpose(1, 0, 2)
    inv = dft(t).T * (2.0 / n)
    inv[0] /= 2
    inv[T] /= 2
    hyc["idft"] = inv.reshape(4, P, T).transpose(1, 0, 2)
    tt = (np.arange(T, dtype=f4) / f4(T - 1)).astype(f4)
    lo, hi = math.log(1e-2) / 1.5, math.log(1e-2) / 0.3
    deltas = np.abs(np.linspace(lo, hi, 512, dtype=f4))
    window = (np.exp(-tt[:, None] * deltas[None]) + f4(0.05)).astype(f4)
    window = window.reshape(TT, P, 512).transpose(1, 0, 2)
    w = (2.0 * math.pi * np.arange(T, dtype=f4) / T).astype(f4)
    bands = np.linspace(1e-4, 15, 16, dtype=f4)
    ang = (w[:, None] * bands[None]).astype(f4)
    z = np.concatenate([tt[:, None], np.cos(ang), -np.sin(ang)], -1).astype(f4)
    zT = np.zeros((P, T), f4)
    zT[:33] = z.T

    def flat(x):
        return np.ascontiguousarray(np.asarray(x, f4).reshape(P, -1))
    return {
        "mats": np.concatenate([mats[k] for k in MATS], 1),
        "tabs": np.concatenate([tabs[k] for k in TABS], 1),
        "masks": np.ascontiguousarray(masks.reshape(P, -1)),
        "posemb": flat(posemb),
        "hyc": np.concatenate([flat(hyc[k]) for k in HYC], 1),
        "window": flat(window),
        "zT": zT,
    }


def build(nc, stream, xT, ctxT, vec1, vec2, lbrow, hyw, mats, tabs, masks, posemb, hyc, window, zT, out):
    with ExitStack() as ctx:
        def sb(name, shape, dt=F32):
            return ctx.enter_context(nc.sbuf_tensor(name, shape, dt))

        def sem(name):
            return ctx.enter_context(nc.semaphore(name))

        landing = sb("landing", [P, SLOTS, PANEL])
        whi, wlo = (sb(n, [P, 2, PANEL], F32R) for n in ("whi", "wlo"))
        xhi, xlo = (sb(n, [P, KD, 2 * T], F32R) for n in ("xhi", "xlo"))
        ahi, alo = (x[:, 0:2 * ROWK].rearrange("p (r k) t -> p r k t", k=ROWK) for x in (xhi, xlo))
        h = sb("h", [P, KD, T])
        big = sb("big", [P, 50, T])
        bigf = big[:].rearrange("p c t -> p (c t)")
        v1 = sb("v1", [P, NV1])
        v2 = sb("v2", [P, NV2])
        mat = sb("mat", [P, NMATS])
        msk = sb("msk", [P, 2 * len(LEVELS) + 1, P], U8)
        ones = sb("ones", [P, P])
        mcol = sb("mcol", [P, 72, 2])
        scol = sb("scol", [P, 64])
        gains = sb("gains", [P, 8, KD])
        eps = sb("eps", [P, 2])
        rstd = sb("rstd", [P, 2, T])
        ws = sb("ws", [P, 11008])
        ps = ctx.enter_context(nc.psum_tensor("ps", [P, 8, 512], F32))

        def W(at, *shape):
            n = int(np.prod(shape))
            v = ws[:, at:at + n]
            if len(shape) == 2:
                v = v.rearrange("p (a b) -> p a b", b=shape[1])
            if len(shape) == 3:
                v = v.rearrange("p (a b c) -> p a b c", b=shape[1], c=shape[2])
            if len(shape) == 4:
                v = v.rearrange("p (a b c d) -> p a b c d", b=shape[1], c=shape[2], d=shape[3])
            return v

        def chunks(a, n):
            return big[:, a:a + n, :]

        def flatc(a, n):
            return bigf[:, a * T:(a + n) * T]

        def m1(name, i=0, n=1):
            a = VEC1[name][0] + i
            return v1[:, a:a + n]

        def m2(name, i=0, n=1):
            a = VEC2[name][0] + i
            return v2[:, a:a + n]

        def mt(name):
            a = MATS[name][0]
            return mat[:, a:a + P]

        ident = mt("ident")

        hc = W(0, KD, T)
        pos = W(2048, KD, T)
        mrow = W(4096, UNROLL, COLS)
        mask_in = W(6144, (2 * len(LEVELS) + 1) * P)
        Vx = W(0, TT, 512)
        Vc = W(1024, TT, 512)
        sc = [W(2048, TT, 512), W(3072, TT, 512)]
        lrow = W(4096, 2, 1024)
        lgc = W(6144, TT, 512)
        XC = [W(1024, HEADS * TT, P + 1), W(2056, HEADS * TT, P + 1)]
        S = W(3088, TT, HEADS, T)
        EM = [W(7168, HEADS * TT, P), W(8192, HEADS * TT, P)]
        EMf = [W(7168, HEADS * TT * P), W(8192, HEADS * TT * P)]
        Q0, KF, G0, HY, MG = 0, (4, 8), 12, 16, 28
        s0 = [bigf[:, 44 * T + d * 512:44 * T + (d + 1) * 512].rearrange("p (a b) -> p a b", b=P) for d in range(2)]
        hcon = W(0, NHYC)
        def hy_const(name, a):
            b, n = HYC[name]
            return ws[:, b:b + n].rearrange("p (a b) -> p a b", a=a)
        dft = [hy_const("dft", TT), hy_const("dft_back", TT)]
        idft = hy_const("idft", 4)
        kern = W(NHYC, TT, 2, 512)
        Kf = W(NHYC + 2048, 4, 512)
        win = W(NHYC + 4096, TT, 512)
        h2 = W(NHYC + 5120, T)
        zfeat = W(NHYC + 5120 + T, T)
        hyin = W(NHYC + 5120 + 2 * T, 2176)
        hw1, hw2, hw3 = hyin[0:33, 0:64], hyin[0:64, 64:128], hyin[0:64, 128:2176]
        ZC = (4, 8, 16)
        absk = bigf[:, 20 * T:28 * T]
        uT = bigf[:, 20 * T:24 * T].rearrange("p (a b) -> p a b", b=512)
        ptmp = uT
        Pi = bigf[:, 24 * T:28 * T].rearrange("p (a b) -> p a b", b=512)
        Pf = bigf[:, 44 * T:48 * T].rearrange("p (a b) -> p a b", b=512)
        ang = bigf[:, 44 * T:46 * T].rearrange("p (a b) -> p a b", b=T)
        l1 = bigf[:, 48 * T:50 * T]
        DQ, DK, GQ, GK, RQ, RK, RG, GT = 0, 4, 8, 12, 14, 18, 22, 26
        tab = W(0, NTABS)
        def tb(name):
            a, n = TABS[name]
            return ws[:, a:a + n]
        VD = W(NTABS, TT, 512)
        VR = W(NTABS + 1024, TT, 512)
        VG = W(NTABS + 2048, TT, P)
        tmpA = NTABS + 2304
        nsq = W(tmpA, 4, T)
        nrs = W(tmpA + 1024, 4, T)
        nrot = W(tmpA + 2048, 4, T)
        ew = [W(tmpA + 3072, 2, T), W(tmpA + 3584, 2, T)]
        wT = [W(tmpA + 4096, 2, TT, T), W(tmpA + 5120, 2, TT, T)]
        rtmp = [W(tmpA, 2 * T), W(tmpA + 512, 2 * T)]
        ROPES = ((DQ, 4, "dq_norm", "rot_part", "cos_part", "sin_part"), (DK, 4, "dk_norm", "rot_part", "cos_part", "sin_part"),
                 (GQ, 4, "gq_norm", "rot_axial", "cos_axial", "sin_axial"),
                 (GK, 2, "gk_norm", "rot_axial", "cos_axial", "sin_axial"),
                 (RQ, 4, None, "rot_ret", "cos_ret", "sin_ret"), (RK, 4, None, "rot_ret", "cos_ret", "sin_ret"))

        def hid_chunk(i, t):
            w = t // T
            return big[:, ds(i * w, w), :].rearrange("p c t -> p (c t)")

        def hid_src(t):
            if t == T:
                return lambda i: big[:, ds(i * ROWK, ROWK), :]
            return lambda i: big[:, ds(i * (2 * ROWK), 2 * ROWK), :].rearrange("p (k b) t -> p k (b t)", b=2)

        def chunk_src(c0):
            return lambda i: big[:, ds(i * ROWK + c0, ROWK), :]

        def halves(x, hh):
            b = x.rearrange("p (n u s) -> p n u s", u=2, s=hh)
            return b[:, :, 0], b[:, :, 1]

        NL = len(LEVELS) + 1
        levels = [(d, n) for d in range(2) for n in range(NL)] + [(2, 0)]
        smx = sb("smx", [P, 4, 8])
        Dm = [W(tmpA + 1024, TT, T), W(tmpA + 1536, TT, T)]
        sD = [W(tmpA + 2048, TT, T), W(tmpA + 2560, TT, T)]
        PLAIN = (DQ, DQ + 2, DK, DK + 2, GQ, GQ + 2, GK, RQ, RQ + 2, RK, RK + 2, RG, RG + 2) + tuple(range(GT, GT + 24, 2))
        N_VALUES, N_HEADS = 5, 18
        SUM_AFTER = {7: 0, 9: 1, 11: 2, 12: 3}
        ROT_AFTER = {8: (0, 0), 10: (1, 0), 12: (2, 0), 13: (3, 0), 14: (4, 14), 16: (5, 16)}
        SQUARE_AFTER = {6: 0, 8: 1, 10: 2, 11: 3}
        RMS_AFTER = SUM_AFTER
        SCALE_IN = {8: 0, 10: 1, 12: 2, 13: 3}
        ROPE_IN = {9: 0, 11: 1, 13: 2, 14: 3, 15: 4, 17: 5}
        PAIRS = 16
        BRANCHES = ((GQ, 16), (DQ, 0), (RQ, 8))

        per = {}
        def lsem(name, n=0):
            s = sem(name)
            per[name] = n
            return s

        landed = [sem(f"landed{i}") for i in range(SLOTS)]
        hi_done = sem("hi_done")
        lo_done = sem("lo_done")
        panel_used = sem("panel_used")
        act_hi = sem("act_hi")
        act_lo = sem("act_lo")
        small_in = sem("small_in")
        x_in = sem("x_in")
        lb_in = sem("lb_in")
        hy_in = sem("hy_in")
        tab_in = sem("tab_in")
        v2_in = sem("v2_in")
        out_done = sem("out_done")
        const_set = sem("const_set")
        dve_chain, act_chain = sem("dve_chain"), sem("act_chain")
        dve_link = lsem("dve_link", DVE_LINKS)
        act_link = lsem("act_link", ACT_LINKS)
        c_silu, c_split, x_zero = sem("c_silu"), sem("c_split"), sem("x_zero")
        mod_copied, mod_turned, mod_added = sem("mod_copied"), sem("mod_turned"), sem("mod_added")
        cols_set = sem("cols_set")
        h_set = sem("h_set")
        sq_done, sum_done, rstd_done = lsem("sq_done", 2), lsem("sum_done", 2), lsem("rstd_done", 2)
        norm_scaled, norm_hi, norm_lo = lsem("norm_scaled", 16), lsem("norm_hi", 16), lsem("norm_lo", 16)
        silu_done, hid_done = sem("silu_done"), sem("hid_done")
        res_done = lsem("res_done", 1)
        win_out = sem("win_out")
        lb_diff, lb_sig, lb_set = sem("lb_diff"), sem("lb_sig"), sem("lb_set")
        cf_done, cln_done, ck_done, csum_done, cdec_done, ckey_done, cst_done, cst_out = (
            sem(n) for n in ("cf_done", "cln_done", "ck_done", "csum_done", "cdec_done", "ckey_done", "cst_done",
                             "cst_out"))
        xf_done, xln_done = sem("xf_done"), sem("xln_done")
        lv_diff, lv_exp, lv_mul, lv_score, lv_sel = (sem("lv_" + n) for n in ("diff", "exp", "mul", "score", "sel"))
        qe_diff, qe_exp, qe_done, o_done, osq_done, osum_done, orstd_done, oa_done = (
            sem(n) for n in ("qe_diff", "qe_exp", "qe_done", "o_done", "osq_done", "osum_done", "orstd_done", "oa_done"))
        conv_done, fl_mm, fl_arg, fl_sin, h3_mm, win_mul, abs_done, l1_mm, kf_mm, kf_done = (
            sem(n) for n in ("conv_done", "fl_mm", "fl_arg", "fl_sin", "h3_mm", "win_mul", "abs_done", "l1_mm", "kf_mm",
                             "kf_done"))
        turn_done, uT_done, uf_mm, pf_done, y_mm, z_done = (
            sem(n) for n in ("turn_done", "uT_done", "uf_mm", "pf_done", "y_mm", "z_done"))
        gate_done = lsem("gate_done", 3)
        gate1_done = sem("gate1_done")
        gate_on = lsem("gate_on", 4)
        proj_out = lsem("proj_out", N_PROJ)
        lam_mul, lam_mm, lam_exp, lam_set = (lsem("lam_" + n, 1) for n in ("mul", "mm", "exp", "set"))
        rp_sq, rp_sum, rp_rs = (lsem("rp_" + n, 4) for n in ("sq", "sum", "rs"))
        rp_n, rp_rot, rp_done = lsem("rp_n", 4), lsem("rp_rot", 6), lsem("rp_done", 6)
        sc_mm, sc_max, sc_exp, sc_w, sc_turn, sc_wT = (lsem("sc_" + n, 16) for n in ("mm", "max", "exp", "w", "turn", "wT"))
        pv_mm, pv_out = lsem("pv_mm", 8), lsem("pv_out", 8)
        rt_arg, rt_dec, rt_mm, rt_mul, rt_pv, rt_out = (lsem("rt_" + n, 4) for n in ("arg", "dec", "mm", "mul", "pv", "out"))
        sub_sq, sub_sum, sub_rs, sub_done = (lsem("sub_" + n, 1) for n in ("sq", "sum", "rs", "done"))
        gn_mean, gn_cen, gn_sq, gn_sum, gn_rs, gn_done = (
            lsem("gn_" + n, 1) for n in ("mean", "cen", "sq", "sum", "rs", "done"))
        relu_done, m_done = lsem("relu_done", N_MIN), lsem("m_done", N_MIN)
        layer_done = lsem("layer_done", 1)

        def at(s, l, c, base=0):
            return l * per[s.name] + (base + c)

        def panel_loop(eng, first, count, body):
            phase = first[1] if isinstance(first, tuple) else first
            g0 = first[0] if isinstance(first, tuple) else first
            if count >= 2 * UNROLL:
                with eng.Fori(0, count // UNROLL) as i:
                    for j in range(UNROLL):
                        body(i * UNROLL + j, g0 + (i * UNROLL + j), (phase + j) % UNROLL)
            else:
                for j in range(count - count % UNROLL):
                    body(j, g0 + j, (phase + j) % UNROLL)
            for j in range(count - count % UNROLL, count):
                body(j, g0 + j, (phase + j) % UNROLL)

        def layer_panel(l, off):
            return (l * PER_LAYER + (G_LAYER + off), G_LAYER + off)

        block = ctx.enter_context(nc.Block())

        @block.sync
        def _(sp):
            for g in range(SLOTS):
                sp.dma_start(landing[:, g], stream[g]).then_inc(landed[g], 16)

            def load(g, s):
                sp.wait_ge(lo_done, g - (SLOTS - 1))
                sp.dma_start(landing[:, s], stream[ds(g, 1)].rearrange("a p n -> p (a n)")).then_inc(landed[s], 16)

            with sp.Fori(1, PANELS // UNROLL) as i:
                for j in range(UNROLL):
                    load(i * UNROLL + j, j)
            for g in range(PANELS - PANELS % UNROLL, PANELS):
                load(g, g % SLOTS)
            sp.wait_ge(layer_done, 1 + LAYERS)
            sp.dma_start(out, h[:].rearrange("p k t -> p (k t)")).then_inc(out_done, 16)
            sp.wait_ge(out_done, 16)

        @block.gpsimd
        def _(pool):
            pool.wait_ge(const_set, 3)

            def high(g, s, turn):
                pool.wait_ge(landed[s], (turn + 1) * 16)
                if not isinstance(g, int) or g >= 2:
                    pool.wait_ge(panel_used, g - 1)
                hi, panel = whi[:, s % 2], landing[:, s]
                pool.tensor_tensor(hi[:, 0:P], panel[:, 0:P], ones[:], ALU.mult)
                pool.tensor_scalar(hi[:, P:], panel[:, P:], 1.0, 0.0, ALU.mult, ALU.add).then_inc(hi_done, 1)

            for g in range(UNROLL):
                high(g, g, 0)
            with pool.Fori(1, PANELS // UNROLL) as i:
                for j in range(UNROLL):
                    high(i * UNROLL + j, j, i)
            for g in range(PANELS - PANELS % UNROLL, PANELS):
                high(g, g % SLOTS, g // SLOTS)

        @block.vector
        def _(dve):
            v = nc.vector
            count = [0]
            link = [0, 0]

            def step(ins):
                count[0] += 1
                ins.then_inc(dve_chain, 1)
                dve.wait_ge(dve_chain, count[0])

            def lstep(ins):
                link[1] += 1
                ins.then_inc(dve_link, 1)
                dve.wait_ge(dve_link, at(dve_link, link[0], link[1]))

            def low(g, s):
                dve.wait_ge(hi_done, g + 1)
                if not isinstance(g, int) or g >= 2:
                    dve.wait_ge(panel_used, g - 1)
                v.tensor_tensor(wlo[:, s % 2], landing[:, s], whi[:, s % 2].bitcast(F32), ALU.subtract
                                ).then_inc(lo_done, 1)

            def low_stage(first, n, last=True):
                panel_loop(dve, first, n if last else n - 1, lambda i, g, s: low(g + 1, (s + 1) % SLOTS))

            def part_low(src, r, r_phase, t):
                dve.wait_ge(act_hi, r + 1)
                v.tensor_tensor(alo[:, r_phase % 2, :, 0:t], src, ahi[:, r_phase % 2, :, 0:t].bitcast(F32),
                                ALU.subtract).then_inc(act_lo, 1)

            def row_stage(first, n, src, r0, r_phase, t, last=True):
                part_low(src(0), r0, r_phase, t)

                g0, phase = first if isinstance(first, tuple) else (first, first)

                def body(i, g, s):
                    low(g + 1, (s + 1) % SLOTS)
                    part_low(src(i + 1), r0 + (i + 1), r_phase + (s - phase) % UNROLL + 1, t)
                panel_loop(dve, first, n - 1, body)
                if last:
                    low(g0 + n, (phase + n) % SLOTS)
                return g0 + n

            def norm(n, src, gain, shift, dst0, l=None):
                val = (lambda s, c: at(s, l, c, base=(6 if s is rstd_done else 5 * KD))) if l is not None \
                    else (lambda s, c: c)
                c0 = n * KD
                tmp = bigf[:, 4096:4096 + KD * T].rearrange("p (k t) -> p k t", t=T)
                dve.wait_ge(rstd_done, val(rstd_done, n + 1))
                rs = rstd[:, n % 2]
                for k in range(KD + 1):
                    if k < KD:
                        v.scalar_tensor_tensor(tmp[:, k], src[:, k], gain(k), rs, ALU.mult, ALU.mult
                                               ).then_inc(norm_scaled, 1)
                    if k >= 1:
                        dve.wait_ge(norm_hi, val(norm_hi, c0 + k))
                        j = k - 1
                        hi = xhi[:, j, dst0:dst0 + T].bitcast(F32)
                        lo = xlo[:, j, dst0:dst0 + T]
                        if shift is None:
                            v.tensor_tensor(lo, tmp[:, j], hi, ALU.subtract).then_inc(norm_lo, 1)
                        else:
                            v.scalar_tensor_tensor(lo, tmp[:, j], shift(j), hi, ALU.add, ALU.subtract
                                                   ).then_inc(norm_lo, 1)

            v.memset(ones[:], 1.0).then_inc(const_set, 1)
            v.memset(eps[:, 0:1], EPS).then_inc(const_set, 1)
            v.memset(eps[:, 1:2], EPS2).then_inc(const_set, 1)
            v.memset(mcol[:], 0.0).then_inc(mod_added, 1)
            v.memset(xhi[:].bitcast(F32), 0.0).then_inc(x_zero, 1)
            v.memset(xlo[:].bitcast(F32), 0.0).then_inc(x_zero, 1)
            dve.wait_ge(small_in, 48)
            v.tensor_copy(msk[:].rearrange("p n s -> p (n s)"), mask_in)
            dve.wait_ge(x_in, 48)
            for b in range(2):
                v.tensor_tensor(h[:, 4 * b:4 * b + 4], h[:, 4 * b:4 * b + 4], pos[:, 4 * b:4 * b + 4], ALU.add
                                ).then_inc(h_set, 1)
            dve.wait_ge(c_silu, 2)
            cs = scol[:, 0:2 * KD].rearrange("p (k b) -> p k b", b=2)
            dve.wait_ge(x_zero, 2)
            v.tensor_tensor(xlo[:, :, 0:2], cs, xhi[:, :, 0:2].bitcast(F32), ALU.subtract).then_inc(c_split, 1)

            low(0, 0)
            with dve.Fori(0, N_MOD // UNROLL) as i:
                for j in range(UNROLL):
                    low(i * UNROLL + j + 1, (j + 1) % SLOTS)
                dve.wait_ge(mod_turned, i * UNROLL + UNROLL)
                v.tensor_tensor(mcol[:, ds(i * 8, 8), :], ps[:, 4, 0:16].rearrange("p (c b) -> p c b", b=2),
                                m1("mod_b", 0, 72)[:, ds(i * 8, 8)].unsqueeze(2).to_broadcast([P, 8, 2]), ALU.add
                                ).then_inc(mod_added, 1)
            dve.wait_ge(mod_added, 1 + N_MOD // UNROLL)
            def mod(n, who):
                return mcol[:, 8 * n:8 * n + 8, who]
            for n, (m, who) in enumerate(((1, 0), (1, 1), (4, 0), (4, 1), (7, 0))):
                v.tensor_scalar(gains[:, n], mod(m, who), 1.0, None, ALU.add).then_inc(cols_set, 1)
            for n, (m, who) in enumerate(((2, 0), (2, 1), (8, 0))):
                v.tensor_scalar(gains[:, 5 + n], mod(m, who), 0.5, None, ALU.mult).then_inc(cols_set, 1)
            dve.wait_ge(cols_set, 8)

            def gcol(n):
                return lambda k: gains[:, n, k:k + 1]

            def mcolumn(n, who):
                return lambda k: mcol[:, 8 * n + k, who:who + 1]

            norm(0, h, gcol(0), mcolumn(0, 0), 0)
            norm(1, hc, gcol(1), mcolumn(0, 1), T)

            def up_stage(g0, which, t, last=True):
                def body(i, g, s):
                    low(g + 1, (s + 1) % SLOTS)
                    dve.wait_ge(silu_done, which * KFF + i + 1)
                    hid = hid_chunk(i, t)
                    bank = 2 * ((s - g0) % UNROLL) + 1
                    v.tensor_tensor(hid, hid, ps[:, bank, 0:t], ALU.mult).then_inc(hid_done, 1)
                panel_loop(dve, g0, N_UP, body)

            up_stage(G_UP1, 0, 2 * T)
            dve.wait_ge(hid_done, KFF)
            row_stage(G_DOWN1, N_DOWN, hid_src(2 * T), R_DOWN1, R_DOWN1, 2 * T)
            dve.wait_ge(panel_used, G_DOWN1 + N_DOWN)
            for k in range(KD):
                v.scalar_tensor_tensor(h[:, k], ps[:, k, 0:T], gains[:, 5, k:k + 1], h[:, k], ALU.mult, ALU.add)
                last = v.scalar_tensor_tensor(hc[:, k], ps[:, k, T:2 * T], gains[:, 6, k:k + 1], hc[:, k], ALU.mult,
                                              ALU.add)
            last.then_inc(h_set, 1)
            norm(2, h, gcol(2), mcolumn(3, 0), 0)
            norm(3, hc, gcol(3), mcolumn(3, 1), T)

            low_stage(G_WIN, N_WIN)

            dve.wait_ge(norm_lo, 4 * KD)
            dve.wait_ge(lb_in, 16)
            v.tensor_tensor(scol[:, 16:24], m1("logit0", 0, 8), m1("logit1", 0, 8), ALU.subtract).then_inc(lb_diff, 1)
            v.tensor_tensor(lrow[:, 0], lrow[:, 0], lrow[:, 1], ALU.subtract).then_inc(lb_diff, 1)
            dve.wait_ge(lb_sig, 2)
            v.tensor_scalar(scol[:, 24:32], scol[:, 16:24], -1.0, 1.0, ALU.mult, ALU.add).then_inc(lb_set, 1)
            v.tensor_scalar(lrow[:, 1], lrow[:, 0], -1.0, 1.0, ALU.mult, ALU.add).then_inc(lb_set, 1)
            dve.wait_ge(lb_set, 2)

            dve.wait_ge(win_out, 6)
            for d in range(2):
                def row(n):
                    return lrow[:, n, 512 * d:512 * d + 512].unsqueeze(1).to_broadcast([P, TT, 512])
                step(v.tensor_tensor(sc[d], sc[d], row(1), ALU.mult))
                v.tensor_tensor(sc[d], sc[d], row(0), ALU.add).then_inc(cf_done, 1)
                dve.wait_ge(cln_done, d + 1)
                v.tensor_scalar(sc[d], sc[d], -1.0, 1.0, ALU.mult, ALU.add).then_inc(ck_done, 1)
                dve.wait_ge(ck_done, d + 1)
                dve.wait_ge(cdec_done, d + 1)
                v.tensor_tensor(sc[d], sc[d], lgc, ALU.mult).then_inc(ckey_done, 1)

            for d in range(2):
                for c in range(HEADS):
                    n = 4 * d + c
                    last = v.tensor_scalar(big[:, KF[d] + c], big[:, KF[d] + c], scol[:, 24 + n:25 + n],
                                           scol[:, 16 + n:17 + n], ALU.mult, ALU.add)
                last.then_inc(xf_done, 1)
            dve.wait_ge(cst_out, 2)
            for d in range(2):
                last = v.memset(XC[d][:, :, 0:1], 0.0)
            step(last)
            for d in range(2):
                dve.wait_ge(xln_done, d + 1)
                v.tensor_scalar(flatc(KF[d], 4), flatc(KF[d], 4), -1.0, 1.0, ALU.mult, ALU.add)
                for n in range(HEADS * TT):
                    last = v.tensor_tensor_scan(XC[d][:, n, 1:P + 1], ones[:], EM[d][:, n], 0.0, ALU.mult, ALU.add)
                step(last)

            def q_of(c0):
                return flatc(c0, 4)
            def diff(m):
                d, n = levels[m]
                em = EM[m % 2]
                if m >= 2:
                    dve.wait_ge(lv_score, m - 1)
                if d == 2:
                    v.tensor_tensor(em, chunks(KF[0], 4).rearrange("p c (u s) -> p (c u) s", s=P),
                                    chunks(KF[1], 4).rearrange("p c (u s) -> p (c u) s", s=P), ALU.add
                                    ).then_inc(lv_diff, 1)
                    return
                o = 1 - d
                if n < len(LEVELS):
                    hh = LEVELS[n]
                    x = XC[d][:, :, o:o + P].rearrange("p n (b s) -> p n b s", s=2 * hh)
                    mid = XC[d][:, :, 0:P].rearrange("p n (b s) -> p n b s", s=2 * hh)[:, :, :, hh:hh + 1]
                    mid = mid.to_broadcast([P, HEADS * TT, P // (2 * hh), 2 * hh])
                    v.tensor_tensor(em.rearrange("p n (b s) -> p n b s", s=2 * hh), x, mid, ALU.subtract
                                    ).then_inc(lv_diff, 1)
                else:
                    x = XC[d][:].rearrange("p (g u) s -> p g u s", u=TT)
                    tot = x[:, :, 0, P:P + 1].to_broadcast([P, HEADS, P])
                    v.tensor_tensor(em.rearrange("p (g u) s -> p g u s", u=TT)[:, :, 0], tot, x[:, :, 0, o:o + P],
                                    ALU.subtract).then_inc(lv_diff, 1)

            def mul(m):
                d, n = levels[m]
                if d == 2:
                    return
                hh = (LEVELS + (P,))[n]
                dve.wait_ge(lv_exp, m + 1)
                e = halves(EMf[m % 2], hh)
                q, kk = halves(q_of(Q0), hh), halves(q_of(KF[d]), hh)
                a = (kk, q) if d == 0 else (q, kk)
                v.tensor_tensor(e[0], e[0], a[0][0], ALU.mult)
                v.tensor_tensor(e[1], e[1], a[1][1], ALU.mult).then_inc(lv_mul, 1)

            def select(m):
                d, n = levels[m]
                dve.wait_ge(lv_score, m + 1)
                if d == 2 or n < len(LEVELS):
                    mk = msk[:, 2 * len(LEVELS) if d == 2 else d * len(LEVELS) + n].unsqueeze(1)
                    for u in range(TT):
                        last = v.copy_predicated(S[:, u, :, u * P:(u + 1) * P], mk.to_broadcast([P, HEADS, P]),
                                                 ps[:, 2 * (m % 2) + u].rearrange("p (g s) -> p g s", s=P))
                else:
                    last = v.tensor_copy(S[:, d, :, (1 - d) * P:(2 - d) * P],
                                         ps[:, 2 * (m % 2)].rearrange("p (g s) -> p g s", s=P))
                last.then_inc(lv_sel, 1)

            step(v.memset(S.rearrange("p u g t -> p (u g t)"), 0.0))
            diff(0)
            for m in range(len(levels)):
                mul(m)
                if m >= 1:
                    select(m - 1)
                if m + 1 < len(levels):
                    diff(m + 1)
            select(len(levels) - 1)
            dve.wait_ge(lv_score, len(levels))
            xs = [XC[d][:].rearrange("p (g u) s -> p g u s", u=TT) for d in range(2)]
            es = [EM[d].rearrange("p (g u) s -> p g u s", u=TT) for d in range(2)]
            def total(d, u):
                return xs[d][:, :, u, P:P + 1].to_broadcast([P, HEADS, P])
            v.tensor_copy(es[0][:, :, 0], xs[0][:, :, 0, 1:P + 1])
            v.tensor_tensor(es[0][:, :, 1], total(0, 0), xs[0][:, :, 1, 1:P + 1], ALU.add)
            v.tensor_tensor(es[1][:, :, 1], total(1, 1), xs[1][:, :, 1, 0:P], ALU.subtract)
            step(v.tensor_tensor(es[1][:, :, 0], total(1, 0), xs[1][:, :, 0, 0:P], ALU.subtract))
            v.tensor_tensor(es[1][:, :, 0], total(1, 1), es[1][:, :, 0], ALU.add).then_inc(qe_diff, 1)
            dve.wait_ge(qe_exp, 1)
            for d in range(2):
                last = v.tensor_tensor(EMf[d], EMf[d], q_of(Q0), ALU.mult)
            last.then_inc(qe_done, 1)
            dve.wait_ge(orstd_done, 1)
            for b in range(2):
                step(v.scalar_tensor_tensor(flatc(Q0 + 2 * b, 2), ps[:, 4 + b], m1("a_norm"),
                                            EMf[1][:, b * 512:(b + 1) * 512], ALU.mult, ALU.mult))
            v.tensor_tensor(flatc(Q0, 4), flatc(Q0, 4), flatc(G0, 4), ALU.mult).then_inc(oa_done, 1)

            for c in range(12):
                src = big[:, HY + c]
                dst = big[:, ZC[c // 4] + c % 4]
                step(v.tensor_scalar(dst, src, m1("conv_w", 12 + c), m1("conv_b", c), ALU.mult, ALU.add))
                step(v.scalar_tensor_tensor(dst[:, 1:T], src[:, 0:T - 1], m1("conv_w", c), dst[:, 1:T], ALU.mult, ALU.add))
                last = v.scalar_tensor_tensor(dst[:, 0:T - 1], src[:, 1:T], m1("conv_w", 24 + c), dst[:, 0:T - 1],
                                              ALU.mult, ALU.add)
                if c == 3:
                    last.then_inc(conv_done, 1)
            last.then_inc(conv_done, 1)
            dve.wait_ge(conv_done, 2)

            for n, (b, f) in enumerate((("b1", "fr1"), ("b2", "fr2"))):
                a, k = ang[0:64, 0], ang[0:64, 1]
                dve.wait_ge(fl_mm, n + 1)
                step(v.tensor_scalar(a, ps[0:64, 0, 0:T], m1(b)[0:64], m1(f)[0:64], ALU.add, ALU.mult))
                step(v.tensor_scalar(k, a, 1 / (2 * math.pi), ROUND, ALU.mult, ALU.add))
                step(v.tensor_scalar(k, k, ROUND, None, ALU.subtract))
                for part in (TWO_PI_HI, TWO_PI_MID, TWO_PI_LO):
                    step(v.scalar_tensor_tensor(a, k, -part, a, ALU.mult, ALU.add))
                v.tensor_scalar(a, a, PI_SAFE, -PI_SAFE, ALU.min, ALU.max).then_inc(fl_arg, 1)
            for o in range(2):
                dve.wait_ge(hy_in, 64)
                for u in range(TT):
                    for d in range(2):
                        dve.wait_ge(h3_mm, 4 * o + 2 * u + d + 1)
                        v.tensor_tensor(kern[:, u, d], ps[:, 2 * u + d], win[:, u], ALU.mult).then_inc(win_mul, 1)
                dve.wait_ge(l1_mm, o + 1)
                step(v.tensor_scalar(l1, ps[:, 4], L1_EPS, None, ALU.add))
                step(v.reciprocal(l1, l1))
                for m in range(4):
                    dve.wait_ge(kf_mm, 4 * o + m + 1)
                    last = v.tensor_tensor(Kf[:, m], ps[:, m], l1, ALU.mult)
                last.then_inc(kf_done, 1)
                dve.wait_ge(kf_done, o + 1)
                dve.wait_ge(uf_mm, o + 1)
                ur, ui = ps[:, 4:6], ps[:, 6:8]
                kr, ki = Kf[:, 0:2], Kf[:, 2:4]
                v.tensor_tensor(Pf, ur, kr, ALU.mult)
                step(v.tensor_tensor(ptmp, ui, ki, ALU.mult))
                step(v.tensor_tensor(Pf, Pf, ptmp, ALU.subtract))
                v.tensor_tensor(Pi, ur, ki, ALU.mult)
                step(v.tensor_tensor(ptmp, ui, kr, ALU.mult))
                step(v.tensor_tensor(Pi, Pi, ptmp, ALU.add))
                v.tensor_tensor(Pf[0:1, 0], ur[0:1, 0], kr[0:1, 0], ALU.mult)
                v.tensor_tensor(Pi[0:1, 0], ui[0:1, 0], ki[0:1, 0], ALU.mult).then_inc(pf_done, 1)
                dve.wait_ge(y_mm, o + 1)
                for c in range(4):
                    z, g = big[:, ZC[0] + c], big[:, ZC[1 + o] + c]
                    step(v.scalar_tensor_tensor(z, z, m1("hy_bias", 4 * o + c), ps[:, c // 2, (c % 2) * T:(c % 2 + 1) * T],
                                                ALU.mult, ALU.add))
                    last = v.tensor_tensor(z, z, g, ALU.mult)
                last.then_inc(z_done, 1)

            dve.wait_ge(z_done, 2)
            dve.wait_ge(oa_done, 1)
            row_stage(G_PA, N_BR, chunk_src(Q0), R_PA, R_PA, T)
            dve.wait_ge(panel_used, G_PA + N_BR)
            for b in range(4):
                last = v.tensor_tensor(flatc(MG + 2 * b, 2), flatc(MG + 2 * b, 2), ps[:, b], ALU.mult)
            last.then_inc(gate1_done, 1)
            row_stage(G_PB, N_BR, chunk_src(ZC[0]), R_PB, R_PB, T)
            dve.wait_ge(panel_used, G_PB + N_BR)
            for b in range(4):
                last = v.tensor_tensor(flatc(MG + 8 + 2 * b, 2), flatc(MG + 8 + 2 * b, 2), ps[:, 4 + b], ALU.mult)
            step(last)
            v.tensor_tensor(flatc(MG, 8), flatc(MG, 8), flatc(MG + 8, 8), ALU.add).then_inc(gate1_done, 1)
            dve.wait_ge(gate1_done, 2)
            row_stage(G_OUT1, N_OUT, chunk_src(MG), R_OUT1, R_OUT1, T)
            dve.wait_ge(panel_used, G_OUT1 + N_OUT)
            for k in range(KD):
                last = v.scalar_tensor_tensor(h[:, k], ps[:, k // 2, (k % 2) * T:(k % 2 + 1) * T], mcolumn(5, 0)(k), h[:, k],
                                              ALU.mult, ALU.add)
            last.then_inc(h_set, 1)

            norm(4, h, gcol(4), mcolumn(6, 0), 0)
            up_stage(G_UP2, 1, T)
            dve.wait_ge(hid_done, 2 * KFF)
            row_stage(G_DOWN2, N_DOWN, hid_src(T), R_DOWN2, R_DOWN2, T, last=False)
            dve.wait_ge(panel_used, G_DOWN2 + N_DOWN)
            for k in range(KD):
                last = v.scalar_tensor_tensor(h[:, k], ps[:, k // 2, (k % 2) * T:(k % 2 + 1) * T], gains[:, 7, k:k + 1],
                                              h[:, k], ALU.mult, ALU.add)
            last.then_inc(h_set, 1)
            dve.wait_ge(rstd_done, 6)
            for k in range(KD):
                last = v.scalar_tensor_tensor(h[:, k], h[:, k], m1("final", k), rstd[:, 1], ALU.mult, ALU.mult)
            last.then_inc(layer_done, 1)

            with dve.Fori(0, LAYERS) as l:
                link[0], link[1] = l, 0
                first = layer_panel(l, 0)
                low(first[0], first[1] % SLOTS)
                dve.wait_ge(v2_in, l * 16 + 16)
                v.tensor_tensor(scol[:, 32:34], m2("lam_q", 0, 2), m2("lam_k", 0, 2), ALU.mult).then_inc(lam_mul, 1)
                lstep(v.tensor_tensor(scol[:, 34:35], m2("subln"), m2("one_less"), ALU.mult))
                dve.wait_ge(lam_exp, at(lam_exp, l, 1))
                lstep(v.tensor_tensor(scol[:, 36:37], scol[:, 39:40], scol[:, 38:39], ALU.subtract))
                v.tensor_scalar(scol[:, 40:48], scol[:, 48:56], -1.0, None, ALU.mult)
                v.tensor_tensor(scol[:, 36:37], scol[:, 36:37], m2("lam_init"), ALU.subtract).then_inc(lam_set, 1)
                dve.wait_ge(lam_set, at(lam_set, l, 1))
                norm(0, h, lambda k: m2("attn_norm", k), None, 0, l)
                def low_next(i):
                    low(l * PER_LAYER + (G_LAYER + i + 1), (G_LAYER + i + 1) % SLOTS)

                def head_scale(n):
                    c, w, gain = ROPES[n][:3]
                    dve.wait_ge(rp_rs, at(rp_rs, l, n + 1))
                    v.scalar_tensor_tensor(flatc(c, w), flatc(c, w), m2(gain), nrs[:, 0:w].rearrange("p c t -> p (c t)"),
                                           ALU.mult, ALU.mult).then_inc(rp_n, 1)

                def head_rope(n):
                    c, w, _, _, cs_, sn = ROPES[n]
                    x = chunks(c, w)
                    dve.wait_ge(rp_rot, at(rp_rot, l, n + 1))
                    def wide(name):
                        return tb(name).unsqueeze(1).to_broadcast([P, w, T])
                    v.tensor_tensor(nrot[:, 0:w], ps[:, 4:6].rearrange("p b (c t) -> p (b c) t", t=T)[:, 0:w], wide(sn),
                                    ALU.mult)
                    lstep(v.tensor_tensor(x, x, wide(cs_), ALU.mult))
                    v.tensor_tensor(flatc(c, w), flatc(c, w), nrot[:, 0:w].rearrange("p c t -> p (c t)"), ALU.add
                                    ).then_inc(rp_done, 1)
                dve.wait_ge(tab_in, 16)
                for i in range(N_HEADS):
                    low_next(i)
                    if i in ROPE_IN:
                        head_rope(ROPE_IN[i])
                    if i in SCALE_IN:
                        head_scale(SCALE_IN[i])
                def stats(n):
                    return smx[:, n % 4]
                def top(n):
                    dve.wait_ge(sc_mm, at(sc_mm, l, n + 1))
                    st = stats(n)
                    lstep(v.tensor_reduce(st[:, 0:2], ps[:, 2 + 2 * (n % 2):4 + 2 * (n % 2), 0:T], AX, ALU.max,
                                          negate=True))
                    v.tensor_scalar(st[:, 2:4], st[:, 0:2], 0.125, None, ALU.mult).then_inc(sc_max, 1)
                def weights(n):
                    dve.wait_ge(sc_exp, at(sc_exp, l, n + 1))
                    st, e = stats(n), ew[n % 2]
                    lstep(v.reciprocal(st[:, 6:8], st[:, 4:6]))
                    if n < 8:
                        lstep(v.tensor_tensor(st[:, 7:8], st[:, 7:8], scol[:, 36:37], ALU.mult))
                        lstep(v.tensor_scalar(e[:, 0], e[:, 0], st[:, 6:7], None, ALU.mult))
                        v.scalar_tensor_tensor(e[:, 0], e[:, 1], st[:, 7:8], e[:, 0], ALU.mult, ALU.add).then_inc(sc_w, 1)
                    else:
                        v.tensor_scalar(e[:, 0], e[:, 0], st[:, 6:7], None, ALU.mult)
                        v.tensor_scalar(e[:, 1], e[:, 1], st[:, 7:8], None, ALU.mult).then_inc(sc_w, 1)
                def decay(g):
                    lstep(v.tensor_scalar(Dm[g % 2].rearrange("p u t -> p (u t)"), tb("ahead"), scol[:, 40 + g:41 + g],
                                          None, ALU.mult))
                    v.scalar_tensor_tensor(Dm[g % 2].rearrange("p u t -> p (u t)"), tb("behind"), scol[:, 44 + g:45 + g],
                                           Dm[g % 2].rearrange("p u t -> p (u t)"), ALU.mult, ALU.add).then_inc(rt_arg, 1)

                def decayed(g):
                    dve.wait_ge(rt_dec, at(rt_dec, l, g + 1))
                    dve.wait_ge(rt_mm, at(rt_mm, l, g + 1))
                    if g >= 2:
                        dve.wait_ge(rt_pv, at(rt_pv, l, g - 1))
                    v.scalar_tensor_tensor(sD[g % 2].rearrange("p u t -> p (u t)"), ps[:, 0], P ** -0.5,
                                           Dm[g % 2].rearrange("p u t -> p (u t)"), ALU.mult, ALU.mult
                                           ).then_inc(rt_mul, 1)
                top(0)
                for n in range(PAIRS):
                    if n + 1 < PAIRS:
                        top(n + 1)
                    weights(n)
                    if N_HEADS + n < N_PROJ:
                        low_next(N_HEADS + n)
                    g = n - (PAIRS - HEADS)
                    if g >= 0:
                        decayed(g)
                    if -1 <= g < HEADS - 1:
                        if g >= 1:
                            dve.wait_ge(rt_mul, at(rt_mul, l, g))
                        decay(g + 1)
                rl = l * R_PER_LAYER + R_LAYER

                def branch_stage(n):
                    return row_stage(layer_panel(l, O_BR + n * N_BR), N_BR, chunk_src(BRANCHES[n][0]), rl + RO_BR + n * N_BR,
                                     R_LAYER + RO_BR + n * N_BR, T)
                dve.wait_ge(pv_out, at(pv_out, l, 8))
                end = branch_stage(0)
                dve.wait_ge(gn_mean, at(gn_mean, l, 1))
                for b in range(2):
                    last = v.scalar_tensor_tensor(flatc(RQ + 2 * b, 2), ps[:, 6 + b], -1.0 / P, flatc(RQ + 2 * b, 2),
                                                  ALU.mult, ALU.add)
                last.then_inc(gn_cen, 1)
                dve.wait_ge(sub_rs, at(sub_rs, l, 1))
                v.scalar_tensor_tensor(flatc(DQ, 4), flatc(DQ, 4), scol[:, 34:35], nrs.rearrange("p c t -> p (c t)"),
                                       ALU.mult, ALU.mult).then_inc(sub_done, 1)
                dve.wait_ge(gn_rs, at(gn_rs, l, 1))
                for g in range(HEADS):
                    last = v.scalar_tensor_tensor(big[:, RQ + g], big[:, RQ + g], m2("ret_gain", g), nrot[:, g], ALU.mult,
                                                  ALU.mult)
                lstep(last)
                dve.wait_ge(gate_on, at(gate_on, l, 4))
                v.tensor_tensor(flatc(RQ, 4), flatc(RQ, 4), flatc(RG, 4), ALU.mult).then_inc(gn_done, 1)
                dve.wait_ge(gn_done, at(gn_done, l, 1))
                for n, (_, gt) in enumerate(BRANCHES):
                    if n:
                        end = branch_stage(n)
                    dve.wait_ge(panel_used, end)
                    b0 = 4 * (n % 2)
                    for b in range(4):
                        last = v.tensor_tensor(flatc(GT + gt + 2 * b, 2), flatc(GT + gt + 2 * b, 2), ps[:, b0 + b], ALU.mult)
                    if n:
                        lstep(last)
                        last = v.tensor_tensor(flatc(GT, 8), flatc(GT, 8), flatc(GT + (8 if n == 2 else 16), 8), ALU.add)
                    last.then_inc(gate_done, 1)
                    dve.wait_ge(gate_done, at(gate_done, l, n + 1))
                end = row_stage(layer_panel(l, O_OUT), N_OUT, chunk_src(GT), rl + RO_OUT, R_LAYER + RO_OUT, T)
                dve.wait_ge(panel_used, end)
                for b in range(4):
                    last = v.tensor_tensor(h[:, 2 * b:2 * b + 2].rearrange("p c t -> p (c t)"),
                                           h[:, 2 * b:2 * b + 2].rearrange("p c t -> p (c t)"), ps[:, b], ALU.add)
                last.then_inc(res_done, 1)
                norm(1, h, lambda k: m2("mlp_norm", k), None, 0, l)
                low_stage(layer_panel(l, O_MIN), N_MIN)
                dve.wait_ge(m_done, at(m_done, l, N_MIN))
                end = row_stage(layer_panel(l, O_MOUT), N_MOUT, chunk_src(0), rl + RO_MOUT, R_LAYER + RO_MOUT, T, last=False)
                dve.wait_ge(panel_used, end)
                for b in range(4):
                    last = v.tensor_tensor(h[:, 2 * b:2 * b + 2].rearrange("p c t -> p (c t)"),
                                           h[:, 2 * b:2 * b + 2].rearrange("p c t -> p (c t)"), ps[:, b], ALU.add)
                last.then_inc(layer_done, 1)
            assert link[1] == per["dve_link"], link[1]

        @block.scalar
        def _(act):
            a = nc.scalar
            count = [0]
            link = [0, 0]

            def step(ins):
                count[0] += 1
                ins.then_inc(act_chain, 1)
                act.wait_ge(act_chain, count[0])

            def lstep(ins):
                link[1] += 1
                ins.then_inc(act_link, 1)
                act.wait_ge(act_link, at(act_link, link[0], link[1]))

            def rms(dst, src, n, e, st):
                st(a.activation(dst, src, ACT.Ln, bias=eps[:, e:e + 1], scale=1.0 / n))
                return a.activation(dst, dst, ACT.Exp, scale=-0.5)

            def norm_rms(n, src, l=None):
                val = (lambda s: at(s, l, n + 1, base=6)) if l is not None else (lambda s: n + 1)
                a.activation(bigf[:, (n % 2) * 2048:(n % 2) * 2048 + 2048].rearrange("p (k t) -> p k t", t=T), src,
                             ACT.Square).then_inc(sq_done, 1)
                act.wait_ge(sum_done, val(sum_done))
                rms(rstd[:, n % 2], ps[:, 6 + n % 2, 0:T], D, 0, step if l is None else lstep).then_inc(rstd_done, 1)

            def norm_parts(n, shift, dst0, l=None):
                tmp = bigf[:, 4096:4096 + KD * T].rearrange("p (k t) -> p k t", t=T)
                for k in range(KD):
                    c = n * KD + k + 1
                    act.wait_ge(norm_scaled, at(norm_scaled, l, c, base=5 * KD) if l is not None else c)
                    bias = {} if shift is None else {"bias": shift(k)}
                    a.activation(xhi[:, k, dst0:dst0 + T], tmp[:, k], ACT.Identity, **bias).then_inc(norm_hi, 1)

            def mcolumn(n, who):
                return lambda k: mcol[:, 8 * n + k, who:who + 1]

            def up_stage(g0, which, t):
                def body(i, g, s):
                    act.wait_ge(panel_used, g + 1)
                    a.activation(hid_chunk(i, t), ps[:, 2 * ((s - g0) % UNROLL), 0:t], ACT.Silu).then_inc(silu_done, 1)
                panel_loop(act, g0, N_UP, body)

            def row_stage(first, n, src, r_phase, t):
                phase = first[1] if isinstance(first, tuple) else first

                def body(i, g, s):
                    act.wait_ge(panel_used, g - 1)
                    r = (r_phase + (s - phase) % UNROLL) % 2
                    a.activation(ahi[:, r, :, 0:t], src(i), ACT.Identity).then_inc(act_hi, 1)
                panel_loop(act, first, n, body)

            act.dma_start(v1[:], vec1).then_inc(small_in, 16)
            act.dma_start(h[:].rearrange("p k t -> p (k t)"), xT).then_inc(x_in, 16)
            act.dma_start(ws[:, 2048:4096], posemb).then_inc(x_in, 16)
            act.dma_start(ws[:, 0:2048], ctxT).then_inc(x_in, 16)
            act.dma_start(mat[:], mats).then_inc(small_in, 16)
            act.dma_start(mask_in, masks).then_inc(small_in, 16)
            act.wait_ge(small_in, 48)
            a.activation(scol[:, 0:2 * KD], m1("c", 0, 2 * KD), ACT.Silu).then_inc(c_silu, 1)
            act.wait_ge(c_silu, 1)
            act.wait_ge(x_zero, 2)
            a.activation(xhi[:, :, 0:2], scol[:, 0:2 * KD].rearrange("p (k b) -> p k b", b=2), ACT.Identity
                         ).then_inc(c_silu, 1)
            act.wait_ge(h_set, 2)
            act.wait_ge(const_set, 3)
            norm_rms(0, h[:])
            norm_rms(1, hc)
            with act.Fori(0, N_MOD // UNROLL) as i:
                for j in range(UNROLL):
                    act.wait_ge(panel_used, i * UNROLL + (G_MOD + j + 1))
                    a.activation(mrow[0:2, j], ps[0:2, j, 0:COLS], ACT.Identity).then_inc(mod_copied, 1)
            act.wait_ge(mod_turned, N_MOD)
            act.dma_start(ws[:, 4096:6144], lbrow).then_inc(lb_in, 16)
            norm_parts(0, mcolumn(0, 0), 0)
            norm_parts(1, mcolumn(0, 1), T)
            up_stage(G_UP1, 0, 2 * T)
            act.wait_ge(hid_done, KFF)
            row_stage(G_DOWN1, N_DOWN, hid_src(2 * T), R_DOWN1, 2 * T)
            act.wait_ge(h_set, 3)
            norm_rms(2, h[:])
            norm_rms(3, hc)
            norm_parts(2, mcolumn(3, 0), 0)
            norm_parts(3, mcolumn(3, 1), T)
            for i in range(N_WIN):
                act.wait_ge(panel_used, G_WIN + i + 1)
                two = ps[:, i % 4].rearrange("p (u n) -> p u n", n=COLS)
                ctx_two = ps[:, 4 + i % 2].rearrange("p (u n) -> p u n", n=COLS)
                if i < 2:
                    a.activation(Vx[:, :, i * COLS:(i + 1) * COLS], two, ACT.Identity)
                    last = a.activation(Vc[:, :, i * COLS:(i + 1) * COLS], ctx_two, ACT.Identity)
                elif i < 6:
                    d, half = divmod(i - 2, 2)
                    a.activation(chunks(KF[d] + 2 * half, 2), two, ACT.Sigmoid)
                    last = a.activation(sc[d][:, :, half * COLS:(half + 1) * COLS], ctx_two, ACT.Sigmoid)
                else:
                    c, f = ((Q0, ACT.Silu) if i < 8 else (G0 - 4, ACT.Silu) if i < 10 else (HY - 8, ACT.Identity) if i < 16
                            else (MG - 20, ACT.Sigmoid))
                    last = a.activation(chunks(c + 2 * (i - 6), 2), two, f)
                last.then_inc(win_out, 1)
            act.wait_ge(lb_diff, 2)
            a.activation(scol[:, 16:24], scol[:, 16:24], ACT.Sigmoid).then_inc(lb_sig, 1)
            a.activation(lrow[:, 0], lrow[:, 0], ACT.Sigmoid).then_inc(lb_sig, 1)
            for d in range(2):
                act.wait_ge(cf_done, d + 1)
                if d:
                    act.wait_ge(ckey_done, d)
                a.activation(lgc, sc[d], ACT.Ln).then_inc(cln_done, 1)
                act.wait_ge(csum_done, d + 1)
                a.activation(lgc, ps[:, 0:2], ACT.Exp).then_inc(cdec_done, 1)
                act.wait_ge(cst_done, d + 1)
                a.activation(s0[d], ps[:, 2 + d].rearrange("p (g e) -> p g e", e=P), ACT.Identity).then_inc(cst_out, 1)
            for d in range(2):
                act.wait_ge(xf_done, d + 1)
                a.activation(EMf[d], flatc(KF[d], 4), ACT.Ln).then_inc(xln_done, 1)
            for m, (d, n) in enumerate(levels[:-1]):
                act.wait_ge(lv_diff, m + 1)
                if n < len(LEVELS):
                    first, second = halves(EMf[m % 2], LEVELS[n])
                    a.activation(second, second, ACT.Exp)
                    a.activation(first, first, ACT.Exp, scale=-1.0).then_inc(lv_exp, 1)
                else:
                    e = EM[m % 2].rearrange("p (g u) s -> p g u s", u=TT)
                    x = XC[d].rearrange("p (g u) s -> p g u s", u=TT)
                    a.activation(e[:, :, 0], e[:, :, 0], ACT.Exp)
                    a.activation(e[:, :, 1], x[:, :, 1, 1 - d:1 - d + P], ACT.Exp).then_inc(lv_exp, 1)
            act.wait_ge(qe_diff, 1)
            a.activation(EMf[0], EMf[0], ACT.Exp)
            a.activation(EMf[1], EMf[1], ACT.Exp).then_inc(qe_exp, 1)
            act.wait_ge(o_done, 1)
            a.activation(EMf[0], ps[:, 4:6].rearrange("p b t -> p (b t)"), ACT.Square).then_inc(osq_done, 1)
            act.wait_ge(osum_done, 1)
            rms(EMf[1], ps[:, 6:8].rearrange("p b t -> p (b t)"), P, 0, step).then_inc(orstd_done, 1)
            act.wait_ge(oa_done, 1)
            act.dma_start(hcon, hyc).then_inc(hy_in, 16)
            act.dma_start(win.rearrange("p u c -> p (u c)"), window).then_inc(hy_in, 16)
            act.dma_start(zfeat, zT).then_inc(hy_in, 16)
            act.dma_start(hyin[0:64], hyw).then_inc(hy_in, 16)
            for n in range(2):
                act.wait_ge(fl_arg, n + 1)
                a.activation(h2[0:64], ang[0:64, 0], ACT.Sin).then_inc(fl_sin, 1)
            act.wait_ge(conv_done, 2)
            for o in range(2):
                act.wait_ge(win_mul, 4 * (o + 1))
                if o:
                    act.wait_ge(z_done, o)
                a.activation(absk, kern.rearrange("p u d c -> p (u d c)"), ACT.Abs).then_inc(abs_done, 1)
                act.wait_ge(l1_mm, o + 1)
                act.wait_ge(turn_done, o + 1)
                a.activation(uT, ps[:, 5:7], ACT.Identity).then_inc(uT_done, 1)
            act.wait_ge(oa_done, 1)
            act.wait_ge(z_done, 2)
            act.dma_start(tab, tabs).then_inc(tab_in, 16)
            row_stage(G_PA, N_BR, chunk_src(Q0), R_PA, T)
            row_stage(G_PB, N_BR, chunk_src(ZC[0]), R_PB, T)
            act.wait_ge(gate1_done, 2)
            row_stage(G_OUT1, N_OUT, chunk_src(MG), R_OUT1, T)
            act.wait_ge(h_set, 4)
            norm_rms(4, h[:])
            norm_parts(4, mcolumn(6, 0), 0)
            up_stage(G_UP2, 1, T)
            act.wait_ge(hid_done, 2 * KFF)
            row_stage(G_DOWN2, N_DOWN, hid_src(T), R_DOWN2, T)
            act.wait_ge(h_set, 5)
            norm_rms(5, h[:])

            with act.Fori(0, LAYERS) as l:
                link[0], link[1] = l, 0
                act.wait_ge(layer_done, l + 1)
                act.dma_start(v2[:], vec2[ds(l, 1)].rearrange("a p n -> p (a n)")).then_inc(v2_in, 16)
                norm_rms(0, h[:], l)
                act.wait_ge(v2_in, l * 16 + 16)
                a.activation(scol[:, 48:56], m2("decay", 0, 8), ACT.Exp)
                act.wait_ge(lam_mm, at(lam_mm, l, 1))
                a.activation(scol[:, 38:40], ps[:, 5, 0:2], ACT.Exp).then_inc(lam_exp, 1)
                norm_parts(0, None, 0, l)
                act.wait_ge(tab_in, 16)
                dests = ((VD, 0), (VD, 1), (VR, 0), (VR, 1), (VG, 0))

                def projected(i):
                    act.wait_ge(panel_used, l * PER_LAYER + (G_LAYER + i + 1))
                    two = ps[:, i % 2].rearrange("p (u n) -> p u n", n=COLS)
                    if i < N_VALUES:
                        dst, k = dests[i]
                        if dst is VG:
                            ins = a.activation(VG, two[:, :, 0:P], ACT.Identity)
                        else:
                            ins = a.activation(dst[:, :, k * COLS:(k + 1) * COLS], two, ACT.Identity)
                    else:
                        ins = a.activation(chunks(PLAIN[i - N_VALUES], 2), two, ACT.Identity)
                    ins.then_inc(proj_out, 1)

                def head_square(n):
                    act.wait_ge(proj_out, at(proj_out, l, (7, 9, 11, 12)[n]))
                    c, w = ROPES[n][:2]
                    a.activation(nsq[:, 0:w], chunks(c, w), ACT.Square).then_inc(rp_sq, 1)

                def head_rms(n):
                    w = ROPES[n][1]
                    act.wait_ge(rp_sum, at(rp_sum, l, n + 1))
                    if n:
                        act.wait_ge(rp_n, at(rp_n, l, n))
                    rms(nrs[:, 0:w], ps[:, 2:4].rearrange("p b (c t) -> p (b c) t", t=T)[:, 0:w], 64, 0, lstep
                        ).then_inc(rp_rs, 1)
                for i in range(N_HEADS):
                    projected(i)
                    if i in RMS_AFTER:
                        head_rms(RMS_AFTER[i])
                    if i in SQUARE_AFTER:
                        head_square(SQUARE_AFTER[i])

                def expo(n):
                    act.wait_ge(sc_max, at(sc_max, l, n + 1))
                    if n >= 2:
                        act.wait_ge(sc_turn, at(sc_turn, l, n - 1))
                    st = smx[:, n % 4]
                    for m in range(2):
                        last = a.activation(ew[n % 2][:, m], ps[:, 2 + 2 * (n % 2) + m, 0:T], ACT.Exp, bias=st[:, 2 + m:3 + m],
                                            scale=0.125, accum_out=st[:, 4 + m:5 + m])
                    last.then_inc(sc_exp, 1)

                def turned(n):
                    act.wait_ge(sc_turn, at(sc_turn, l, n + 1))
                    p, u = divmod(n, 2)
                    if p >= 2:
                        act.wait_ge(pv_mm, at(pv_mm, l, p - 1))
                    k = 1 if n < 8 else 2
                    for m in range(k):
                        last = a.activation(wT[p % 2][:, m, :, u * P:(u + 1) * P],
                                            ps[:, 6, m * T:(m + 1) * T].rearrange("p (k q) -> p k q", q=P),
                                            ACT.Identity)
                    last.then_inc(sc_wT, 1)

                def attended(p):
                    act.wait_ge(pv_mm, at(pv_mm, l, p + 1))
                    a.activation(big[:, DQ + p if p < 4 else GQ + p - 4], ps[:, 7, 0:T], ACT.Identity
                                 ).then_inc(pv_out, 1)

                def retained(f):
                    act.wait_ge(rt_pv, at(rt_pv, l, f + 1))
                    a.activation(big[:, RQ + f], ps[:, 1, 0:T], ACT.Identity).then_inc(rt_out, 1)
                expo(0)
                for n in range(PAIRS):
                    if n + 1 < PAIRS:
                        expo(n + 1)
                    if N_HEADS + n < N_PROJ:
                        projected(N_HEADS + n)
                    g = n - (PAIRS - HEADS)
                    if g >= 0:
                        act.wait_ge(rt_arg, at(rt_arg, l, g + 1))
                        a.activation(Dm[g % 2], Dm[g % 2], ACT.Exp).then_inc(rt_dec, 1)
                    turned(n)
                    if g >= 1:
                        retained(g - 1)
                    if n % 2 and n > 1:
                        attended(n // 2 - 1)
                attended(7)
                retained(HEADS - 1)
                act.wait_ge(pv_out, at(pv_out, l, 8))
                act.wait_ge(rt_out, at(rt_out, l, HEADS))
                a.activation(nsq, chunks(DQ, 4), ACT.Square).then_inc(sub_sq, 1)

                def branch_stage(n):
                    row_stage(layer_panel(l, O_BR + n * N_BR), N_BR, chunk_src(BRANCHES[n][0]), R_LAYER + RO_BR + n * N_BR, T)
                branch_stage(0)
                act.wait_ge(sub_sum, at(sub_sum, l, 1))
                act.wait_ge(rt_mul, at(rt_mul, l, HEADS))
                rms(nrs, ps[:, 4:6].rearrange("p b (c t) -> p (b c) t", t=T), P, 1, lstep).then_inc(sub_rs, 1)
                act.wait_ge(proj_out, at(proj_out, l, N_PROJ))
                for _, gt in BRANCHES:
                    a.activation(chunks(GT + gt, 8), chunks(GT + gt, 8), ACT.Sigmoid).then_inc(gate_on, 1)
                a.activation(chunks(RG, 4), chunks(RG, 4), ACT.Silu).then_inc(gate_on, 1)
                act.wait_ge(gn_cen, at(gn_cen, l, 1))
                a.activation(nsq, chunks(RQ, 4), ACT.Square).then_inc(gn_sq, 1)
                act.wait_ge(gn_sum, at(gn_sum, l, 1))
                rms(nrot, ps[:, 4:6].rearrange("p b (c t) -> p (b c) t", t=T), P, 1, lstep).then_inc(gn_rs, 1)
                act.wait_ge(sub_done, at(sub_done, l, 1))
                branch_stage(1)
                act.wait_ge(gn_done, at(gn_done, l, 1))
                branch_stage(2)
                act.wait_ge(gate_done, at(gate_done, l, 3))
                row_stage(layer_panel(l, O_OUT), N_OUT, chunk_src(GT), R_LAYER + RO_OUT, T)
                act.wait_ge(res_done, at(res_done, l, 1))
                norm_rms(1, h[:], l)
                norm_parts(1, None, 0, l)
                mfirst = layer_panel(l, O_MIN)

                def relu2(i, g, s):
                    j = (s - mfirst[1]) % UNROLL
                    act.wait_ge(panel_used, g + 1)
                    a.activation(rtmp[j % 2], ps[:, j], ACT.Relu).then_inc(relu_done, 1)
                    act.wait_ge(relu_done, at(relu_done, l, 1) + i)
                    a.activation(big[:, ds(i * 2, 2), :].rearrange("p c t -> p (c t)"), rtmp[j % 2], ACT.Square
                                 ).then_inc(m_done, 1)
                panel_loop(act, mfirst, N_MIN, relu2)
                act.wait_ge(m_done, at(m_done, l, N_MIN))
                row_stage(layer_panel(l, O_MOUT), N_MOUT, chunk_src(0), R_LAYER + RO_MOUT, T)
            assert link[1] == per["act_link"], link[1]

        @block.tensor
        def _(pe):
            mm = nc.tensor.matmul

            def product(out, w_hi, w_lo, x_hi, x_lo, first, last):
                mm(out, w_hi, x_hi, start=first, stop=False, skip_group_check=True)
                mm(out, w_hi, x_lo, start=False, stop=False, skip_group_check=True)
                return mm(out, w_lo, x_hi, start=False, stop=last, skip_group_check=True)

            def feature_panel(s, outs, x0, t):
                for c, out in enumerate(outs):
                    for k in range(KD):
                        at_ = k * COLS + c * P
                        last = product(out, whi[:, s % 2, at_:at_ + P], wlo[:, s % 2, at_:at_ + P], xhi[:, k, x0:x0 + t],
                                       xlo[:, k, x0:x0 + t], k == 0, k == KD - 1)
                return last

            def token_panel(s, outs, x0, n):
                for u, out in enumerate(outs):
                    for k in range(KD):
                        x = slice(x0 + u * P, x0 + (u + 1) * P)
                        c = slice(k * COLS, k * COLS + n)
                        last = product(out, xhi[:, k, x], xlo[:, k, x], whi[:, s % 2, c], wlo[:, s % 2, c], k == 0, k == KD - 1)
                return last

            def row_panel(s, r, outs, t, first, last):
                for j, (out, opens) in enumerate(outs):
                    for k in range(ROWK):
                        w = slice(k * D + j * P, k * D + (j + 1) * P)
                        ins = product(out, whi[:, s % 2, w], wlo[:, s % 2, w], ahi[:, r % 2, k, 0:t], alo[:, r % 2, k, 0:t],
                                      first and opens and k == 0, last and k == ROWK - 1)
                return ins

            def sums(b0, t=T):
                if t == T:
                    return [(ps[:, b0 + j // 2, (j % 2) * T:(j % 2 + 1) * T], j % 2 == 0) for j in range(KD)]
                return [(ps[:, j, 0:t], True) for j in range(KD)]

            def row_stage(first, n, r0, r_phase, outs, t):
                g0, phase = first if isinstance(first, tuple) else (first, first)

                def one(i, g, s, begins, ends):
                    pe.wait_ge(lo_done, g + 1)
                    pe.wait_ge(act_lo, r0 + i + 1)
                    row_panel(s, r_phase + (s - phase) % UNROLL, outs, t, begins, ends).then_inc(panel_used, 1)
                one(0, g0, phase % UNROLL, True, False)
                nxt = (g0 + 1, phase + 1) if isinstance(first, tuple) else g0 + 1
                panel_loop(pe, nxt, n - 2, lambda i, g, s: one(i + 1, g, s, False, False))
                one(n - 1, g0 + (n - 1), (phase + n - 1) % UNROLL, False, True)

            def norm_sums(n, l=None):
                pe.wait_ge(sq_done, at(sq_done, l, n + 1, base=6) if l is not None else n + 1)
                sq = bigf[:, (n % 2) * 2048:(n % 2) * 2048 + 2048].rearrange("p (k t) -> p k t", t=T)
                for k in range(KD):
                    last = mm(ps[:, 6 + n % 2, 0:T], ones[:], sq[:, k], start=k == 0, stop=k == KD - 1)
                last.then_inc(sum_done, 1)

            def up_stage(g0, which, t):
                def one(i, g, s, reused):
                    j = (s - g0) % UNROLL
                    pe.wait_ge(lo_done, g + 1)
                    if reused:
                        pe.wait_ge(hid_done, i + (which * KFF - UNROLL + 1))
                    feature_panel(s, [ps[:, 2 * j, 0:t], ps[:, 2 * j + 1, 0:t]], 0, t).then_inc(panel_used, 1)
                for i in range(UNROLL):
                    one(i, g0 + i, (g0 + i) % UNROLL, False)
                panel_loop(pe, g0 + UNROLL, N_UP - UNROLL, lambda i, g, s: one(i + UNROLL, g, s, True))

            def halves_of(b):
                return [ps[:, b, 0:T], ps[:, b, T:2 * T]]

            pe.wait_ge(h_set, 2)
            pe.wait_ge(const_set, 3)
            norm_sums(0)
            norm_sums(1)
            pe.wait_ge(c_split, 1)

            def turn(i, j):
                pe.wait_ge(mod_copied, i * UNROLL + (j + 1))
                if j == 0:
                    pe.wait_ge(mod_added, i + 1)
                pe.wait_ge(small_in, 48)
                for c in range(2):
                    last = mm(ps[:, 4, 4 * j + 2 * c:4 * j + 2 * c + 2], mrow[0:2, j, c * P:(c + 1) * P], ident[0:2, 0:2],
                              start=True, stop=True)
                last.then_inc(mod_turned, 1)

            with pe.Fori(0, N_MOD // UNROLL) as i:
                for j in range(UNROLL):
                    pe.wait_ge(lo_done, i * UNROLL + (G_MOD + j + 1))
                    for k in range(KD):
                        w = slice(k * COLS, (k + 1) * COLS)
                        last = product(ps[:, j, 0:COLS], xhi[:, k, 0:P], xlo[:, k, 0:P], whi[:, j % 2, w], wlo[:, j % 2, w],
                                       k == 0, k == KD - 1)
                    last.then_inc(panel_used, 1)
                    if j:
                        turn(i, j - 1)
                turn(i, UNROLL - 1)

            pe.wait_ge(norm_lo, 2 * KD)
            up_stage(G_UP1, 0, 2 * T)
            pe.wait_ge(hid_done, KFF)
            row_stage(G_DOWN1, N_DOWN, R_DOWN1, R_DOWN1, sums(0, 2 * T), 2 * T)
            norm_sums(2)
            norm_sums(3)
            pe.wait_ge(norm_lo, 4 * KD)

            def win_panel(i, g, s):
                pe.wait_ge(lo_done, g + 1)
                if not isinstance(i, int) or i >= 4:
                    pe.wait_ge(win_out, i - 3)
                bank = (s - G_WIN) % 4
                if not isinstance(i, int) or i >= 6:
                    last = feature_panel(s, halves_of(bank), 0, T)
                else:
                    if i >= 2:
                        pe.wait_ge(win_out, i - 1)
                    both = [ps[:, 4 + i % 2, 0:COLS], ps[:, 4 + i % 2, COLS:2 * COLS]]
                    token_panel(s, both, T, COLS)
                    if i < 2:
                        last = token_panel(s, [ps[:, bank, 0:COLS], ps[:, bank, COLS:2 * COLS]], 0, COLS)
                    else:
                        last = feature_panel(s, halves_of(bank), 0, T)
                last.then_inc(panel_used, 1)
            for i in range(6):
                win_panel(i, G_WIN + i, (G_WIN + i) % UNROLL)
            panel_loop(pe, G_WIN + 6, N_WIN - 6, lambda i, g, s: win_panel(i + 6, g, s))
            pe.wait_ge(win_out, N_WIN)
            for d, order in enumerate(("after", "before")):
                pe.wait_ge(cln_done, d + 1)
                if d:
                    pe.wait_ge(cdec_done, d)
                near, far = d, 1 - d
                mm(ps[:, far], mt(order), lgc[:, far], start=True, stop=True)
                mm(ps[:, near], mt(order), lgc[:, near], start=True, stop=False)
                mm(ps[:, near], ones[:], lgc[:, far], start=False, stop=True).then_inc(csum_done, 1)
                pe.wait_ge(ckey_done, d + 1)
                for g in range(HEADS):
                    for u in range(TT):
                        last = mm(ps[:, 2 + d, g * P:(g + 1) * P], sc[d][:, u, g * P:(g + 1) * P], Vc[:, u, g * P:(g + 1) * P],
                                  start=u == 0, stop=u == TT - 1)
                last.then_inc(cst_done, 1)
            q = flatc(Q0, 4)
            pe.wait_ge(cst_out, 2)
            for m, (d, n) in enumerate(levels):
                if d == 2:
                    pe.wait_ge(lv_diff, m + 1)
                else:
                    pe.wait_ge(lv_mul, m + 1)
                if m >= 2:
                    pe.wait_ge(lv_sel, m - 1)
                e, b = EM[m % 2], 2 * (m % 2)
                for x in range(HEADS * TT):
                    g, u = divmod(x, TT)
                    o = slice(g * P, (g + 1) * P)
                    if d == 2:
                        last = mm(ps[:, b + u, o], e[:, x], q[:, x * P:(x + 1) * P], start=True, stop=True)
                    elif n < len(LEVELS):
                        last = mm(ps[:, b + u, o], e[:, x], e[:, x], start=True, stop=True)
                    elif u == d:
                        last = mm(ps[:, b, o], e[:, x], e[:, 2 * g + 1 - d], start=True, stop=True)
                last.then_inc(lv_score, 1)
            pe.wait_ge(lv_sel, len(levels))
            pe.wait_ge(qe_done, 1)
            for g in range(HEADS):
                o = halves_of(4 + g // 2)[g % 2]
                for u in range(TT):
                    mm(o, Vx[:, u, g * P:(g + 1) * P], S[:, u, g], start=u == 0, stop=False)
                for d in range(2):
                    last = mm(o, s0[d][:, g], EMf[d][:, g * T:(g + 1) * T], start=False, stop=d == 1)
            last.then_inc(o_done, 1)
            pe.wait_ge(osq_done, 1)
            for g in range(HEADS):
                last = mm(halves_of(6 + g // 2)[g % 2], ones[:], EMf[0][:, g * T:(g + 1) * T], start=True, stop=True)
            last.then_inc(osum_done, 1)
            pe.wait_ge(hy_in, 64)
            pe.wait_ge(oa_done, 1)
            mm(ps[0:64, 0, 0:T], hw1, zfeat[0:33], start=True, stop=True).then_inc(fl_mm, 1)
            pe.wait_ge(fl_sin, 1)
            mm(ps[0:64, 0, 0:T], hw2, h2[0:64], start=True, stop=True).then_inc(fl_mm, 1)
            pe.wait_ge(fl_sin, 2)
            for o in range(2):
                if o:
                    pe.wait_ge(z_done, o)
                for u in range(TT):
                    for d in range(2):
                        mm(ps[:, 2 * u + d], h2[0:64, u * P:(u + 1) * P], hw3[:, (2 * o + d) * 512:(2 * o + d + 1) * 512],
                           start=True, stop=True).then_inc(h3_mm, 1)
                pe.wait_ge(abs_done, o + 1)
                for x in range(4):
                    last = mm(ps[:, 4], ones[:], absk[:, x * 512:(x + 1) * 512], start=x == 0, stop=x == 3)
                last.then_inc(l1_mm, 1)
                if o == 0:
                    pe.wait_ge(conv_done, 1)
                for c in range(4):
                    for u in range(TT):
                        last = nc.tensor.transpose(ps[:, 5 + u, c * P:(c + 1) * P], big[:, ZC[0] + c, u * P:(u + 1) * P], ident)
                last.then_inc(turn_done, 1)
                pe.wait_ge(win_mul, 4 * (o + 1))
                for m in range(4):
                    f = slice(m * P, (m + 1) * P)
                    for u in range(TT):
                        for d in range(2):
                            last = mm(ps[:, m], dft[d][:, u, f], kern[:, u, d], start=u + d == 0, stop=u + d == 2)
                    last.then_inc(kf_mm, 1)
                pe.wait_ge(uT_done, o + 1)
                pe.wait_ge(kf_done, o + 1)
                for m in range(4):
                    for u in range(TT):
                        last = mm(ps[:, 4 + m], dft[0][:, u, m * P:(m + 1) * P], uT[:, u], start=u == 0, stop=u == 1)
                last.then_inc(uf_mm, 1)
                pe.wait_ge(pf_done, o + 1)
                for c in range(4):
                    for m in range(4):
                        f = (Pf, Pi)[m // 2][:, m % 2, c * P:(c + 1) * P]
                        last = mm(halves_of(c // 2)[c % 2], f, idft[:, m], start=m == 0, stop=m == 3)
                last.then_inc(y_mm, 1)
            row_stage(G_PA, N_BR, R_PA, R_PA, sums(0), T)
            row_stage(G_PB, N_BR, R_PB, R_PB, sums(4), T)
            row_stage(G_OUT1, N_OUT, R_OUT1, R_OUT1, sums(0), T)
            norm_sums(4)
            pe.wait_ge(norm_lo, 5 * KD)
            up_stage(G_UP2, 1, T)
            row_stage(G_DOWN2, N_DOWN, R_DOWN2, R_DOWN2, sums(0), T)
            norm_sums(5)

            with pe.Fori(0, LAYERS) as l:
                norm_sums(0, l)
                pe.wait_ge(lam_mul, at(lam_mul, l, 1))
                mm(ps[:, 5, 0:2], ones[:], scol[:, 32:34], start=True, stop=True).then_inc(lam_mm, 1)
                pe.wait_ge(norm_lo, at(norm_lo, l, KD, base=5 * KD))
                def proj(i):
                    pe.wait_ge(lo_done, l * PER_LAYER + (G_LAYER + i + 1))
                    if i >= 2:
                        pe.wait_ge(proj_out, at(proj_out, l, i - 1))
                    s, j = (G_LAYER + i) % UNROLL, i % 2
                    if i < N_VALUES:
                        n = COLS if i < 4 else P
                        last = token_panel(s, [ps[:, j, 0:n], ps[:, j, COLS:COLS + n]], 0, n)
                    else:
                        last = feature_panel(s, halves_of(j), 0, T)
                    last.then_inc(panel_used, 1)

                def head_sums(n):
                    c, w = ROPES[n][:2]
                    pe.wait_ge(rp_sq, at(rp_sq, l, n + 1))
                    for x in range(w):
                        last = mm(halves_of(2 + x // 2)[x % 2], mt("block64"), nsq[:, x], start=True, stop=True)
                    last.then_inc(rp_sum, 1)

                def head_rotate(n, out):
                    c, w, gain, rot = ROPES[n][:4]
                    if gain:
                        pe.wait_ge(rp_n, at(rp_n, l, n + 1))
                    else:
                        pe.wait_ge(proj_out, at(proj_out, l, out))
                    if n:
                        pe.wait_ge(rp_done, at(rp_done, l, n))
                    for x in range(w):
                        last = mm(halves_of(4 + x // 2)[x % 2], mt(rot), big[:, c + x], start=True, stop=True)
                    last.then_inc(rp_rot, 1)
                for i in range(N_HEADS):
                    proj(i)
                    if i in ROT_AFTER:
                        head_rotate(*ROT_AFTER[i])
                    if i in SUM_AFTER:
                        head_sums(SUM_AFTER[i])

                def scores(n):
                    if n >= 2:
                        pe.wait_ge(sc_exp, at(sc_exp, l, n - 1))
                    hd, u = divmod(n, 2)
                    qc, kc = (DQ + hd, DK + hd) if n < 8 else (GQ + hd - 4, GK + (hd - 4) // 2)
                    for m in range(2):
                        r = slice(64 * m, 64 * m + 64)
                        last = mm(ps[:, 2 + 2 * (n % 2) + m, 0:T], big[r, qc, u * P:(u + 1) * P], big[r, kc], start=True,
                                  stop=True)
                    last.then_inc(sc_mm, 1)

                def turn_weights(n):
                    pe.wait_ge(sc_w, at(sc_w, l, n + 1))
                    if n >= 1:
                        pe.wait_ge(sc_wT, at(sc_wT, l, n))
                    for x in range(2 if n < 8 else 4):
                        m, k = divmod(x, 2)
                        last = nc.tensor.transpose(ps[:, 6, x * P:(x + 1) * P], ew[n % 2][:, m, k * P:(k + 1) * P], ident)
                    last.then_inc(sc_turn, 1)

                def attend(p):
                    pe.wait_ge(sc_wT, at(sc_wT, l, 2 * p + 2))
                    if p >= 1:
                        pe.wait_ge(pv_out, at(pv_out, l, p))
                    for m in range(1 if p < 4 else 2):
                        for k in range(TT):
                            if p < 4:
                                out_, val = ps[:, 7, 0:T], VD[:, k, p * P:(p + 1) * P]
                            else:
                                kv = (p - 4) // 2
                                out_, val = ps[64 * m:64 * m + 64, 7, 0:T], VG[:, k, kv * 64:kv * 64 + 64]
                            last = mm(out_, val, wT[p % 2][:, m, k], start=k == 0, stop=k == TT - 1)
                    last.then_inc(pv_mm, 1)

                def retention_scores(g):
                    if g == 0:
                        pe.wait_ge(proj_out, at(proj_out, l, N_PROJ))
                    else:
                        pe.wait_ge(rt_mul, at(rt_mul, l, g))
                    for u in range(TT):
                        last = mm(halves_of(0)[u], big[:, RK + g, u * P:(u + 1) * P], big[:, RQ + g], start=True, stop=True)
                    last.then_inc(rt_mm, 1)

                def retain(f):
                    pe.wait_ge(rt_mul, at(rt_mul, l, f + 1))
                    if f >= 1:
                        pe.wait_ge(rt_out, at(rt_out, l, f))
                    for u in range(TT):
                        last = mm(ps[:, 1, 0:T], VR[:, u, f * P:(f + 1) * P], sD[f % 2][:, u], start=u == 0, stop=u == TT - 1)
                    last.then_inc(rt_pv, 1)
                pe.wait_ge(rp_done, at(rp_done, l, len(ROPES)))
                scores(0)
                for n in range(PAIRS):
                    if n + 1 < PAIRS:
                        scores(n + 1)
                    if N_HEADS + n < N_PROJ:
                        proj(N_HEADS + n)
                    g = n - (PAIRS - HEADS)
                    if g >= 0:
                        retention_scores(g)
                    turn_weights(n)
                    if g >= 1:
                        retain(g - 1)
                    if n % 2 and n > 1:
                        attend(n // 2 - 1)
                attend(7)
                retain(HEADS - 1)
                pe.wait_ge(sub_sq, at(sub_sq, l, 1))
                for x in range(4):
                    last = mm(halves_of(4 + x // 2)[x % 2], ones[:], nsq[:, x], start=True, stop=True)
                last.then_inc(sub_sum, 1)
                pe.wait_ge(rt_out, at(rt_out, l, HEADS))
                for x in range(4):
                    last = mm(halves_of(6 + x // 2)[x % 2], ones[:], big[:, RQ + x], start=True, stop=True)
                last.then_inc(gn_mean, 1)
                rl = l * R_PER_LAYER + R_LAYER

                def branch_stage(n):
                    row_stage(layer_panel(l, O_BR + n * N_BR), N_BR, rl + RO_BR + n * N_BR, R_LAYER + RO_BR + n * N_BR,
                              sums(4 * (n % 2)), T)
                branch_stage(0)
                pe.wait_ge(gn_sq, at(gn_sq, l, 1))
                for x in range(4):
                    last = mm(halves_of(4 + x // 2)[x % 2], ones[:], nsq[:, x], start=True, stop=True)
                last.then_inc(gn_sum, 1)
                pe.wait_ge(gn_rs, at(gn_rs, l, 1))
                branch_stage(1)
                branch_stage(2)
                row_stage(layer_panel(l, O_OUT), N_OUT, rl + RO_OUT, R_LAYER + RO_OUT, sums(0), T)
                norm_sums(1, l)
                pe.wait_ge(norm_lo, at(norm_lo, l, 2 * KD, base=5 * KD))
                mfirst = layer_panel(l, O_MIN)

                def up(i, g, s):
                    pe.wait_ge(lo_done, g + 1)
                    if not isinstance(i, int) or i >= 4:
                        pe.wait_ge(relu_done, at(relu_done, l, 0) + (i - 3))
                    feature_panel(s, halves_of((s - mfirst[1]) % 4), 0, T).then_inc(panel_used, 1)
                for i in range(4):
                    up(i, mfirst[0] + i, (mfirst[1] + i) % UNROLL)
                panel_loop(pe, layer_panel(l, O_MIN + 4), N_MIN - 4, lambda i, g, s: up(i + 4, g, s))
                row_stage(layer_panel(l, O_MOUT), N_MOUT, rl + RO_MOUT, R_LAYER + RO_MOUT, sums(0), T)


def _column_panels(w, cols):
    w = w[:, cols] if cols is not None else w
    n = w.shape[1] // COLS
    return w.reshape(KD, P, n, COLS).transpose(2, 1, 0, 3).reshape(n, P, PANEL)


def _row_panels(w):
    n = w.shape[0] // (P * ROWK)
    return w.reshape(n, ROWK, P, D).transpose(0, 2, 1, 3).reshape(n, P, PANEL)


def _cols(x):
    x = np.asarray(x).reshape(-1)
    return x.reshape(-1, P).T


def _pad(x):
    out = np.zeros((P, 1), np.float32)
    out[:x.size, 0] = x.reshape(-1)
    return out


def _up_panels(gate, up):
    both = np.stack([gate.reshape(D, KFF, P), up.reshape(D, KFF, P)], 2).reshape(D, KFF * 2 * P)
    return _column_panels(both, None)


def kernel(**inputs):
    import concourse.bacc as _bacc
    from concourse import mybir as _mybir
    from concourse.bass_utils import run_bass_kernel_spmd as _run

    x = {k: np.asarray(v) for k, v in inputs.items()}
    def first(name):
        return x[name][0]

    panels = [_column_panels(first("mod_w"), None)]
    ffn = [[_up_panels(first("ffn_w_gate")[i], first("ffn_w_up")[i]), _row_panels(first("ffn_w_down")[i])] for i in range(2)]
    panels += ffn[0] + [_column_panels(first("w_in"), None), _row_panels(first("w_proj_a")), _row_panels(first("w_proj_b")),
                        _row_panels(first("w_out"))] + ffn[1]
    at = np.cumsum([0, 512, 512, 512, 512, 512, 512, 512, 512, 128, 128, 3072])
    dq, dk, dv, rq, rk, rv, rg, gq, gk, gv, gates = (np.arange(at[i], at[i + 1]) for i in range(11))
    order = np.concatenate([dv, rv, gv, gv, dq, dk, gq, gk[:64], gk[:64], gk[64:], gk[64:], rq, rk, rg, gates])
    for l in range(LAYERS):
        panels += [_column_panels(x["w_in_2"][l], order)] + [_row_panels(x["w_branch_2"][l][b]) for b in (2, 0, 1)]
        panels += [_row_panels(x["w_out_2"][l]), _column_panels(x["w_mlp_in_2"][l], None), _row_panels(x["w_mlp_out_2"][l])]

    c = np.stack([_cols(x["c"]), _cols(x["c_ctx"])], 2).reshape(P, -1)
    logits = x["hgrn_lb_logits"]
    vec1 = np.concatenate([
        c, _cols(first("mod_b")), _cols(logits[0]), _cols(logits[1]), _cols(first("hgrn_norm_w")), _cols(first("hyena_conv_w")),
        _cols(first("hyena_conv_b")), _cols(first("hyena_bias")), _cols(x["final_norm_w"]), _pad(first("hyena_b1")),
        _pad(first("hyena_freq1")), _pad(first("hyena_b2")), _pad(first("hyena_freq2"))], 1)
    vec2 = []
    for l in range(LAYERS):
        twice = [_cols(np.concatenate([x[n][l], x[n][l]])) for n in ("diff_q_norm_2", "diff_k_norm_2", "gqa_q_norm_2",
                                                                     "gqa_k_norm_2")]
        decay = np.concatenate([x["ret_decay_fwd_2"][l], x["ret_decay_bwd_2"][l]])
        start = 0.8 - 0.6 * math.exp(-0.3 * l)
        vec2.append(np.concatenate(
            [_cols(x["attn_norm_2"][l]), _cols(x["mlp_norm_2"][l])] + twice
            + [_cols(x["diff_subln_2"][l]), _cols(x["ret_group_norm_2"][l]), np.broadcast_to(decay, (P, 8))]
            + [_pad(x[f"diff_lam_{n}_2"][l]) for n in ("q1", "q2", "k1", "k2")]
            + [np.full((P, 1), start, np.float32), np.full((P, 1), 1.0 - start, np.float32)], 1))
    hyw = np.zeros((64, 2176), np.float32)
    hyw[:33, 0:64] = first("hyena_w1")
    hyw[:, 64:128] = first("hyena_w2")
    hyw[:, 128:] = first("hyena_w3")

    def tokens(a):
        return a[0].T.reshape(KD, P, T).transpose(1, 0, 2).reshape(P, KD * T)

    arrays = {
        "stream": np.concatenate(panels, 0), "xT": tokens(x["x"]), "ctxT": tokens(x["ctx"]), "vec1": vec1,
        "vec2": np.stack(vec2), "lbrow": np.broadcast_to(logits.reshape(1, 2048), (P, 2048)), "hyw": hyw,
        **shape_constants(),
    }
    arrays = {f"in_{k}": np.ascontiguousarray(v) for k, v in arrays.items()}
    nc = _bacc.Bacc("TRN2", target_bir_lowering=False, num_devices=1)
    args = {k[3:]: nc.dram_tensor(k, v.shape, _mybir.dt.from_np(v.dtype), kind="ExternalInput").ap()
            for k, v in arrays.items()}
    args["out"] = nc.dram_tensor("out_0", (P, KD * T), _mybir.dt.float32, kind="ExternalOutput").ap()
    build(nc, **args)
    r = _run(nc, [arrays], core_ids=[0])
    got = r.results[0]["out_0"]
    return got.reshape(P, KD, T).transpose(2, 1, 0).reshape(1, T, D)
```

```python
import math
from contextlib import ExitStack

import numpy as np
import concourse.bass as bass
from concourse import mybir

F32 = mybir.dt.float32
F32R = mybir.dt.float32r
U8 = mybir.dt.uint8
ALU = mybir.AluOpType
ACT = mybir.ActivationFunctionType
AX = mybir.AxisListType.X
ds = bass.ds

P = 128
T = 256
TT = T // P
D = 1024
KD = D // P
DFF, MLP = 2816, 4096
KFF, KMLP = DFF // P, MLP // P
HEADS = 4
LAYERS = 2
PANEL = 2048
COLS = PANEL // KD
ROWK = PANEL // D
SLOTS = 4
UNROLL = 4
LEVELS = (64, 32, 16, 8, 4, 2, 1)
EPS = 1e-6
EPS2 = 1e-5
L1_EPS = 1e-6
TWO_PI_HI, TWO_PI_MID = 6.28125, 0.0019350051879882812
TWO_PI_LO = 2 * math.pi - TWO_PI_HI - TWO_PI_MID
ROUND = 1.5 * 2.0 ** 23
PI_SAFE = 3.1415925

N_MOD, N_WIN = 9 * D // COLS, 6144 // COLS
N_UP, N_DOWN, N_BR, N_OUT = DFF // P, DFF // (P * ROWK), 512 // (P * ROWK), D // (P * ROWK)
G_MOD = 0
G_UP1 = G_MOD + N_MOD
G_DOWN1 = G_UP1 + N_UP
G_WIN = G_DOWN1 + N_DOWN
G_PA = G_WIN + N_WIN
G_PB = G_PA + N_BR
G_OUT1 = G_PB + N_BR
G_UP2 = G_OUT1 + N_OUT
G_DOWN2 = G_UP2 + N_UP
G_LAYER = G_DOWN2 + N_DOWN
N_PROJ, N_MIN, N_MOUT = 30, MLP // COLS, MLP // (P * ROWK)
O_BR = N_PROJ
O_OUT = O_BR + 3 * N_BR
O_MIN = O_OUT + N_OUT
O_MOUT = O_MIN + N_MIN
PER_LAYER = O_MOUT + N_MOUT
PANELS = G_LAYER + LAYERS * PER_LAYER
DVE_LINKS, ACT_LINKS = 65, 8
R_DOWN1 = 0
R_PA = R_DOWN1 + N_DOWN
R_PB = R_PA + N_BR
R_OUT1 = R_PB + N_BR
R_DOWN2 = R_OUT1 + N_OUT
R_LAYER = R_DOWN2 + N_DOWN
RO_BR = 0
RO_OUT = RO_BR + 3 * N_BR
RO_MOUT = RO_OUT + N_OUT
R_PER_LAYER = RO_MOUT + N_MOUT
assert PER_LAYER % UNROLL == 0 and R_PER_LAYER % 2 == 0

def columns(*sizes):
    out, at = {}, 0
    for name, n in sizes:
        out[name] = (at, n)
        at += n
    return out, at

VEC1, NV1 = columns(("c", 2 * KD), ("mod_b", 72), ("logit0", 8), ("logit1", 8), ("a_norm", 1), ("conv_w", 36),
                    ("conv_b", 12), ("hy_bias", 8), ("final", 8), ("b1", 1), ("fr1", 1), ("b2", 1), ("fr2", 1))
VEC2, NV2 = columns(("attn_norm", 8), ("mlp_norm", 8), ("dq_norm", 1), ("dk_norm", 1), ("gq_norm", 1), ("gk_norm", 1),
                    ("subln", 1), ("ret_gain", 4), ("decay", 8), ("lam_q", 2), ("lam_k", 2), ("lam_init", 1),
                    ("one_less", 1))
MATS, NMATS = columns(("ident", P), ("block64", P), ("after", P), ("before", P), ("rot_part", P), ("rot_axial", P),
                      ("rot_ret", P), ("fold", 2))
TABS, NTABS = columns(("cos_part", T), ("sin_part", T), ("cos_axial", T), ("sin_axial", T), ("cos_ret", T),
                      ("sin_ret", T), ("ahead", TT * T), ("behind", TT * T))
HYC, NHYC = columns(("dft", TT * 512), ("dft_back", TT * 512), ("idft", 4 * T))


def shape_constants():
    f4 = np.float32
    p = np.arange(P)
    mats = {n: np.zeros((P, k), f4) for n, (_, k) in MATS.items()}
    mats["ident"][:] = np.eye(P)
    mats["fold"][0:4] = np.tile(np.eye(2), (2, 1))
    mats["block64"][:] = (p[:, None] // 64 == p[None] // 64)
    mats["after"][:] = p[:, None] > p[None]
    mats["before"][:] = p[:, None] < p[None]

    def rotation(m, base, half):
        for i in range(half):
            m[base + half + i, base + i] = -1
            m[base + i, base + half + i] = 1

    for b in (0, 64):
        rotation(mats["rot_part"], b, 8)
        rotation(mats["rot_axial"], b, 16)
        rotation(mats["rot_axial"], b + 32, 16)
    rotation(mats["rot_ret"], 0, 64)

    pos = np.arange(T, dtype=f4)
    def angles(pos, dim, theta):
        inv = f4(theta) ** (-np.arange(0, dim, 2, dtype=f4) / f4(dim))
        return (pos[:, None] * inv[None, :]).astype(f4)

    tabs = {n: np.zeros((P, k), f4) for n, (_, k) in TABS.items()}
    a = angles(pos, 16, 500000.0)
    tabs["cos_part"][:] = 1
    for b in (0, 64):
        for h in (0, 8):
            tabs["cos_part"][b + h:b + h + 8] = np.cos(a).T
            tabs["sin_part"][b + h:b + h + 8] = np.sin(a).T
    for off, q in ((0, np.repeat(np.arange(T // 64), 64)), (32, np.tile(np.arange(64), T // 64))):
        a = angles(q.astype(f4), 32, 10000.0)
        for b in (0, 64):
            for h in (0, 16):
                tabs["cos_axial"][b + off + h:b + off + h + 16] = np.cos(a).T
                tabs["sin_axial"][b + off + h:b + off + h + 16] = np.sin(a).T
    a = angles(pos, 128, 10000.0)
    for h in (0, 64):
        tabs["cos_ret"][h:h + 64] = np.cos(a).T
        tabs["sin_ret"][h:h + 64] = np.sin(a).T
    j = (np.arange(TT)[None, :, None] * P + p[:, None, None])
    i = np.arange(T)[None, None, :]
    tabs["ahead"][:] = np.maximum(i - j, 0).reshape(P, -1)
    tabs["behind"][:] = np.maximum(j - i, 0).reshape(P, -1)

    masks = np.zeros((P, 2 * len(LEVELS) + 1, P), f4)
    for n, h in enumerate(LEVELS):
        same = (p[:, None] // (2 * h)) == (p[None] // (2 * h))
        first = (p // h) % 2 == 0
        masks[:, n] = same & first[:, None] & ~first[None]
        masks[:, len(LEVELS) + n] = same & ~first[:, None] & first[None]
    masks[:, -1] = np.eye(P)

    quarter = D // 4
    omega = (1.0 / (f4(10000.0) ** (np.arange(quarter, dtype=f4) / f4(quarter)))).astype(f4)
    rows = T // 64
    ar = np.arange(rows, dtype=f4)[:, None] * omega
    ac = np.arange(64, dtype=f4)[:, None] * omega
    er = np.concatenate([np.sin(ar), np.cos(ar)], -1)
    ec = np.concatenate([np.sin(ac), np.cos(ac)], -1)
    emb = np.concatenate([np.broadcast_to(er[:, None], (rows, 64, D // 2)),
                          np.broadcast_to(ec[None], (rows, 64, D // 2))], -1).reshape(T, D).astype(f4)
    posemb = emb.T.reshape(KD, P, T).transpose(1, 0, 2)

    n = 2 * T
    f = np.arange(T)
    def dft(t):
        w = 2 * np.pi * ((t[:, None] * f[None]) % n) / n
        im = -np.sin(w)
        im[:, 0] = np.cos(np.pi * t)
        return np.concatenate([np.cos(w), im], 1)
    t = np.arange(T)
    hyc = {}
    hyc["dft"] = dft(t).reshape(TT, P, n).transpose(1, 0, 2)
    hyc["dft_back"] = dft(n - 1 - t).reshape(TT, P, n).transpose(1, 0, 2)
    inv = dft(t).T * (2.0 / n)
    inv[0] /= 2
    inv[T] /= 2
    hyc["idft"] = inv.reshape(4, P, T).transpose(1, 0, 2)
    tt = (np.arange(T, dtype=f4) / f4(T - 1)).astype(f4)
    lo, hi = math.log(1e-2) / 1.5, math.log(1e-2) / 0.3
    deltas = np.abs(np.linspace(lo, hi, 512, dtype=f4))
    window = (np.exp(-tt[:, None] * deltas[None]) + f4(0.05)).astype(f4)
    window = window.reshape(TT, P, 512).transpose(1, 0, 2)
    w = (2.0 * math.pi * np.arange(T, dtype=f4) / T).astype(f4)
    bands = np.linspace(1e-4, 15, 16, dtype=f4)
    ang = (w[:, None] * bands[None]).astype(f4)
    z = np.concatenate([tt[:, None], np.cos(ang), -np.sin(ang)], -1).astype(f4)
    zT = np.zeros((P, T), f4)
    zT[:33] = z.T

    def flat(x):
        return np.ascontiguousarray(np.asarray(x, f4).reshape(P, -1))
    return {
        "mats": np.concatenate([mats[k] for k in MATS], 1),
        "tabs": np.concatenate([tabs[k] for k in TABS], 1),
        "masks": np.ascontiguousarray(masks.reshape(P, -1)),
        "posemb": flat(posemb),
        "hyc": np.concatenate([flat(hyc[k]) for k in HYC], 1),
        "window": flat(window),
        "zT": zT,
    }


def build(nc, stream, xT, ctxT, vec1, vec2, lbrow, hyw, mats, tabs, masks, posemb, hyc, window, zT, spectra, out):
    with ExitStack() as ctx:
        def sb(name, shape, dt=F32):
            return ctx.enter_context(nc.sbuf_tensor(name, shape, dt))

        def sem(name):
            return ctx.enter_context(nc.semaphore(name))

        landing = sb("landing", [P, SLOTS, PANEL])
        whi, wlo = (sb(n, [P, 2, PANEL], F32R) for n in ("whi", "wlo"))
        xhi, xlo = (sb(n, [P, KD, 2 * T], F32R) for n in ("xhi", "xlo"))
        ahi, alo = (x[:, 0:2 * ROWK].rearrange("p (r k) t -> p r k t", k=ROWK) for x in (xhi, xlo))
        h = sb("h", [P, KD, T])
        big = sb("big", [P, 50, T])
        bigf = big[:].rearrange("p c t -> p (c t)")
        v1 = sb("v1", [P, NV1])
        v2 = sb("v2", [P, NV2])
        v2all = sb("v2all", [P, LAYERS, NV2])
        cst = sb("cst", [P, 4 * (KD - 1) + P], F32R)
        mat = sb("mat", [P, NMATS])
        msk = sb("msk", [P, 2 * len(LEVELS) + 1, P], U8)
        ones = sb("ones", [P, P])
        mcol = sb("mcol", [P, 72, 2])
        scol = sb("scol", [P, 64])
        gains = sb("gains", [P, 8, KD])
        eps = sb("eps", [P, 2])
        rstd = sb("rstd", [P, 2, T])
        ws = sb("ws", [P, 10880])
        ps = ctx.enter_context(nc.psum_tensor("ps", [P, 8, 512], F32))

        def W(at, *shape):
            n = int(np.prod(shape))
            v = ws[:, at:at + n]
            if len(shape) == 2:
                v = v.rearrange("p (a b) -> p a b", b=shape[1])
            if len(shape) == 3:
                v = v.rearrange("p (a b c) -> p a b c", b=shape[1], c=shape[2])
            if len(shape) == 4:
                v = v.rearrange("p (a b c d) -> p a b c d", b=shape[1], c=shape[2], d=shape[3])
            return v

        def chunks(a, n):
            return big[:, a:a + n, :]

        def flatc(a, n):
            return bigf[:, a * T:(a + n) * T]

        def m1(name, i=0, n=1):
            a = VEC1[name][0] + i
            return v1[:, a:a + n]

        def m2(name, i=0, n=1):
            a = VEC2[name][0] + i
            return v2[:, a:a + n]

        def mt(name):
            a = MATS[name][0]
            return mat[:, a:a + P]

        ident = mt("ident")

        hc = W(0, KD, T)
        pos = W(2048, KD, T)
        mrow = W(4096, UNROLL, COLS)
        mask_in = W(6144, (2 * len(LEVELS) + 1) * P)
        Vx = W(0, TT, 512)
        Vc = W(1024, TT, 512)
        sc = [W(2048, TT, 512), W(3072, TT, 512)]
        lrow = W(4096, 2, 1024)
        lgc = W(6144, TT, 512)
        XC = [W(1024, HEADS * TT, P + 1), W(2056, HEADS * TT, P + 1)]
        S = W(3088, TT, HEADS, T)
        EM = [W(7168, HEADS * TT, P), W(8192, HEADS * TT, P)]
        EMf = [W(7168, HEADS * TT * P), W(8192, HEADS * TT * P)]
        Q0, KF, G0, HY, MG = 0, (4, 8), 12, 16, 28
        s0 = [bigf[:, 44 * T + d * 512:44 * T + (d + 1) * 512].rearrange("p (a b) -> p a b", b=P) for d in range(2)]
        FILT = 5120
        fdft = W(FILT, 2, TT, 512)
        hwindow = W(FILT + 2048, TT, 512)
        zfeat = W(FILT + 3072, T)
        h2 = W(FILT + 3072 + T, T)
        hyin = W(FILT + 3072 + 2 * T, 2176)
        hw1, hw2, hw3 = hyin[0:33, 0:64], hyin[0:64, 64:128], hyin[0:64, 128:2176]
        kern = bigf[:, 6144:8192].rearrange("p (u d c) -> p u d c", u=TT, d=2)
        absk = bigf[:, 8192:10240]
        Kst = bigf[:, 10240:12288].rearrange("p (m c) -> p m c", c=512)
        l1 = bigf[:, 12288:12800]
        ang = bigf[:, 12288:12800].rearrange("p (a b) -> p a b", b=T)
        F_MLP, F_ORDER, F_STEPS = 8, 12, 12
        idft = W(0, 4, T)
        Kf = W(1024, 2, 4, 512)
        dft = W(9216, TT, 512)
        ZC = (4, 8, 16)
        uT = W(5120, TT, 512)
        ptmp = uT
        Pi = bigf[:, 24 * T:28 * T].rearrange("p (a b) -> p a b", b=512)
        Pf = bigf[:, 44 * T:48 * T].rearrange("p (a b) -> p a b", b=512)
        DQ, DK, GQ, GK, RQ, RK, RG, GT = 0, 4, 8, 12, 14, 18, 22, 26
        tab = W(0, NTABS)
        def tb(name):
            a, n = TABS[name]
            return ws[:, a:a + n]
        VD = W(NTABS, TT, 512)
        VR = W(NTABS + 1024, TT, 512)
        VG = W(NTABS + 2048, TT, P)
        tmpA = NTABS + 2304
        nsq = W(tmpA, 4, T)
        nrs = W(tmpA + 1024, 4, T)
        nrot = W(tmpA + 2048, 4, T)
        ew = [W(tmpA, 2, T), W(tmpA + 512, 2, T)]
        wT = [W(tmpA + 3072, 2, TT, T), W(tmpA + 4096, 2, TT, T)]
        rtmp = [W(tmpA, 2 * T), W(tmpA + 512, 2 * T)]
        ROPES = ((DQ, 4, "dq_norm", "rot_part", "cos_part", "sin_part"), (DK, 4, "dk_norm", "rot_part", "cos_part", "sin_part"),
                 (GQ, 4, "gq_norm", "rot_axial", "cos_axial", "sin_axial"),
                 (GK, 2, "gk_norm", "rot_axial", "cos_axial", "sin_axial"),
                 (RQ, 4, None, "rot_ret", "cos_ret", "sin_ret"), (RK, 4, None, "rot_ret", "cos_ret", "sin_ret"))

        def hid_chunk(i, t):
            w = t // T
            return big[:, ds(i * w, w), :].rearrange("p c t -> p (c t)")

        def hid_src(t):
            if t == T:
                return lambda i: big[:, ds(i * ROWK, ROWK), :]
            return lambda i: big[:, ds(i * (2 * ROWK), 2 * ROWK), :].rearrange("p (k b) t -> p k (b t)", b=2)

        def chunk_src(c0):
            return lambda i: big[:, ds(i * ROWK + c0, ROWK), :]

        def halves(x, hh):
            b = x.rearrange("p (n u s) -> p n u s", u=2, s=hh)
            return b[:, :, 0], b[:, :, 1]

        NL = len(LEVELS) + 1
        levels = [(d, n) for d in range(2) for n in range(NL)] + [(2, 0)]
        smx = sb("smx", [P, 4, 8])
        Dm = [W(tmpA + 1024, TT, T), W(tmpA + 1536, TT, T)]
        sD = [W(tmpA + 2048, TT, T), W(tmpA + 2560, TT, T)]
        PLAIN = (DQ, DQ + 2, DK, DK + 2, GQ, GQ + 2, GK, RQ, RQ + 2, RK, RK + 2, RG, RG + 2) + tuple(range(GT, GT + 24, 2))
        N_VALUES, N_HEADS = 5, 18
        N_FIRST = 8
        SUM_AFTER = {7: 0, 9: 1, 11: 2, 12: 3}
        ROT_AFTER = {8: (0, 0), 10: (1, 0), 12: (2, 0), 13: (3, 0), 14: (4, 14), 16: (5, 16)}
        SQUARE_AFTER = {6: 0, 8: 1, 10: 2, 11: 3}
        RMS_AFTER = SUM_AFTER
        SCALE_IN = {8: 0, 10: 1, 12: 2, 13: 3}
        ROPE_IN = {9: 0, 11: 1, 13: 2, 14: 3, 15: 4, 17: 5}
        PAIRS = 16
        BRANCHES = ((GQ, 16), (DQ, 0), (RQ, 8))

        per = {}
        def lsem(name, n=0):
            s = sem(name)
            per[name] = n
            return s

        landed = [sem(f"landed{i}") for i in range(SLOTS)]
        hi_done = sem("hi_done")
        lo_done = sem("lo_done")
        panel_used = sem("panel_used")
        act_hi = sem("act_hi")
        act_lo = sem("act_lo")
        small_in = sem("small_in")
        mask_landed, mask_set = sem("mask_landed"), sem("mask_set")
        x_in = sem("x_in")
        lb_in = sem("lb_in")
        hy2_in = sem("hy2_in")
        kf_out = sem("kf_out")
        hy_in = sem("hy_in")
        tab_in = sem("tab_in")
        v2_in = lsem("v2_in", 1)
        out_done = sem("out_done")
        const_set = sem("const_set")
        dve_chain, act_chain = sem("dve_chain"), sem("act_chain")
        dve_link = lsem("dve_link", DVE_LINKS)
        act_link = lsem("act_link", ACT_LINKS)
        c_silu, c_split, c_zero = sem("c_silu"), sem("c_split"), sem("c_zero")
        mod_copied, mod_turned, mod_added = sem("mod_copied"), sem("mod_turned"), sem("mod_added")
        cols_set = sem("cols_set")
        h_set = sem("h_set")
        sums_out = lsem("sums_out", 9)
        sq_done, sum_done, rstd_done = lsem("sq_done", 8), lsem("sum_done", 2), lsem("rstd_done", 2)
        norm_scaled, norm_hi, norm_lo = lsem("norm_scaled", 16), lsem("norm_hi", 16), lsem("norm_lo", 16)
        silu_done, hid_done = sem("silu_done"), sem("hid_done")
        res_done = lsem("res_done", 4)
        win_out = sem("win_out")
        lb_diff, lb_sig, lb_set = sem("lb_diff"), sem("lb_sig"), sem("lb_set")
        cf_done, cln_done, ck_done, csum_done, cdec_done, ckey_done, cst_done, cst_out = (
            sem(n) for n in ("cf_done", "cln_done", "ck_done", "csum_done", "cdec_done", "ckey_done", "cst_done",
                             "cst_out"))
        xf_done, xln_done = sem("xf_done"), sem("xln_done")
        lv_diff, lv_exp, lv_mul, lv_score, lv_sel = (sem("lv_" + n) for n in ("diff", "exp", "mul", "score", "sel"))
        qe_diff, qe_exp, qe_done, o_done, osq_done, osum_done, orstd_done, oa_done = (
            sem(n) for n in ("qe_diff", "qe_exp", "qe_done", "o_done", "osq_done", "osum_done", "orstd_done", "oa_done"))
        conv_done, fl_mm, fl_arg, fl_sin, h3_mm, win_mul, abs_done, l1_mm, kf_mm, kf_done = (
            sem(n) for n in ("conv_done", "fl_mm", "fl_arg", "fl_sin", "h3_mm", "win_mul", "abs_done", "l1_mm", "kf_mm",
                             "kf_done"))
        turn_done, uT_done, uf_mm, pf_done, y_mm, z_done = (
            sem(n) for n in ("turn_done", "uT_done", "uf_mm", "pf_done", "y_mm", "z_done"))
        gate_done = lsem("gate_done", 6)
        gate1_done = sem("gate1_done")
        gate1_on = sem("gate1_on")
        gate_on = lsem("gate_on", 4)
        proj_out = lsem("proj_out", N_PROJ)
        lam_mul, lam_mm, lam_exp, lam_set = (lsem("lam_" + n, 1) for n in ("mul", "mm", "exp", "set"))
        rp_sq, rp_sum, rp_rs = (lsem("rp_" + n, 4) for n in ("sq", "sum", "rs"))
        rp_n, rp_rot, rp_done = lsem("rp_n", 4), lsem("rp_rot", 6), lsem("rp_done", 6)
        sc_mm, sc_max, sc_exp, sc_w, sc_turn, sc_wT = (lsem("sc_" + n, 16) for n in ("mm", "max", "exp", "w", "turn", "wT"))
        pv_mm, pv_out = lsem("pv_mm", 8), lsem("pv_out", 8)
        rt_arg, rt_dec, rt_mm, rt_mul, rt_pv, rt_out = (lsem("rt_" + n, 4) for n in ("arg", "dec", "mm", "mul", "pv", "out"))
        sub_sq, sub_sum, sub_rs, sub_done = (lsem("sub_" + n, 1) for n in ("sq", "sum", "rs", "done"))
        gn_mean, gn_cen, gn_sq, gn_sum, gn_rs, gn_done = (
            lsem("gn_" + n, 1) for n in ("mean", "cen", "sq", "sum", "rs", "done"))
        relu_done, m_done = lsem("relu_done", N_MIN), lsem("m_done", N_MIN)
        layer_done = lsem("layer_done", 4)

        def at(s, l, c, base=0):
            return l * per[s.name] + (base + c)

        def panel_loop(eng, first, count, body):
            phase = first[1] if isinstance(first, tuple) else first
            g0 = first[0] if isinstance(first, tuple) else first
            if count >= 2 * UNROLL:
                with eng.Fori(0, count // UNROLL) as i:
                    for j in range(UNROLL):
                        body(i * UNROLL + j, g0 + (i * UNROLL + j), (phase + j) % UNROLL)
            else:
                for j in range(count - count % UNROLL):
                    body(j, g0 + j, (phase + j) % UNROLL)
            for j in range(count - count % UNROLL, count):
                body(j, g0 + j, (phase + j) % UNROLL)

        def layer_panel(l, off):
            return (l * PER_LAYER + (G_LAYER + off), G_LAYER + off)

        block = ctx.enter_context(nc.Block())

        @block.sync
        def _(sp):
            for g in range(SLOTS):
                sp.dma_start(landing[:, g], stream[g]).then_inc(landed[g], 16)

            def load(g, s):
                sp.wait_ge(lo_done, g - (SLOTS - 1))
                sp.dma_start(landing[:, s], stream[ds(g, 1)].rearrange("a p n -> p (a n)")).then_inc(landed[s], 16)

            with sp.Fori(1, PANELS // UNROLL) as i:
                for j in range(UNROLL):
                    load(i * UNROLL + j, j)
            for g in range(PANELS - PANELS % UNROLL, PANELS):
                load(g, g % SLOTS)
            sp.wait_ge(layer_done, 4 * (1 + LAYERS))
            sp.dma_start(out, h[:].rearrange("p k t -> p (k t)")).then_inc(out_done, 16)
            sp.wait_ge(out_done, 16)

        @block.gpsimd
        def _(pool):
            pool.wait_ge(const_set, 3)

            def high(g, s, turn):
                pool.wait_ge(landed[s], (turn + 1) * 16)
                if not isinstance(g, int) or g >= 2:
                    pool.wait_ge(panel_used, g - 1)
                hi, panel = whi[:, s % 2], landing[:, s]
                pool.tensor_tensor(hi[:, 0:P], panel[:, 0:P], ones[:], ALU.mult)
                pool.tensor_scalar(hi[:, P:], panel[:, P:], 1.0, 0.0, ALU.mult, ALU.add).then_inc(hi_done, 1)

            for g in range(UNROLL):
                high(g, g, 0)
            with pool.Fori(1, PANELS // UNROLL) as i:
                for j in range(UNROLL):
                    high(i * UNROLL + j, j, i)
            for g in range(PANELS - PANELS % UNROLL, PANELS):
                high(g, g % SLOTS, g // SLOTS)

        @block.vector
        def _(dve):
            v = nc.vector
            count = [0]
            link = [0, 0]

            def step(ins):
                count[0] += 1
                ins.then_inc(dve_chain, 1)
                dve.wait_ge(dve_chain, count[0])

            def lstep(ins):
                link[1] += 1
                ins.then_inc(dve_link, 1)
                dve.wait_ge(dve_link, at(dve_link, link[0], link[1]))

            def low(g, s):
                dve.wait_ge(hi_done, g + 1)
                if not isinstance(g, int) or g >= 2:
                    dve.wait_ge(panel_used, g - 1)
                v.tensor_tensor(wlo[:, s % 2], landing[:, s], whi[:, s % 2].bitcast(F32), ALU.subtract
                                ).then_inc(lo_done, 1)

            def low_stage(first, n, last=True):
                panel_loop(dve, first, n if last else n - 1, lambda i, g, s: low(g + 1, (s + 1) % SLOTS))

            def part_low(src, r, r_phase, t):
                dve.wait_ge(act_hi, r + 1)
                v.tensor_tensor(alo[:, r_phase % 2, :, 0:t], src, ahi[:, r_phase % 2, :, 0:t].bitcast(F32),
                                ALU.subtract).then_inc(act_lo, 1)

            def row_stage(first, n, src, r0, r_phase, t, last=True, begun=False):
                if not begun:
                    part_low(src(0), r0, r_phase, t)

                g0, phase = first if isinstance(first, tuple) else (first, first)

                def body(i, g, s):
                    low(g + 1, (s + 1) % SLOTS)
                    part_low(src(i + 1), r0 + (i + 1), r_phase + (s - phase) % UNROLL + 1, t)
                panel_loop(dve, first, n - 1, body)
                if last:
                    low(g0 + n, (phase + n) % SLOTS)
                return g0 + n

            def norm_step(k, n, src, gain, shift, dst0, l=None):
                val = (lambda c: at(norm_hi, l, c, base=5 * KD)) if l is not None else (lambda c: c)
                tmp = bigf[:, 4096:4096 + KD * T].rearrange("p (k t) -> p k t", t=T)
                if k == 0:
                    dve.wait_ge(rstd_done, n + 1 if l is None else at(rstd_done, l, n + 1, base=6))
                if k < KD:
                    v.scalar_tensor_tensor(tmp[:, k], src[:, k], gain(k), rstd[:, n % 2], ALU.mult, ALU.mult
                                           ).then_inc(norm_scaled, 1)
                if k >= 1:
                    j = k - 1
                    dve.wait_ge(norm_hi, val(n * KD + k))
                    hi = xhi[:, j, dst0:dst0 + T].bitcast(F32)
                    lo = xlo[:, j, dst0:dst0 + T]
                    if shift is None:
                        v.tensor_tensor(lo, tmp[:, j], hi, ALU.subtract).then_inc(norm_lo, 1)
                    else:
                        v.scalar_tensor_tensor(lo, tmp[:, j], shift(j), hi, ALU.add, ALU.subtract).then_inc(norm_lo, 1)

            def norm(*args):
                for k in range(KD + 1):
                    norm_step(k, *args)

            def residual(out0, end, add):
                for b in range(4):
                    if b < 3:
                        dve.wait_ge(sums_out, out0 + (b + 1))
                    else:
                        dve.wait_ge(panel_used, end)
                    add(b)

            v.memset(ones[:], 1.0).then_inc(const_set, 1)
            v.memset(eps[:, 0:1], EPS).then_inc(const_set, 1)
            v.memset(eps[:, 1:2], EPS2).then_inc(const_set, 1)
            v.memset(mcol[:], 0.0).then_inc(mod_added, 1)
            v.memset(cst[:].bitcast(F32), 0.0).then_inc(c_zero, 1)
            dve.wait_ge(c_silu, 2)
            cs = scol[:, 0:2 * KD].rearrange("p (k b) -> p k b", b=2)
            cparts = cst[:, 0:4 * KD].rearrange("p (k b) -> p k b", b=4)
            v.tensor_tensor(cparts[:, :, 2:4], cs, cparts[:, :, 0:2].bitcast(F32), ALU.subtract).then_inc(c_split, 1)

            def gcol(n):
                return lambda k: gains[:, n, k:k + 1]

            def mcolumn(n, who):
                return lambda k: mcol[:, 8 * n + k, who:who + 1]

            def mod(n, who):
                return mcol[:, 8 * n:8 * n + 8, who]

            def sine_argument(n):
                b, f = (("b1", "fr1"), ("b2", "fr2"))[n]
                x, k = ang[0:64, 0], ang[0:64, 1]
                dve.wait_ge(fl_mm, n + 1)
                step(v.tensor_scalar(x, ps[0:64, 5, 0:T], m1(b)[0:64], m1(f)[0:64], ALU.add, ALU.mult))
                step(v.tensor_scalar(k, x, 1 / (2 * math.pi), ROUND, ALU.mult, ALU.add))
                step(v.tensor_scalar(k, k, ROUND, None, ALU.subtract))
                for part in (TWO_PI_HI, TWO_PI_MID, TWO_PI_LO):
                    step(v.scalar_tensor_tensor(x, k, -part, x, ALU.mult, ALU.add))
                v.tensor_scalar(x, x, PI_SAFE, -PI_SAFE, ALU.min, ALU.max).then_inc(fl_arg, 1)

            def windowed(o, u):
                dve.wait_ge(h3_mm, 2 * o + u + 1)
                for d in range(2):
                    last = v.tensor_tensor(kern[:, u, d], ps[:, 6 + d], hwindow[:, u], ALU.mult)
                last.then_inc(win_mul, 1)

            def inverse_norm(o):
                dve.wait_ge(l1_mm, o + 1)
                step(v.tensor_scalar(l1, ps[:, 5], L1_EPS, None, ALU.add))
                step(v.reciprocal(l1, l1))

            def normed_spectrum(o, m):
                dve.wait_ge(kf_mm, 4 * o + m + 1)
                if o and m == 0:
                    dve.wait_ge(kf_out, 16)
                v.tensor_tensor(Kst[:, m], ps[:, 6 + m % 2], l1, ALU.mult).then_inc(kf_done, 1)

            def filter_step(q):
                if q in (F_MLP + 1, F_MLP + 3):
                    sine_argument((q - F_MLP) // 2)
                for o in range(2):
                    t = q - F_ORDER - o * F_STEPS
                    if t in (1, 2):
                        windowed(o, t - 1)
                    if t == 4:
                        inverse_norm(o)
                    if t in (6, 8, 10, 12):
                        normed_spectrum(o, t // 2 - 3)

            def mod_group(i, beside=lambda j: None):
                for j in range(UNROLL):
                    low(i * UNROLL + j + 1, (j + 1) % SLOTS)
                    beside(j)
                    if isinstance(i, int):
                        filter_step(i * UNROLL + j)
                dve.wait_ge(mod_turned, i * UNROLL + UNROLL)
                v.tensor_tensor(mcol[:, ds(i * 8, 8), :], ps[:, 4, 0:16].rearrange("p (c b) -> p c b", b=2),
                                m1("mod_b", 0, 72)[:, ds(i * 8, 8)].unsqueeze(2).to_broadcast([P, 8, 2]), ALU.add
                                ).then_inc(mod_added, 1)
            low(0, 0)
            with dve.Fori(0, 2) as i:
                mod_group(i)
            dve.wait_ge(x_in, 48)
            for b in range(4):
                v.tensor_tensor(h[:, 2 * b:2 * b + 2], h[:, 2 * b:2 * b + 2], pos[:, 2 * b:2 * b + 2], ALU.add
                                ).then_inc(h_set, 1)
            dve.wait_ge(mod_added, 1 + 2)
            for n, (m, who) in enumerate(((1, 0), (1, 1))):
                v.tensor_scalar(gains[:, n], mod(m, who), 1.0, None, ALU.add).then_inc(cols_set, 1)
            mod_group(2)
            dve.wait_ge(cols_set, 2)
            for n, src, g0 in ((0, h, 3), (1, hc, 5)):
                for half in range(2):
                    def beside(j):
                        norm_step(4 * half + j, n, src, gcol(n), mcolumn(0, n), n * T)
                        if half and j == 3:
                            norm_step(KD, n, src, gcol(n), mcolumn(0, n), n * T)
                    mod_group(g0 + half, beside)
            for i in range(7, N_MOD // UNROLL):
                mod_group(i)
            filter_step(N_MOD)
            dve.wait_ge(mod_added, 1 + N_MOD // UNROLL)
            for n, (m, who) in ((2, (4, 0)), (3, (4, 1)), (4, (7, 0))):
                v.tensor_scalar(gains[:, n], mod(m, who), 1.0, None, ALU.add).then_inc(cols_set, 1)
            for n, (m, who) in enumerate(((2, 0), (2, 1), (8, 0))):
                v.tensor_scalar(gains[:, 5 + n], mod(m, who), 0.5, None, ALU.mult).then_inc(cols_set, 1)
            dve.wait_ge(cols_set, 8)

            def up_stage(g0, which, t, last=True):
                def body(i, g, s):
                    low(g + 1, (s + 1) % SLOTS)
                    dve.wait_ge(silu_done, which * KFF + i + 1)
                    hid = hid_chunk(i, t)
                    bank = 2 * ((s - g0) % UNROLL) + 1
                    v.tensor_tensor(hid, hid, ps[:, bank, 0:t], ALU.mult).then_inc(hid_done, 1)
                panel_loop(dve, g0, N_UP, body)

            up_stage(G_UP1, 0, 2 * T)
            dve.wait_ge(hid_done, KFF)
            row_stage(G_DOWN1, N_DOWN, hid_src(2 * T), R_DOWN1, R_DOWN1, 2 * T)
            def down1(b):
                for k in (2 * b, 2 * b + 1):
                    v.scalar_tensor_tensor(h[:, k], ps[:, k, 0:T], gains[:, 5, k:k + 1], h[:, k], ALU.mult, ALU.add)
                    last = v.scalar_tensor_tensor(hc[:, k], ps[:, k, T:2 * T], gains[:, 6, k:k + 1], hc[:, k], ALU.mult,
                                                  ALU.add)
                last.then_inc(h_set, 1)
            residual(0, G_DOWN1 + N_DOWN, down1)
            norm(2, h, gcol(2), mcolumn(3, 0), 0)
            norm(3, hc, gcol(3), mcolumn(3, 1), T)

            low_stage(G_WIN, N_FIRST)

            def win(i):
                low(G_WIN + i + 1, (G_WIN + i + 1) % SLOTS)

            dve.wait_ge(norm_lo, 4 * KD)
            dve.wait_ge(mask_landed, 16)
            v.tensor_copy(msk[:].rearrange("p n s -> p (n s)"), mask_in).then_inc(mask_set, 1)
            dve.wait_ge(mask_set, 1)
            dve.wait_ge(lb_in, 16)
            v.tensor_tensor(scol[:, 16:24], m1("logit0", 0, 8), m1("logit1", 0, 8), ALU.subtract).then_inc(lb_diff, 1)
            v.tensor_tensor(lrow[:, 0], lrow[:, 0], lrow[:, 1], ALU.subtract).then_inc(lb_diff, 1)
            dve.wait_ge(lb_sig, 2)
            v.tensor_scalar(scol[:, 24:32], scol[:, 16:24], -1.0, 1.0, ALU.mult, ALU.add).then_inc(lb_set, 1)
            v.tensor_scalar(lrow[:, 1], lrow[:, 0], -1.0, 1.0, ALU.mult, ALU.add).then_inc(lb_set, 1)
            dve.wait_ge(lb_set, 2)

            dve.wait_ge(win_out, 6)
            for d in range(2):
                def row(n):
                    return lrow[:, n, 512 * d:512 * d + 512].unsqueeze(1).to_broadcast([P, TT, 512])
                step(v.tensor_tensor(sc[d], sc[d], row(1), ALU.mult))
                v.tensor_tensor(sc[d], sc[d], row(0), ALU.add).then_inc(cf_done, 1)
                win(N_FIRST + 2 * d)
                dve.wait_ge(cln_done, d + 1)
                v.tensor_scalar(sc[d], sc[d], -1.0, 1.0, ALU.mult, ALU.add).then_inc(ck_done, 1)
                win(N_FIRST + 2 * d + 1)
                dve.wait_ge(ck_done, d + 1)
                dve.wait_ge(cdec_done, d + 1)
                v.tensor_tensor(sc[d], sc[d], lgc, ALU.mult).then_inc(ckey_done, 1)

            for d in range(2):
                for c in range(HEADS):
                    n = 4 * d + c
                    last = v.tensor_scalar(big[:, KF[d] + c], big[:, KF[d] + c], scol[:, 24 + n:25 + n],
                                           scol[:, 16 + n:17 + n], ALU.mult, ALU.add)
                last.then_inc(xf_done, 1)
            win(N_FIRST + 4)
            dve.wait_ge(cst_out, 2)
            for d in range(2):
                last = v.memset(XC[d][:, :, 0:1], 0.0)
            step(last)
            for d in range(2):
                dve.wait_ge(xln_done, d + 1)
                v.tensor_scalar(flatc(KF[d], 4), flatc(KF[d], 4), -1.0, 1.0, ALU.mult, ALU.add)
                for n in range(HEADS * TT):
                    last = v.tensor_tensor_scan(XC[d][:, n, 1:P + 1], ones[:], EM[d][:, n], 0.0, ALU.mult, ALU.add)
                step(last)
                win(N_FIRST + 5 + d)

            def q_of(c0):
                return flatc(c0, 4)
            def diff(m):
                d, n = levels[m]
                em = EM[m % 2]
                if m >= 2:
                    dve.wait_ge(lv_score, m - 1)
                if d == 2:
                    v.tensor_tensor(em, chunks(KF[0], 4).rearrange("p c (u s) -> p (c u) s", s=P),
                                    chunks(KF[1], 4).rearrange("p c (u s) -> p (c u) s", s=P), ALU.add
                                    ).then_inc(lv_diff, 1)
                    return
                o = 1 - d
                if n < len(LEVELS):
                    hh = LEVELS[n]
                    x = XC[d][:, :, o:o + P].rearrange("p n (b s) -> p n b s", s=2 * hh)
                    mid = XC[d][:, :, 0:P].rearrange("p n (b s) -> p n b s", s=2 * hh)[:, :, :, hh:hh + 1]
                    mid = mid.to_broadcast([P, HEADS * TT, P // (2 * hh), 2 * hh])
                    v.tensor_tensor(em.rearrange("p n (b s) -> p n b s", s=2 * hh), x, mid, ALU.subtract
                                    ).then_inc(lv_diff, 1)
                else:
                    x = XC[d][:].rearrange("p (g u) s -> p g u s", u=TT)
                    tot = x[:, :, 0, P:P + 1].to_broadcast([P, HEADS, P])
                    v.tensor_tensor(em.rearrange("p (g u) s -> p g u s", u=TT)[:, :, 0], tot, x[:, :, 0, o:o + P],
                                    ALU.subtract).then_inc(lv_diff, 1)

            def mul(m):
                d, n = levels[m]
                if d == 2:
                    return
                hh = (LEVELS + (P,))[n]
                dve.wait_ge(lv_exp, m + 1)
                e = halves(EMf[m % 2], hh)
                q, kk = halves(q_of(Q0), hh), halves(q_of(KF[d]), hh)
                a = (kk, q) if d == 0 else (q, kk)
                v.tensor_tensor(e[0], e[0], a[0][0], ALU.mult)
                v.tensor_tensor(e[1], e[1], a[1][1], ALU.mult).then_inc(lv_mul, 1)

            def select(m):
                d, n = levels[m]
                dve.wait_ge(lv_score, m + 1)
                if d == 2 or n < len(LEVELS):
                    mk = msk[:, 2 * len(LEVELS) if d == 2 else d * len(LEVELS) + n].unsqueeze(1)
                    for u in range(TT):
                        last = v.copy_predicated(S[:, u, :, u * P:(u + 1) * P], mk.to_broadcast([P, HEADS, P]),
                                                 ps[:, 2 * (m % 2) + u].rearrange("p (g s) -> p g s", s=P))
                else:
                    last = v.tensor_copy(S[:, d, :, (1 - d) * P:(2 - d) * P],
                                         ps[:, 2 * (m % 2)].rearrange("p (g s) -> p g s", s=P))
                last.then_inc(lv_sel, 1)

            step(v.memset(S.rearrange("p u g t -> p (u g t)"), 0.0))
            diff(0)
            for m in range(len(levels)):
                mul(m)
                if m >= 1:
                    select(m - 1)
                if m + 1 < len(levels):
                    diff(m + 1)
                if N_FIRST + 7 + m < N_WIN:
                    win(N_FIRST + 7 + m)
            select(len(levels) - 1)
            dve.wait_ge(lv_score, len(levels))
            xs = [XC[d][:].rearrange("p (g u) s -> p g u s", u=TT) for d in range(2)]
            es = [EM[d].rearrange("p (g u) s -> p g u s", u=TT) for d in range(2)]
            def total(d, u):
                return xs[d][:, :, u, P:P + 1].to_broadcast([P, HEADS, P])
            v.tensor_copy(es[0][:, :, 0], xs[0][:, :, 0, 1:P + 1])
            v.tensor_tensor(es[0][:, :, 1], total(0, 0), xs[0][:, :, 1, 1:P + 1], ALU.add)
            v.tensor_tensor(es[1][:, :, 1], total(1, 1), xs[1][:, :, 1, 0:P], ALU.subtract)
            step(v.tensor_tensor(es[1][:, :, 0], total(1, 0), xs[1][:, :, 0, 0:P], ALU.subtract))
            v.tensor_tensor(es[1][:, :, 0], total(1, 1), es[1][:, :, 0], ALU.add).then_inc(qe_diff, 1)
            dve.wait_ge(qe_exp, 1)
            for d in range(2):
                last = v.tensor_tensor(EMf[d], EMf[d], q_of(Q0), ALU.mult)
            last.then_inc(qe_done, 1)
            dve.wait_ge(orstd_done, 1)
            for b in range(2):
                step(v.scalar_tensor_tensor(flatc(Q0 + 2 * b, 2), ps[:, 4 + b], m1("a_norm"),
                                            EMf[1][:, b * 512:(b + 1) * 512], ALU.mult, ALU.mult))
            dve.wait_ge(gate1_on, 1)
            v.tensor_tensor(flatc(Q0, 4), flatc(Q0, 4), flatc(G0, 4), ALU.mult).then_inc(oa_done, 1)

            dve.wait_ge(win_out, N_WIN)
            for c in range(12):
                src = big[:, HY + c]
                dst = big[:, ZC[c // 4] + c % 4]
                step(v.tensor_scalar(dst, src, m1("conv_w", 12 + c), m1("conv_b", c), ALU.mult, ALU.add))
                step(v.scalar_tensor_tensor(dst[:, 1:T], src[:, 0:T - 1], m1("conv_w", c), dst[:, 1:T], ALU.mult, ALU.add))
                last = v.scalar_tensor_tensor(dst[:, 0:T - 1], src[:, 1:T], m1("conv_w", 24 + c), dst[:, 0:T - 1],
                                              ALU.mult, ALU.add)
                if c == 3:
                    last.then_inc(conv_done, 1)
            last.then_inc(conv_done, 1)
            dve.wait_ge(conv_done, 2)

            dve.wait_ge(hy2_in, 64)
            for o in range(2):
                dve.wait_ge(uf_mm, o + 1)
                ur, ui = ps[:, 0:2], ps[:, 2:4]
                kr, ki = Kf[:, o, 0:2], Kf[:, o, 2:4]
                v.tensor_tensor(Pf, ur, kr, ALU.mult)
                step(v.tensor_tensor(ptmp, ui, ki, ALU.mult))
                step(v.tensor_tensor(Pf, Pf, ptmp, ALU.subtract))
                v.tensor_tensor(Pf[0:1, 0], ur[0:1, 0], kr[0:1, 0], ALU.mult).then_inc(pf_done, 1)
                v.tensor_tensor(Pi, ur, ki, ALU.mult)
                step(v.tensor_tensor(ptmp, ui, kr, ALU.mult))
                step(v.tensor_tensor(Pi, Pi, ptmp, ALU.add))
                v.tensor_tensor(Pi[0:1, 0], ui[0:1, 0], ki[0:1, 0], ALU.mult).then_inc(pf_done, 1)
                dve.wait_ge(y_mm, o + 1)
                for c in range(4):
                    z, g = big[:, ZC[0] + c], big[:, ZC[1 + o] + c]
                    step(v.scalar_tensor_tensor(z, z, m1("hy_bias", 4 * o + c), ps[:, 6 + c // 2, (c % 2) * T:(c % 2 + 1) * T],
                                                ALU.mult, ALU.add))
                    last = v.tensor_tensor(z, z, g, ALU.mult)
                last.then_inc(z_done, 1)

            dve.wait_ge(z_done, 2)
            dve.wait_ge(oa_done, 1)
            row_stage(G_PA, N_BR, chunk_src(Q0), R_PA, R_PA, T)
            part_low(chunk_src(ZC[0])(0), R_PB, R_PB, T)
            dve.wait_ge(panel_used, G_PA + N_BR)
            dve.wait_ge(gate1_on, 2)
            for b in range(4):
                last = v.tensor_tensor(flatc(MG + 2 * b, 2), flatc(MG + 2 * b, 2), ps[:, b], ALU.mult)
            last.then_inc(gate1_done, 1)
            row_stage(G_PB, N_BR, chunk_src(ZC[0]), R_PB, R_PB, T, begun=True)
            dve.wait_ge(gate1_done, 1)

            def gated(b):
                one, two = flatc(MG + 2 * b, 2), flatc(MG + 8 + 2 * b, 2)
                step(v.tensor_tensor(two, two, ps[:, 4 + b], ALU.mult))
                v.tensor_tensor(one, one, two, ALU.add).then_inc(gate1_done, 1)
                if b == 1:
                    part_low(chunk_src(MG)(0), R_OUT1, R_OUT1, T)
            residual(3, G_PB + N_BR, gated)
            row_stage(G_OUT1, N_OUT, chunk_src(MG), R_OUT1, R_OUT1, T, begun=True)

            def scaled_add(col):
                def add(b):
                    for k in (2 * b, 2 * b + 1):
                        last = v.scalar_tensor_tensor(h[:, k], ps[:, k // 2, (k % 2) * T:(k % 2 + 1) * T], col(k), h[:, k],
                                                      ALU.mult, ALU.add)
                    last.then_inc(h_set, 1)
                return add
            residual(6, G_OUT1 + N_OUT, scaled_add(mcolumn(5, 0)))

            norm(4, h, gcol(4), mcolumn(6, 0), 0)
            up_stage(G_UP2, 1, T)
            dve.wait_ge(hid_done, 2 * KFF)
            row_stage(G_DOWN2, N_DOWN, hid_src(T), R_DOWN2, R_DOWN2, T, last=False)
            residual(9, G_DOWN2 + N_DOWN, scaled_add(gcol(7)))
            dve.wait_ge(rstd_done, 6)
            for k in range(KD):
                last = v.scalar_tensor_tensor(h[:, k], h[:, k], m1("final", k), rstd[:, 1], ALU.mult, ALU.mult)
                if k % 2:
                    last.then_inc(layer_done, 1)

            with dve.Fori(0, LAYERS) as l:
                link[0], link[1] = l, 0
                first = layer_panel(l, 0)
                low(first[0], first[1] % SLOTS)
                dve.wait_ge(v2_in, at(v2_in, l, 1))
                v.tensor_tensor(scol[:, 32:34], m2("lam_q", 0, 2), m2("lam_k", 0, 2), ALU.mult).then_inc(lam_mul, 1)
                v.tensor_tensor(scol[:, 34:35], m2("subln"), m2("one_less"), ALU.mult)
                norm(0, h, lambda k: m2("attn_norm", k), None, 0, l)
                dve.wait_ge(lam_exp, at(lam_exp, l, 1))
                lstep(v.tensor_tensor(scol[:, 36:37], scol[:, 39:40], scol[:, 38:39], ALU.subtract))
                v.tensor_scalar(scol[:, 40:48], scol[:, 48:56], -1.0, None, ALU.mult)
                v.tensor_tensor(scol[:, 36:37], scol[:, 36:37], m2("lam_init"), ALU.subtract).then_inc(lam_set, 1)
                dve.wait_ge(lam_set, at(lam_set, l, 1))
                def low_next(i):
                    low(l * PER_LAYER + (G_LAYER + i + 1), (G_LAYER + i + 1) % SLOTS)

                def head_scale(n):
                    c, w, gain = ROPES[n][:3]
                    dve.wait_ge(rp_rs, at(rp_rs, l, n + 1))
                    v.scalar_tensor_tensor(flatc(c, w), flatc(c, w), m2(gain), nrs[:, 0:w].rearrange("p c t -> p (c t)"),
                                           ALU.mult, ALU.mult).then_inc(rp_n, 1)

                def head_rope(n):
                    c, w, _, _, cs_, sn = ROPES[n]
                    x = chunks(c, w)
                    dve.wait_ge(rp_rot, at(rp_rot, l, n + 1))
                    def wide(name):
                        return tb(name).unsqueeze(1).to_broadcast([P, w, T])
                    v.tensor_tensor(nrot[:, 0:w], ps[:, 4:6].rearrange("p b (c t) -> p (b c) t", t=T)[:, 0:w], wide(sn),
                                    ALU.mult)
                    lstep(v.tensor_tensor(x, x, wide(cs_), ALU.mult))
                    v.tensor_tensor(flatc(c, w), flatc(c, w), nrot[:, 0:w].rearrange("p c t -> p (c t)"), ALU.add
                                    ).then_inc(rp_done, 1)
                dve.wait_ge(tab_in, 16)
                for i in range(N_HEADS):
                    low_next(i)
                    if i in ROPE_IN:
                        head_rope(ROPE_IN[i])
                    if i in SCALE_IN:
                        head_scale(SCALE_IN[i])
                def stats(n):
                    return smx[:, n % 4]
                def top(n):
                    dve.wait_ge(sc_mm, at(sc_mm, l, n + 1))
                    st = stats(n)
                    lstep(v.tensor_reduce(st[:, 0:2], ps[:, 2 + 2 * (n % 2):4 + 2 * (n % 2), 0:T], AX, ALU.max,
                                          negate=True))
                    v.tensor_scalar(st[:, 2:4], st[:, 0:2], 0.125, None, ALU.mult).then_inc(sc_max, 1)
                def weights(n):
                    dve.wait_ge(sc_exp, at(sc_exp, l, n + 1))
                    st, e = stats(n), ew[n % 2]
                    lstep(v.reciprocal(st[:, 6:8], st[:, 4:6]))
                    if n < 8:
                        lstep(v.tensor_tensor(st[:, 7:8], st[:, 7:8], scol[:, 36:37], ALU.mult))
                        lstep(v.tensor_scalar(e[:, 0], e[:, 0], st[:, 6:7], None, ALU.mult))
                        v.scalar_tensor_tensor(e[:, 0], e[:, 1], st[:, 7:8], e[:, 0], ALU.mult, ALU.add).then_inc(sc_w, 1)
                    else:
                        v.tensor_scalar(e[:, 0], e[:, 0], st[:, 6:7], None, ALU.mult)
                        v.tensor_scalar(e[:, 1], e[:, 1], st[:, 7:8], None, ALU.mult).then_inc(sc_w, 1)
                def decay(g):
                    lstep(v.tensor_scalar(Dm[g % 2].rearrange("p u t -> p (u t)"), tb("ahead"), scol[:, 40 + g:41 + g],
                                          None, ALU.mult))
                    v.scalar_tensor_tensor(Dm[g % 2].rearrange("p u t -> p (u t)"), tb("behind"), scol[:, 44 + g:45 + g],
                                           Dm[g % 2].rearrange("p u t -> p (u t)"), ALU.mult, ALU.add).then_inc(rt_arg, 1)

                def decayed(g):
                    dve.wait_ge(rt_dec, at(rt_dec, l, g + 1))
                    dve.wait_ge(rt_mm, at(rt_mm, l, g + 1))
                    if g >= 2:
                        dve.wait_ge(rt_pv, at(rt_pv, l, g - 1))
                    v.scalar_tensor_tensor(sD[g % 2].rearrange("p u t -> p (u t)"), ps[:, 0], P ** -0.5,
                                           Dm[g % 2].rearrange("p u t -> p (u t)"), ALU.mult, ALU.mult
                                           ).then_inc(rt_mul, 1)
                top(0)
                for n in range(PAIRS):
                    if n + 1 < PAIRS:
                        top(n + 1)
                    weights(n)
                    if N_HEADS + n < N_PROJ:
                        low_next(N_HEADS + n)
                    g = n - (PAIRS - HEADS)
                    if g >= 0:
                        decayed(g)
                    if -1 <= g < HEADS - 1:
                        if g >= 1:
                            dve.wait_ge(rt_mul, at(rt_mul, l, g))
                        decay(g + 1)
                rl = l * R_PER_LAYER + R_LAYER

                def branch_low(n, i):
                    g = O_BR + n * N_BR + i
                    low(layer_panel(l, g)[0], (G_LAYER + g) % SLOTS)

                def branch_part(n, i):
                    j = RO_BR + n * N_BR + i
                    part_low(chunk_src(BRANCHES[n][0])(i), rl + j, R_LAYER + j, T)

                def branch_end(n):
                    return layer_panel(l, O_BR + (n + 1) * N_BR)[0]

                def gated(n, b):
                    gt = GT + BRANCHES[n][1] + 2 * b
                    return v.tensor_tensor(flatc(gt, 2), flatc(gt, 2), ps[:, 4 * (n % 2) + b], ALU.mult)
                dve.wait_ge(pv_out, at(pv_out, l, 8))
                branch_part(0, 0)
                dve.wait_ge(gn_mean, at(gn_mean, l, 1))
                for b in range(2):
                    last = v.scalar_tensor_tensor(flatc(RQ + 2 * b, 2), ps[:, 6 + b], -1.0 / P, flatc(RQ + 2 * b, 2),
                                                  ALU.mult, ALU.add)
                last.then_inc(gn_cen, 1)
                branch_low(0, 1)
                branch_part(0, 1)
                dve.wait_ge(sub_rs, at(sub_rs, l, 1))
                v.scalar_tensor_tensor(flatc(DQ, 4), flatc(DQ, 4), scol[:, 34:35], nrs.rearrange("p c t -> p (c t)"),
                                       ALU.mult, ALU.mult).then_inc(sub_done, 1)
                dve.wait_ge(sub_done, at(sub_done, l, 1))
                branch_low(1, 0)
                branch_part(1, 0)
                branch_low(1, 1)
                branch_part(1, 1)
                dve.wait_ge(gn_rs, at(gn_rs, l, 1))
                for g in range(HEADS):
                    last = v.scalar_tensor_tensor(big[:, RQ + g], big[:, RQ + g], m2("ret_gain", g), nrot[:, g], ALU.mult,
                                                  ALU.mult)
                lstep(last)
                dve.wait_ge(gate_on, at(gate_on, l, 1))
                v.tensor_tensor(flatc(RQ, 4), flatc(RQ, 4), flatc(RG, 4), ALU.mult).then_inc(gn_done, 1)
                dve.wait_ge(panel_used, branch_end(0))
                dve.wait_ge(gate_on, at(gate_on, l, 2))
                for b in range(4):
                    last = gated(0, b)
                last.then_inc(gate_done, 1)
                dve.wait_ge(gn_done, at(gn_done, l, 1))
                branch_low(2, 0)
                branch_part(2, 0)
                branch_low(2, 1)
                branch_part(2, 1)
                dve.wait_ge(panel_used, branch_end(1))
                dve.wait_ge(gate_on, at(gate_on, l, 4))
                dve.wait_ge(gate_done, at(gate_done, l, 1))
                for b in range(4):
                    last = gated(1, b)
                lstep(last)
                v.tensor_tensor(flatc(GT, 8), flatc(GT, 8), flatc(GT + 16, 8), ALU.add).then_inc(gate_done, 1)
                dve.wait_ge(gate_done, at(gate_done, l, 2))
                branch_low(2, 2)

                def gated_last(b):
                    lstep(gated(2, b))
                    v.tensor_tensor(flatc(GT + 2 * b, 2), flatc(GT + 2 * b, 2), flatc(GT + 8 + 2 * b, 2), ALU.add
                                    ).then_inc(gate_done, 1)
                    if b == 1:
                        part_low(chunk_src(GT)(0), rl + RO_OUT, R_LAYER + RO_OUT, T)
                residual(at(sums_out, l, 0, base=12), branch_end(2), gated_last)
                end = row_stage(layer_panel(l, O_OUT), N_OUT, chunk_src(GT), rl + RO_OUT, R_LAYER + RO_OUT, T, begun=True)

                def add_res_done(b):
                    two = h[:, 2 * b:2 * b + 2].rearrange("p c t -> p (c t)")
                    v.tensor_tensor(two, two, ps[:, 4 + b], ALU.add).then_inc(res_done, 1)
                residual(at(sums_out, l, 3, base=12), end, add_res_done)
                norm(1, h, lambda k: m2("mlp_norm", k), None, 0, l)
                low_stage(layer_panel(l, O_MIN), N_MIN)
                dve.wait_ge(m_done, at(m_done, l, N_MIN))
                end = row_stage(layer_panel(l, O_MOUT), N_MOUT, chunk_src(0), rl + RO_MOUT, R_LAYER + RO_MOUT, T, last=False)
                def add_layer_done(b):
                    two = h[:, 2 * b:2 * b + 2].rearrange("p c t -> p (c t)")
                    v.tensor_tensor(two, two, ps[:, b], ALU.add).then_inc(layer_done, 1)
                residual(at(sums_out, l, 6, base=12), end, add_layer_done)
            assert link[1] == per["dve_link"], link[1]

        @block.scalar
        def _(act):
            a = nc.scalar
            count = [0]
            link = [0, 0]

            def step(ins):
                count[0] += 1
                ins.then_inc(act_chain, 1)
                act.wait_ge(act_chain, count[0])

            def lstep(ins):
                link[1] += 1
                ins.then_inc(act_link, 1)
                act.wait_ge(act_link, at(act_link, link[0], link[1]))

            def rms(dst, src, n, e, st):
                st(a.activation(dst, src, ACT.Ln, bias=eps[:, e:e + 1], scale=1.0 / n))
                return a.activation(dst, dst, ACT.Exp, scale=-0.5)

            def squares(n, src, b):
                sq = bigf[:, (n % 2) * 2048:(n % 2) * 2048 + 2048].rearrange("p (k t) -> p k t", t=T)
                a.activation(sq[:, 2 * b:2 * b + 2], src[:, 2 * b:2 * b + 2], ACT.Square).then_inc(sq_done, 1)

            def norm_rms(n, bank, l=None):
                act.wait_ge(sum_done, n + 1 if l is None else at(sum_done, l, n + 1, base=6))
                rms(rstd[:, n % 2], ps[:, bank, 0:T], D, 0, step if l is None else lstep).then_inc(rstd_done, 1)

            def norm_high(k, n, shift, dst0, l=None):
                tmp = bigf[:, 4096:4096 + KD * T].rearrange("p (k t) -> p k t", t=T)
                c = n * KD + k + 1
                act.wait_ge(norm_scaled, at(norm_scaled, l, c, base=5 * KD) if l is not None else c)
                bias = {} if shift is None else {"bias": shift(k)}
                a.activation(xhi[:, k, dst0:dst0 + T], tmp[:, k], ACT.Identity, **bias).then_inc(norm_hi, 1)

            def norm_parts(n, shift, dst0, l=None):
                for k in range(KD):
                    norm_high(k, n, shift, dst0, l)

            def mcolumn(n, who):
                return lambda k: mcol[:, 8 * n + k, who:who + 1]

            def up_stage(g0, which, t):
                def body(i, g, s):
                    act.wait_ge(panel_used, g + 1)
                    a.activation(hid_chunk(i, t), ps[:, 2 * ((s - g0) % UNROLL), 0:t], ACT.Silu).then_inc(silu_done, 1)
                panel_loop(act, g0, N_UP, body)

            def row_stage(first, n, src, r_phase, t, ready=None):
                phase = first[1] if isinstance(first, tuple) else first

                def body(i, g, s):
                    if ready is not None:
                        ready(i)
                    act.wait_ge(panel_used, g - 1)
                    r = (r_phase + (s - phase) % UNROLL) % 2
                    a.activation(ahi[:, r, :, 0:t], src(i), ACT.Identity).then_inc(act_hi, 1)
                panel_loop(act, first, n, body)

            act.dma_start(v1[:], vec1).then_inc(small_in, 16)
            act.dma_start(mat[:], mats).then_inc(small_in, 16)
            act.dma_start(v2all[:], vec2.rearrange("l p n -> p l n")).then_inc(small_in, 16)
            act.dma_start(h[:].rearrange("p k t -> p (k t)"), xT).then_inc(x_in, 16)
            act.dma_start(ws[:, 2048:4096], posemb).then_inc(x_in, 16)
            act.dma_start(ws[:, 0:2048], ctxT).then_inc(x_in, 16)
            act.dma_start(hyin[0:64], hyw).then_inc(hy_in, 16)
            act.dma_start(zfeat, zT).then_inc(hy_in, 16)
            act.dma_start(hwindow.rearrange("p u c -> p (u c)"), window).then_inc(hy_in, 16)
            act.dma_start(ws[:, FILT:FILT + 2048], hyc[:, 0:2048]).then_inc(hy_in, 16)
            act.wait_ge(small_in, 48)
            a.activation(scol[:, 0:2 * KD], m1("c", 0, 2 * KD), ACT.Silu).then_inc(c_silu, 1)
            act.wait_ge(c_silu, 1)
            act.wait_ge(c_zero, 1)
            a.activation(cst[:, 0:4 * KD].rearrange("p (k b) -> p k b", b=4)[:, :, 0:2],
                         scol[:, 0:2 * KD].rearrange("p (k b) -> p k b", b=2), ACT.Identity).then_inc(c_silu, 1)
            def spill(o):
                act.wait_ge(kf_done, 4 * (o + 1))
                act.dma_start(spectra[o], Kst.rearrange("p m c -> p (m c)")).then_inc(kf_out, 16)

            def filter_step(q):
                if q in (F_MLP + 1, F_MLP + 3):
                    n = (q - F_MLP) // 2
                    act.wait_ge(fl_arg, n + 1)
                    a.activation(h2[0:64], ang[0:64, 0], ACT.Sin).then_inc(fl_sin, 1)
                for o in range(2):
                    t = q - F_ORDER - o * F_STEPS
                    if t == 2:
                        act.wait_ge(win_mul, 2 * (o + 1))
                        a.activation(absk, kern.rearrange("p u d c -> p (u d c)"), ACT.Abs).then_inc(abs_done, 1)
                    if t == 13:
                        spill(o)

            def mod_group(i, beside=lambda j: None):
                for j in range(UNROLL):
                    act.wait_ge(panel_used, i * UNROLL + (G_MOD + j + 1))
                    a.activation(mrow[0:4, j], ps[0:4, j, 0:COLS], ACT.Identity).then_inc(mod_copied, 1)
                    beside(j)
                    if isinstance(i, int):
                        filter_step(i * UNROLL + j)
            with act.Fori(0, 2) as i:
                mod_group(i)
            act.wait_ge(x_in, 48)
            act.wait_ge(const_set, 3)
            for b in range(4):
                act.wait_ge(h_set, b + 1)
                squares(0, h, b)
            for b in range(4):
                squares(1, hc, b)
            mod_group(2)
            norm_rms(0, 6)
            norm_rms(1, 7)
            act.wait_ge(mod_added, 1 + 2)
            for n, g0 in ((0, 3), (1, 5)):
                for half in range(2):
                    mod_group(g0 + half, lambda j: norm_high(4 * half + j, n, mcolumn(0, n), n * T))
            for i in range(7, N_MOD // UNROLL):
                mod_group(i)
            spill(1)
            act.wait_ge(mod_turned, N_MOD)
            act.dma_start(ws[:, 4096:6144], lbrow).then_inc(lb_in, 16)
            act.dma_start(mask_in, masks).then_inc(mask_landed, 16)
            act.dma_start(dft.rearrange("p u f -> p (u f)"), hyc[:, 0:1024]).then_inc(hy2_in, 16)
            act.wait_ge(kf_out, 32)
            up_stage(G_UP1, 0, 2 * T)
            act.wait_ge(hid_done, KFF)
            row_stage(G_DOWN1, N_DOWN, hid_src(2 * T), R_DOWN1, 2 * T)
            for b in range(4):
                act.wait_ge(h_set, 4 + b + 1)
                squares(2, h, b)
                squares(3, hc, b)
            norm_rms(2, 0)
            norm_rms(3, 1)
            norm_parts(2, mcolumn(3, 0), 0)
            norm_parts(3, mcolumn(3, 1), T)
            def win(i):
                act.wait_ge(panel_used, G_WIN + i + 1)
                two = ps[:, i % 4 if i < N_FIRST else 4 + i % 2].rearrange("p (u n) -> p u n", n=COLS)
                ctx_two = ps[:, 4 + i % 2].rearrange("p (u n) -> p u n", n=COLS)
                if i < 2:
                    a.activation(Vx[:, :, i * COLS:(i + 1) * COLS], two, ACT.Identity)
                    last = a.activation(Vc[:, :, i * COLS:(i + 1) * COLS], ctx_two, ACT.Identity)
                elif i < 6:
                    d, half = divmod(i - 2, 2)
                    a.activation(chunks(KF[d] + 2 * half, 2), two, ACT.Sigmoid)
                    last = a.activation(sc[d][:, :, half * COLS:(half + 1) * COLS], ctx_two, ACT.Sigmoid)
                else:
                    c = Q0 if i < 8 else G0 - 4 if i < 10 else HY - 8 if i < 16 else MG - 20
                    last = a.activation(chunks(c + 2 * (i - 6), 2), two, ACT.Silu if i < 8 else ACT.Identity)
                last.then_inc(win_out, 1)
            for i in range(N_FIRST):
                win(i)
            act.wait_ge(lb_diff, 2)
            a.activation(scol[:, 16:24], scol[:, 16:24], ACT.Sigmoid).then_inc(lb_sig, 1)
            a.activation(lrow[:, 0], lrow[:, 0], ACT.Sigmoid).then_inc(lb_sig, 1)
            for d in range(2):
                act.wait_ge(cf_done, d + 1)
                if d:
                    act.wait_ge(ckey_done, d)
                a.activation(lgc, sc[d], ACT.Ln).then_inc(cln_done, 1)
                win(N_FIRST + 2 * d)
                act.wait_ge(csum_done, d + 1)
                a.activation(lgc, ps[:, 0:2], ACT.Exp).then_inc(cdec_done, 1)
                win(N_FIRST + 2 * d + 1)
                act.wait_ge(cst_done, d + 1)
                a.activation(s0[d], ps[:, 2 + d].rearrange("p (g e) -> p g e", e=P), ACT.Identity).then_inc(cst_out, 1)
            for d in range(2):
                act.wait_ge(xf_done, d + 1)
                a.activation(EMf[d], flatc(KF[d], 4), ACT.Ln).then_inc(xln_done, 1)
            for i in range(4, 7):
                win(N_FIRST + i)
            for m, (d, n) in enumerate(levels[:-1]):
                act.wait_ge(lv_diff, m + 1)
                if n < len(LEVELS):
                    first, second = halves(EMf[m % 2], LEVELS[n])
                    a.activation(second, second, ACT.Exp)
                    a.activation(first, first, ACT.Exp, scale=-1.0).then_inc(lv_exp, 1)
                else:
                    e = EM[m % 2].rearrange("p (g u) s -> p g u s", u=TT)
                    x = XC[d].rearrange("p (g u) s -> p g u s", u=TT)
                    a.activation(e[:, :, 0], e[:, :, 0], ACT.Exp)
                    a.activation(e[:, :, 1], x[:, :, 1, 1 - d:1 - d + P], ACT.Exp).then_inc(lv_exp, 1)
                if m and N_FIRST + 6 + m < N_WIN:
                    win(N_FIRST + 6 + m)
            act.wait_ge(win_out, N_WIN)
            a.activation(chunks(G0, 4), chunks(G0, 4), ACT.Silu).then_inc(gate1_on, 1)
            act.wait_ge(qe_diff, 1)
            a.activation(EMf[0], EMf[0], ACT.Exp)
            a.activation(EMf[1], EMf[1], ACT.Exp).then_inc(qe_exp, 1)
            act.wait_ge(o_done, 1)
            act.dma_start(idft.rearrange("p m t -> p (m t)"), hyc[:, 2048:3072]).then_inc(hy2_in, 16)
            for o in range(2):
                act.dma_start(Kf[:, o].rearrange("p m c -> p (m c)"), spectra[o]).then_inc(hy2_in, 16)
            a.activation(EMf[0], ps[:, 4:6].rearrange("p b t -> p (b t)"), ACT.Square).then_inc(osq_done, 1)
            act.wait_ge(osum_done, 1)
            rms(EMf[1], ps[:, 6:8].rearrange("p b t -> p (b t)"), P, 0, step).then_inc(orstd_done, 1)
            a.activation(chunks(MG, 16), chunks(MG, 16), ACT.Sigmoid).then_inc(gate1_on, 1)
            for o in range(2):
                act.wait_ge(turn_done, o + 1)
                a.activation(uT, ps[:, 4:6], ACT.Identity).then_inc(uT_done, 1)
            act.wait_ge(oa_done, 1)
            act.wait_ge(z_done, 2)
            act.dma_start(tab, tabs).then_inc(tab_in, 16)
            row_stage(G_PA, N_BR, chunk_src(Q0), R_PA, T)
            row_stage(G_PB, N_BR, chunk_src(ZC[0]), R_PB, T)
            row_stage(G_OUT1, N_OUT, chunk_src(MG), R_OUT1, T, lambda i: act.wait_ge(gate1_done, 1 + i + 1))
            for b in range(4):
                act.wait_ge(h_set, 8 + b + 1)
                squares(4, h, b)
            norm_rms(4, 6)
            norm_parts(4, mcolumn(6, 0), 0)
            up_stage(G_UP2, 1, T)
            act.wait_ge(hid_done, 2 * KFF)
            row_stage(G_DOWN2, N_DOWN, hid_src(T), R_DOWN2, T)
            for b in range(4):
                act.wait_ge(h_set, 12 + b + 1)
                squares(5, h, b)
            norm_rms(5, 7)

            with act.Fori(0, LAYERS) as l:
                link[0], link[1] = l, 0
                for b in range(4):
                    act.wait_ge(layer_done, at(layer_done, l, b + 1))
                    squares(0, h, b)
                a.activation(v2[:].unsqueeze(1), v2all[:, ds(l, 1), :], ACT.Identity).then_inc(v2_in, 1)
                norm_rms(0, 6, l)
                norm_parts(0, None, 0, l)
                act.wait_ge(v2_in, at(v2_in, l, 1))
                a.activation(scol[:, 48:56], m2("decay", 0, 8), ACT.Exp)
                act.wait_ge(lam_mm, at(lam_mm, l, 1))
                a.activation(scol[:, 38:40], ps[:, 5, 0:2], ACT.Exp).then_inc(lam_exp, 1)
                act.wait_ge(tab_in, 16)
                dests = ((VD, 0), (VD, 1), (VR, 0), (VR, 1), (VG, 0))

                def projected(i):
                    act.wait_ge(panel_used, l * PER_LAYER + (G_LAYER + i + 1))
                    two = ps[:, i % 2].rearrange("p (u n) -> p u n", n=COLS)
                    if i < N_VALUES:
                        dst, k = dests[i]
                        if dst is VG:
                            ins = a.activation(VG, two[:, :, 0:P], ACT.Identity)
                        else:
                            ins = a.activation(dst[:, :, k * COLS:(k + 1) * COLS], two, ACT.Identity)
                    else:
                        ins = a.activation(chunks(PLAIN[i - N_VALUES], 2), two, ACT.Identity)
                    ins.then_inc(proj_out, 1)

                def head_square(n):
                    act.wait_ge(proj_out, at(proj_out, l, (7, 9, 11, 12)[n]))
                    c, w = ROPES[n][:2]
                    a.activation(nsq[:, 0:w], chunks(c, w), ACT.Square).then_inc(rp_sq, 1)

                def head_rms(n):
                    w = ROPES[n][1]
                    act.wait_ge(rp_sum, at(rp_sum, l, n + 1))
                    if n:
                        act.wait_ge(rp_n, at(rp_n, l, n))
                    rms(nrs[:, 0:w], ps[:, 2:4].rearrange("p b (c t) -> p (b c) t", t=T)[:, 0:w], 64, 0, lstep
                        ).then_inc(rp_rs, 1)
                for i in range(N_HEADS):
                    projected(i)
                    if i in RMS_AFTER:
                        head_rms(RMS_AFTER[i])
                    if i in SQUARE_AFTER:
                        head_square(SQUARE_AFTER[i])

                def expo(n):
                    act.wait_ge(sc_max, at(sc_max, l, n + 1))
                    if n >= 2:
                        act.wait_ge(sc_turn, at(sc_turn, l, n - 1))
                    st = smx[:, n % 4]
                    for m in range(2):
                        last = a.activation(ew[n % 2][:, m], ps[:, 2 + 2 * (n % 2) + m, 0:T], ACT.Exp, bias=st[:, 2 + m:3 + m],
                                            scale=0.125, accum_out=st[:, 4 + m:5 + m])
                    last.then_inc(sc_exp, 1)

                def turned(n):
                    act.wait_ge(sc_turn, at(sc_turn, l, n + 1))
                    p, u = divmod(n, 2)
                    if p >= 2:
                        act.wait_ge(pv_mm, at(pv_mm, l, p - 1))
                    k = 1 if n < 8 else 2
                    for m in range(k):
                        last = a.activation(wT[p % 2][:, m, :, u * P:(u + 1) * P],
                                            ps[:, 6, m * T:(m + 1) * T].rearrange("p (k q) -> p k q", q=P),
                                            ACT.Identity)
                    last.then_inc(sc_wT, 1)

                def attended(p):
                    act.wait_ge(pv_mm, at(pv_mm, l, p + 1))
                    a.activation(big[:, DQ + p if p < 4 else GQ + p - 4], ps[:, 7, 0:T], ACT.Identity
                                 ).then_inc(pv_out, 1)

                def retained(f):
                    act.wait_ge(rt_pv, at(rt_pv, l, f + 1))
                    a.activation(big[:, RQ + f], ps[:, 1, 0:T], ACT.Identity).then_inc(rt_out, 1)
                expo(0)
                for n in range(PAIRS):
                    if n + 1 < PAIRS:
                        expo(n + 1)
                    if N_HEADS + n < N_PROJ:
                        projected(N_HEADS + n)
                    g = n - (PAIRS - HEADS)
                    if g >= 0:
                        act.wait_ge(rt_arg, at(rt_arg, l, g + 1))
                        a.activation(Dm[g % 2], Dm[g % 2], ACT.Exp).then_inc(rt_dec, 1)
                    turned(n)
                    if g >= 1:
                        retained(g - 1)
                    if n % 2 and n > 1:
                        attended(n // 2 - 1)
                attended(7)
                retained(HEADS - 1)
                act.wait_ge(pv_out, at(pv_out, l, 8))
                act.wait_ge(rt_out, at(rt_out, l, HEADS))
                a.activation(nsq, chunks(DQ, 4), ACT.Square).then_inc(sub_sq, 1)

                def branch_high(n, i):
                    g, j = O_BR + n * N_BR + i, R_LAYER + RO_BR + n * N_BR + i
                    act.wait_ge(panel_used, layer_panel(l, g)[0] - 1)
                    a.activation(ahi[:, j % 2, :, 0:T], chunk_src(BRANCHES[n][0])(i), ACT.Identity).then_inc(act_hi, 1)
                branch_high(0, 0)
                branch_high(0, 1)
                act.wait_ge(sub_sum, at(sub_sum, l, 1))
                act.wait_ge(rt_mul, at(rt_mul, l, HEADS))
                rms(nrs, ps[:, 4:6].rearrange("p b (c t) -> p (b c) t", t=T), P, 1, lstep).then_inc(sub_rs, 1)
                act.wait_ge(gn_cen, at(gn_cen, l, 1))
                a.activation(nsq, chunks(RQ, 4), ACT.Square).then_inc(gn_sq, 1)
                act.wait_ge(proj_out, at(proj_out, l, N_PROJ))
                a.activation(chunks(RG, 4), chunks(RG, 4), ACT.Silu).then_inc(gate_on, 1)
                act.wait_ge(sub_done, at(sub_done, l, 1))
                branch_high(1, 0)
                act.wait_ge(gn_sum, at(gn_sum, l, 1))
                rms(nrot, ps[:, 4:6].rearrange("p b (c t) -> p (b c) t", t=T), P, 1, lstep).then_inc(gn_rs, 1)
                branch_high(1, 1)
                for _, gt in BRANCHES:
                    a.activation(chunks(GT + gt, 8), chunks(GT + gt, 8), ACT.Sigmoid).then_inc(gate_on, 1)
                act.wait_ge(gn_done, at(gn_done, l, 1))
                branch_high(2, 0)
                branch_high(2, 1)
                row_stage(layer_panel(l, O_OUT), N_OUT, chunk_src(GT), R_LAYER + RO_OUT, T,
                          lambda i: act.wait_ge(gate_done, at(gate_done, l, 2 + i + 1)))
                for b in range(4):
                    act.wait_ge(res_done, at(res_done, l, b + 1))
                    squares(1, h, b)
                norm_rms(1, 0, l)
                norm_parts(1, None, 0, l)
                mfirst = layer_panel(l, O_MIN)

                def relu2(i, g, s):
                    j = (s - mfirst[1]) % UNROLL
                    act.wait_ge(panel_used, g + 1)
                    a.activation(rtmp[j % 2], ps[:, j], ACT.Relu).then_inc(relu_done, 1)
                    act.wait_ge(relu_done, at(relu_done, l, 1) + i)
                    a.activation(big[:, ds(i * 2, 2), :].rearrange("p c t -> p (c t)"), rtmp[j % 2], ACT.Square
                                 ).then_inc(m_done, 1)
                panel_loop(act, mfirst, N_MIN, relu2)
                act.wait_ge(m_done, at(m_done, l, N_MIN))
                row_stage(layer_panel(l, O_MOUT), N_MOUT, chunk_src(0), R_LAYER + RO_MOUT, T)
            assert link[1] == per["act_link"], link[1]

        @block.tensor
        def _(pe):
            mm = nc.tensor.matmul

            def product(out, w_hi, w_lo, x_hi, x_lo, first, last):
                mm(out, w_hi, x_hi, start=first, stop=False, skip_group_check=True)
                mm(out, w_hi, x_lo, start=False, stop=False, skip_group_check=True)
                return mm(out, w_lo, x_hi, start=False, stop=last, skip_group_check=True)

            def feature_panel(s, outs, x0, t):
                for c, out in enumerate(outs):
                    for k in range(KD):
                        at_ = k * COLS + c * P
                        last = product(out, whi[:, s % 2, at_:at_ + P], wlo[:, s % 2, at_:at_ + P], xhi[:, k, x0:x0 + t],
                                       xlo[:, k, x0:x0 + t], k == 0, k == KD - 1)
                return last

            def token_panel(s, outs, x0, n):
                for u, out in enumerate(outs):
                    for k in range(KD):
                        x = slice(x0 + u * P, x0 + (u + 1) * P)
                        c = slice(k * COLS, k * COLS + n)
                        last = product(out, xhi[:, k, x], xlo[:, k, x], whi[:, s % 2, c], wlo[:, s % 2, c], k == 0, k == KD - 1)
                return last

            def row_panel(s, r, outs, t, first, last, by_banks=False):
                for j, (out, opens) in enumerate(outs):
                    for k in range(ROWK):
                        w = slice(k * D + j * P, k * D + (j + 1) * P)
                        ins = product(out, whi[:, s % 2, w], wlo[:, s % 2, w], ahi[:, r % 2, k, 0:t], alo[:, r % 2, k, 0:t],
                                      first and opens and k == 0, last and k == ROWK - 1)
                    if by_banks and j % 2 and j < KD - 1:
                        ins.then_inc(sums_out, 1)
                return ins

            def streamed(s, outs, x0, t, base, token=False):
                for k in range(KD):
                    pe.wait_ge(norm_lo, base + (k + 1))
                    for c, (out, opens) in enumerate(outs):
                        w = slice(k * COLS, (k + 1) * COLS) if token else slice(k * COLS + c * P, k * COLS + (c + 1) * P)
                        x = slice(x0 + c * P, x0 + (c + 1) * P) if token else slice(x0, x0 + t)
                        a = whi[:, s % 2, w], wlo[:, s % 2, w]
                        b = xhi[:, k, x], xlo[:, k, x]
                        last = product(out, *(b + a if token else a + b), k == 0 and opens, k == KD - 1)
                return last

            def opened(outs):
                return [(out, c == 0) for c, out in enumerate(outs)]

            def sums(b0, t=T):
                if t == T:
                    return [(ps[:, b0 + j // 2, (j % 2) * T:(j % 2 + 1) * T], j % 2 == 0) for j in range(KD)]
                return [(ps[:, j, 0:t], True) for j in range(KD)]

            def row_stage(first, n, r0, r_phase, outs, t, by_banks=False, between=lambda: None):
                g0, phase = first if isinstance(first, tuple) else (first, first)

                def one(i, g, s, begins, ends):
                    pe.wait_ge(lo_done, g + 1)
                    pe.wait_ge(act_lo, r0 + i + 1)
                    row_panel(s, r_phase + (s - phase) % UNROLL, outs, t, begins, ends, by_banks and ends).then_inc(panel_used, 1)
                one(0, g0, phase % UNROLL, True, False)
                between()
                nxt = (g0 + 1, phase + 1) if isinstance(first, tuple) else g0 + 1
                panel_loop(pe, nxt, n - 2, lambda i, g, s: one(i + 1, g, s, False, False))
                one(n - 1, g0 + (n - 1), (phase + n - 1) % UNROLL, False, True)

            def norm_sums(n, bank, l=None):
                sq = bigf[:, (n % 2) * 2048:(n % 2) * 2048 + 2048].rearrange("p (k t) -> p k t", t=T)
                for k in range(KD):
                    if k % 2 == 0:
                        c = 4 * n + k // 2 + 1
                        pe.wait_ge(sq_done, c if l is None else at(sq_done, l, c, base=24))
                    last = mm(ps[:, bank, 0:T], ones[:], sq[:, k], start=k == 0, stop=k == KD - 1)
                last.then_inc(sum_done, 1)

            def up_stage(g0, which, t, base=None):
                def one(i, g, s, reused):
                    j = (s - g0) % UNROLL
                    pe.wait_ge(lo_done, g + 1)
                    if reused:
                        pe.wait_ge(hid_done, i + (which * KFF - UNROLL + 1))
                    outs = [ps[:, 2 * j, 0:t], ps[:, 2 * j + 1, 0:t]]
                    if isinstance(i, int) and i == 0 and base is not None:
                        last = streamed(s, [(o, True) for o in outs], 0, t, base)
                    else:
                        last = feature_panel(s, outs, 0, t)
                    last.then_inc(panel_used, 1)
                for i in range(UNROLL):
                    one(i, g0 + i, (g0 + i) % UNROLL, False)
                panel_loop(pe, g0 + UNROLL, N_UP - UNROLL, lambda i, g, s: one(i + UNROLL, g, s, True))

            def halves_of(b):
                return [ps[:, b, 0:T], ps[:, b, T:2 * T]]

            pe.wait_ge(c_split, 1)

            def turn(i, j):
                pe.wait_ge(mod_copied, i * UNROLL + (j + 1))
                if j == 0:
                    pe.wait_ge(mod_added, i + 1)
                pe.wait_ge(small_in, 48)
                fold = mat[0:4, MATS["fold"][0]:MATS["fold"][0] + 2]
                for c in range(2):
                    last = mm(ps[:, 4, 4 * j + 2 * c:4 * j + 2 * c + 2], mrow[0:4, j, c * P:(c + 1) * P], fold, start=True,
                              stop=True)
                last.then_inc(mod_turned, 1)

            def filter_step(q):
                if q == F_MLP:
                    pe.wait_ge(hy_in, 64)
                    mm(ps[0:64, 5, 0:T], hw1, zfeat[0:33], start=True, stop=True).then_inc(fl_mm, 1)
                if q == F_MLP + 2:
                    pe.wait_ge(fl_sin, 1)
                    mm(ps[0:64, 5, 0:T], hw2, h2[0:64], start=True, stop=True).then_inc(fl_mm, 1)
                for o in range(2):
                    t = q - F_ORDER - o * F_STEPS
                    if t in (0, 1):
                        if t:
                            pe.wait_ge(win_mul, 2 * o + 1)
                        elif o:
                            pe.wait_ge(kf_done, 4)
                        else:
                            pe.wait_ge(fl_sin, 2)
                            pe.wait_ge(rstd_done, 2)
                        for d in range(2):
                            last = mm(ps[:, 6 + d], h2[0:64, t * P:(t + 1) * P], hw3[:, (2 * o + d) * 512:(2 * o + d + 1) * 512],
                                      start=True, stop=True)
                        last.then_inc(h3_mm, 1)
                    if t == 3:
                        pe.wait_ge(abs_done, o + 1)
                        for x in range(4):
                            last = mm(ps[:, 5], ones[:], absk[:, x * 512:(x + 1) * 512], start=x == 0, stop=x == 3)
                        last.then_inc(l1_mm, 1)
                    if 4 <= t < F_STEPS:
                        m, u = divmod(t - 4, 2)
                        if u == 0:
                            pe.wait_ge(win_mul, 2 * (o + 1))
                            if m >= 2:
                                pe.wait_ge(kf_done, 4 * o + m - 1)
                        for d in range(2):
                            last = mm(ps[:, 6 + m % 2], fdft[:, d, u, m * P:(m + 1) * P], kern[:, u, d], start=u + d == 0,
                                      stop=u + d == 2)
                        if u:
                            last.then_inc(kf_mm, 1)

            def mod_group(i):
                for j in range(UNROLL):
                    pe.wait_ge(lo_done, i * UNROLL + (G_MOD + j + 1))
                    for k in range(KD):
                        c, w = cst[:, 4 * k:4 * k + P], slice(k * COLS, (k + 1) * COLS)
                        mm(ps[:, j, 0:COLS], c, whi[:, j % 2, w], start=k == 0, stop=False)
                        last = mm(ps[:, j, 0:COLS], c, wlo[:, j % 2, w], start=False, stop=k == KD - 1)
                    last.then_inc(panel_used, 1)
                    if j:
                        turn(i, j - 1)
                    if isinstance(i, int):
                        filter_step(i * UNROLL + j)
                turn(i, UNROLL - 1)

            with pe.Fori(0, 2) as i:
                mod_group(i)
            mod_group(2)
            pe.wait_ge(const_set, 3)
            norm_sums(0, 6)
            norm_sums(1, 7)
            for i in range(3, N_MOD // UNROLL):
                mod_group(i)

            pe.wait_ge(norm_lo, 2 * KD)
            up_stage(G_UP1, 0, 2 * T)
            pe.wait_ge(hid_done, KFF)
            row_stage(G_DOWN1, N_DOWN, R_DOWN1, R_DOWN1, sums(0, 2 * T), 2 * T, by_banks=True)
            for k in range(KD):
                if k % 2 == 0:
                    pe.wait_ge(sq_done, 8 + k + 2)
                for n in range(2):
                    sq = bigf[:, n * 2048 + k * T:n * 2048 + (k + 1) * T]
                    last = mm(ps[:, n, 0:T], ones[:], sq, start=k == 0, stop=k == KD - 1)
                    if k == KD - 1:
                        last.then_inc(sum_done, 1)

            def win(i):
                g, s = G_WIN + i, (G_WIN + i) % UNROLL
                pe.wait_ge(lo_done, g + 1)
                if i >= 4:
                    pe.wait_ge(win_out, i - 3 if i < N_FIRST else i - 1)
                bank = i % 4 if i < N_FIRST else 4 + i % 2
                if i >= 6:
                    last = feature_panel(s, halves_of(bank), 0, T)
                else:
                    if i >= 2:
                        pe.wait_ge(win_out, i - 1)
                    both = [ps[:, 4 + i % 2, 0:COLS], ps[:, 4 + i % 2, COLS:2 * COLS]]
                    if i == 0:
                        streamed(s, opened([ps[:, bank, 0:COLS], ps[:, bank, COLS:2 * COLS]]), 0, COLS, 2 * KD, token=True)
                        streamed(s, opened(both), T, COLS, 3 * KD, token=True).then_inc(panel_used, 1)
                        return
                    token_panel(s, both, T, COLS)
                    if i < 2:
                        last = token_panel(s, [ps[:, bank, 0:COLS], ps[:, bank, COLS:2 * COLS]], 0, COLS)
                    else:
                        last = feature_panel(s, halves_of(bank), 0, T)
                last.then_inc(panel_used, 1)
            for i in range(N_FIRST):
                win(i)
            pe.wait_ge(win_out, N_FIRST)
            for d, order in enumerate(("after", "before")):
                win(N_FIRST + 2 * d)
                pe.wait_ge(cln_done, d + 1)
                if d:
                    pe.wait_ge(cdec_done, d)
                near, far = d, 1 - d
                mm(ps[:, far], mt(order), lgc[:, far], start=True, stop=True)
                mm(ps[:, near], mt(order), lgc[:, near], start=True, stop=False)
                mm(ps[:, near], ones[:], lgc[:, far], start=False, stop=True).then_inc(csum_done, 1)
                win(N_FIRST + 2 * d + 1)
                pe.wait_ge(ckey_done, d + 1)
                for g in range(HEADS):
                    for u in range(TT):
                        last = mm(ps[:, 2 + d, g * P:(g + 1) * P], sc[d][:, u, g * P:(g + 1) * P], Vc[:, u, g * P:(g + 1) * P],
                                  start=u == 0, stop=u == TT - 1)
                last.then_inc(cst_done, 1)
            q = flatc(Q0, 4)
            for i in range(4, 7):
                win(N_FIRST + i)
            pe.wait_ge(cst_out, 2)
            for m, (d, n) in enumerate(levels):
                if d == 2:
                    pe.wait_ge(lv_diff, m + 1)
                else:
                    pe.wait_ge(lv_mul, m + 1)
                if m >= 2:
                    pe.wait_ge(lv_sel, m - 1)
                e, b = EM[m % 2], 2 * (m % 2)
                for x in range(HEADS * TT):
                    g, u = divmod(x, TT)
                    o = slice(g * P, (g + 1) * P)
                    if d == 2:
                        last = mm(ps[:, b + u, o], e[:, x], q[:, x * P:(x + 1) * P], start=True, stop=True)
                    elif n < len(LEVELS):
                        last = mm(ps[:, b + u, o], e[:, x], e[:, x], start=True, stop=True)
                    elif u == d:
                        last = mm(ps[:, b, o], e[:, x], e[:, 2 * g + 1 - d], start=True, stop=True)
                last.then_inc(lv_score, 1)
                if N_FIRST + 7 + m < N_WIN:
                    win(N_FIRST + 7 + m)
            pe.wait_ge(win_out, N_WIN)
            pe.wait_ge(lv_sel, len(levels))
            pe.wait_ge(qe_done, 1)
            for g in range(HEADS):
                o = halves_of(4 + g // 2)[g % 2]
                for u in range(TT):
                    mm(o, Vx[:, u, g * P:(g + 1) * P], S[:, u, g], start=u == 0, stop=False)
                for d in range(2):
                    last = mm(o, s0[d][:, g], EMf[d][:, g * T:(g + 1) * T], start=False, stop=d == 1)
            last.then_inc(o_done, 1)
            pe.wait_ge(osq_done, 1)
            for g in range(HEADS):
                last = mm(halves_of(6 + g // 2)[g % 2], ones[:], EMf[0][:, g * T:(g + 1) * T], start=True, stop=True)
            last.then_inc(osum_done, 1)
            pe.wait_ge(hy2_in, 64)
            for o in range(2):
                if o == 0:
                    pe.wait_ge(conv_done, 1)
                    pe.wait_ge(oa_done, 1)
                else:
                    pe.wait_ge(z_done, 1)
                for c in range(4):
                    for u in range(TT):
                        last = nc.tensor.transpose(ps[:, 4 + u, c * P:(c + 1) * P], big[:, ZC[0] + c, u * P:(u + 1) * P], ident)
                last.then_inc(turn_done, 1)
                pe.wait_ge(uT_done, o + 1)
                for m in range(4):
                    for u in range(TT):
                        last = mm(ps[:, m], dft[:, u, m * P:(m + 1) * P], uT[:, u], start=u == 0, stop=u == 1)
                last.then_inc(uf_mm, 1)
                for m in range(4):
                    if m % 2 == 0:
                        pe.wait_ge(pf_done, 2 * o + m // 2 + 1)
                    for c in range(4):
                        f = (Pf, Pi)[m // 2][:, m % 2, c * P:(c + 1) * P]
                        last = mm(halves_of(6 + c // 2)[c % 2], f, idft[:, m], start=m == 0 and c % 2 == 0, stop=m == 3,
                                  skip_group_check=True)
                last.then_inc(y_mm, 1)
            row_stage(G_PA, N_BR, R_PA, R_PA, sums(0), T)
            row_stage(G_PB, N_BR, R_PB, R_PB, sums(4), T, by_banks=True)
            row_stage(G_OUT1, N_OUT, R_OUT1, R_OUT1, sums(0), T, by_banks=True)
            norm_sums(4, 6)
            up_stage(G_UP2, 1, T, base=4 * KD)
            row_stage(G_DOWN2, N_DOWN, R_DOWN2, R_DOWN2, sums(0), T, by_banks=True)
            norm_sums(5, 7)

            with pe.Fori(0, LAYERS) as l:
                norm_sums(0, 6, l)
                pe.wait_ge(lam_mul, at(lam_mul, l, 1))
                mm(ps[:, 5, 0:2], ones[:], scol[:, 32:34], start=True, stop=True).then_inc(lam_mm, 1)
                def proj(i):
                    pe.wait_ge(lo_done, l * PER_LAYER + (G_LAYER + i + 1))
                    if i >= 2:
                        pe.wait_ge(proj_out, at(proj_out, l, i - 1))
                    s, j = (G_LAYER + i) % UNROLL, i % 2
                    if i == 0:
                        last = streamed(s, opened(halves_of(j)), 0, COLS, at(norm_lo, l, 0, base=5 * KD), token=True)
                    elif i < N_VALUES:
                        n = COLS if i < 4 else P
                        last = token_panel(s, [ps[:, j, 0:n], ps[:, j, COLS:COLS + n]], 0, n)
                    else:
                        last = feature_panel(s, halves_of(j), 0, T)
                    last.then_inc(panel_used, 1)

                def head_sums(n):
                    c, w = ROPES[n][:2]
                    pe.wait_ge(rp_sq, at(rp_sq, l, n + 1))
                    for x in range(w):
                        last = mm(halves_of(2 + x // 2)[x % 2], mt("block64"), nsq[:, x], start=True, stop=True)
                    last.then_inc(rp_sum, 1)

                def head_rotate(n, out):
                    c, w, gain, rot = ROPES[n][:4]
                    if gain:
                        pe.wait_ge(rp_n, at(rp_n, l, n + 1))
                    else:
                        pe.wait_ge(proj_out, at(proj_out, l, out))
                    if n:
                        pe.wait_ge(rp_done, at(rp_done, l, n))
                    for x in range(w):
                        last = mm(halves_of(4 + x // 2)[x % 2], mt(rot), big[:, c + x], start=True, stop=True)
                    last.then_inc(rp_rot, 1)
                for i in range(N_HEADS):
                    proj(i)
                    if i in ROT_AFTER:
                        head_rotate(*ROT_AFTER[i])
                    if i in SUM_AFTER:
                        head_sums(SUM_AFTER[i])

                def scores(n):
                    if n >= 2:
                        pe.wait_ge(sc_exp, at(sc_exp, l, n - 1))
                    hd, u = divmod(n, 2)
                    qc, kc = (DQ + hd, DK + hd) if n < 8 else (GQ + hd - 4, GK + (hd - 4) // 2)
                    for m in range(2):
                        r = slice(64 * m, 64 * m + 64)
                        last = mm(ps[:, 2 + 2 * (n % 2) + m, 0:T], big[r, qc, u * P:(u + 1) * P], big[r, kc], start=True,
                                  stop=True)
                    last.then_inc(sc_mm, 1)

                def turn_weights(n):
                    pe.wait_ge(sc_w, at(sc_w, l, n + 1))
                    if n >= 1:
                        pe.wait_ge(sc_wT, at(sc_wT, l, n))
                    for x in range(2 if n < 8 else 4):
                        m, k = divmod(x, 2)
                        last = nc.tensor.transpose(ps[:, 6, x * P:(x + 1) * P], ew[n % 2][:, m, k * P:(k + 1) * P], ident)
                    last.then_inc(sc_turn, 1)

                def attend(p):
                    pe.wait_ge(sc_wT, at(sc_wT, l, 2 * p + 2))
                    if p >= 1:
                        pe.wait_ge(pv_out, at(pv_out, l, p))
                    for m in range(1 if p < 4 else 2):
                        for k in range(TT):
                            if p < 4:
                                out_, val = ps[:, 7, 0:T], VD[:, k, p * P:(p + 1) * P]
                            else:
                                kv = (p - 4) // 2
                                out_, val = ps[64 * m:64 * m + 64, 7, 0:T], VG[:, k, kv * 64:kv * 64 + 64]
                            last = mm(out_, val, wT[p % 2][:, m, k], start=k == 0, stop=k == TT - 1)
                    last.then_inc(pv_mm, 1)

                def retention_scores(g):
                    if g == 0:
                        pe.wait_ge(proj_out, at(proj_out, l, N_PROJ))
                    else:
                        pe.wait_ge(rt_mul, at(rt_mul, l, g))
                    for u in range(TT):
                        last = mm(halves_of(0)[u], big[:, RK + g, u * P:(u + 1) * P], big[:, RQ + g], start=True, stop=True)
                    last.then_inc(rt_mm, 1)

                def retain(f):
                    pe.wait_ge(rt_mul, at(rt_mul, l, f + 1))
                    if f >= 1:
                        pe.wait_ge(rt_out, at(rt_out, l, f))
                    for u in range(TT):
                        last = mm(ps[:, 1, 0:T], VR[:, u, f * P:(f + 1) * P], sD[f % 2][:, u], start=u == 0, stop=u == TT - 1)
                    last.then_inc(rt_pv, 1)
                pe.wait_ge(rp_done, at(rp_done, l, len(ROPES)))
                scores(0)
                for n in range(PAIRS):
                    if n + 1 < PAIRS:
                        scores(n + 1)
                    if N_HEADS + n < N_PROJ:
                        proj(N_HEADS + n)
                    g = n - (PAIRS - HEADS)
                    if g >= 0:
                        retention_scores(g)
                    turn_weights(n)
                    if g >= 1:
                        retain(g - 1)
                    if n % 2 and n > 1:
                        attend(n // 2 - 1)
                attend(7)
                retain(HEADS - 1)
                pe.wait_ge(sub_sq, at(sub_sq, l, 1))
                for x in range(4):
                    last = mm(halves_of(4 + x // 2)[x % 2], ones[:], nsq[:, x], start=True, stop=True)
                last.then_inc(sub_sum, 1)
                pe.wait_ge(rt_out, at(rt_out, l, HEADS))
                for x in range(4):
                    last = mm(halves_of(6 + x // 2)[x % 2], ones[:], big[:, RQ + x], start=True, stop=True)
                last.then_inc(gn_mean, 1)
                rl = l * R_PER_LAYER + R_LAYER

                def branch_stage(n, **how):
                    row_stage(layer_panel(l, O_BR + n * N_BR), N_BR, rl + RO_BR + n * N_BR, R_LAYER + RO_BR + n * N_BR,
                              sums(4 * (n % 2)), T, **how)

                def retention_squares():
                    pe.wait_ge(gn_sq, at(gn_sq, l, 1))
                    for x in range(4):
                        last = mm(halves_of(4 + x // 2)[x % 2], ones[:], nsq[:, x], start=True, stop=True)
                    last.then_inc(gn_sum, 1)
                branch_stage(0, between=retention_squares)
                pe.wait_ge(gn_rs, at(gn_rs, l, 1))
                branch_stage(1)
                branch_stage(2, by_banks=True)
                row_stage(layer_panel(l, O_OUT), N_OUT, rl + RO_OUT, R_LAYER + RO_OUT, sums(4), T, by_banks=True)
                norm_sums(1, 0, l)
                mfirst = layer_panel(l, O_MIN)

                def up(i, g, s):
                    pe.wait_ge(lo_done, g + 1)
                    if not isinstance(i, int) or i >= 4:
                        pe.wait_ge(relu_done, at(relu_done, l, 0) + (i - 3))
                    outs = halves_of((s - mfirst[1]) % 4)
                    if isinstance(i, int) and i == 0:
                        last = streamed(s, opened(outs), 0, T, at(norm_lo, l, KD, base=5 * KD))
                    else:
                        last = feature_panel(s, outs, 0, T)
                    last.then_inc(panel_used, 1)
                for i in range(4):
                    up(i, mfirst[0] + i, (mfirst[1] + i) % UNROLL)
                panel_loop(pe, layer_panel(l, O_MIN + 4), N_MIN - 4, lambda i, g, s: up(i + 4, g, s))
                row_stage(layer_panel(l, O_MOUT), N_MOUT, rl + RO_MOUT, R_LAYER + RO_MOUT, sums(0), T, by_banks=True)


def _column_panels(w, cols):
    w = w[:, cols] if cols is not None else w
    n = w.shape[1] // COLS
    return w.reshape(KD, P, n, COLS).transpose(2, 1, 0, 3).reshape(n, P, PANEL)


def _row_panels(w):
    n = w.shape[0] // (P * ROWK)
    return w.reshape(n, ROWK, P, D).transpose(0, 2, 1, 3).reshape(n, P, PANEL)


def _cols(x):
    x = np.asarray(x).reshape(-1)
    return x.reshape(-1, P).T


def _pad(x):
    out = np.zeros((P, 1), np.float32)
    out[:x.size, 0] = x.reshape(-1)
    return out


def _up_panels(gate, up):
    both = np.stack([gate.reshape(D, KFF, P), up.reshape(D, KFF, P)], 2).reshape(D, KFF * 2 * P)
    return _column_panels(both, None)


def kernel(**inputs):
    import concourse.bacc as _bacc
    from concourse import mybir as _mybir
    from concourse.bass_utils import run_bass_kernel_spmd as _run

    x = {k: np.asarray(v) for k, v in inputs.items()}
    def first(name):
        return x[name][0]

    panels = [_column_panels(first("mod_w"), None)]
    ffn = [[_up_panels(first("ffn_w_gate")[i], first("ffn_w_up")[i]), _row_panels(first("ffn_w_down")[i])] for i in range(2)]
    panels += ffn[0] + [_column_panels(first("w_in"), None), _row_panels(first("w_proj_a")), _row_panels(first("w_proj_b")),
                        _row_panels(first("w_out"))] + ffn[1]
    at = np.cumsum([0, 512, 512, 512, 512, 512, 512, 512, 512, 128, 128, 3072])
    dq, dk, dv, rq, rk, rv, rg, gq, gk, gv, gates = (np.arange(at[i], at[i + 1]) for i in range(11))
    order = np.concatenate([dv, rv, gv, gv, dq, dk, gq, gk[:64], gk[:64], gk[64:], gk[64:], rq, rk, rg, gates])
    for l in range(LAYERS):
        panels += [_column_panels(x["w_in_2"][l], order)] + [_row_panels(x["w_branch_2"][l][b]) for b in (2, 0, 1)]
        panels += [_row_panels(x["w_out_2"][l]), _column_panels(x["w_mlp_in_2"][l], None), _row_panels(x["w_mlp_out_2"][l])]

    c = np.stack([_cols(x["c"]), _cols(x["c_ctx"])], 2).reshape(P, -1)
    logits = x["hgrn_lb_logits"]
    vec1 = np.concatenate([
        c, _cols(first("mod_b")), _cols(logits[0]), _cols(logits[1]), _cols(first("hgrn_norm_w")), _cols(first("hyena_conv_w")),
        _cols(first("hyena_conv_b")), _cols(first("hyena_bias")), _cols(x["final_norm_w"]), _pad(first("hyena_b1")),
        _pad(first("hyena_freq1")), _pad(first("hyena_b2")), _pad(first("hyena_freq2"))], 1)
    vec2 = []
    for l in range(LAYERS):
        twice = [_cols(np.concatenate([x[n][l], x[n][l]])) for n in ("diff_q_norm_2", "diff_k_norm_2", "gqa_q_norm_2",
                                                                     "gqa_k_norm_2")]
        decay = np.concatenate([x["ret_decay_fwd_2"][l], x["ret_decay_bwd_2"][l]])
        start = 0.8 - 0.6 * math.exp(-0.3 * l)
        vec2.append(np.concatenate(
            [_cols(x["attn_norm_2"][l]), _cols(x["mlp_norm_2"][l])] + twice
            + [_cols(x["diff_subln_2"][l]), _cols(x["ret_group_norm_2"][l]), np.broadcast_to(decay, (P, 8))]
            + [_pad(x[f"diff_lam_{n}_2"][l]) for n in ("q1", "q2", "k1", "k2")]
            + [np.full((P, 1), start, np.float32), np.full((P, 1), 1.0 - start, np.float32)], 1))
    hyw = np.zeros((64, 2176), np.float32)
    hyw[:33, 0:64] = first("hyena_w1")
    hyw[:, 64:128] = first("hyena_w2")
    hyw[:, 128:] = first("hyena_w3")

    def tokens(a):
        return a[0].T.reshape(KD, P, T).transpose(1, 0, 2).reshape(P, KD * T)

    arrays = {
        "stream": np.concatenate(panels, 0), "xT": tokens(x["x"]), "ctxT": tokens(x["ctx"]), "vec1": vec1,
        "vec2": np.stack(vec2), "lbrow": np.broadcast_to(logits.reshape(1, 2048), (P, 2048)), "hyw": hyw,
        **shape_constants(),
    }
    arrays = {f"in_{k}": np.ascontiguousarray(v) for k, v in arrays.items()}
    nc = _bacc.Bacc("TRN2", target_bir_lowering=False, num_devices=1)
    args = {k[3:]: nc.dram_tensor(k, v.shape, _mybir.dt.from_np(v.dtype), kind="ExternalInput").ap()
            for k, v in arrays.items()}
    args["out"] = nc.dram_tensor("out_0", (P, KD * T), _mybir.dt.float32, kind="ExternalOutput").ap()
    args["spectra"] = nc.dram_tensor("spectra", (2, P, 4 * 512), _mybir.dt.float32).ap()
    build(nc, **args)
    r = _run(nc, [arrays], core_ids=[0])
    got = r.results[0]["out_0"]
    return got.reshape(P, KD, T).transpose(2, 1, 0).reshape(1, T, D)
```

```python
import math
from contextlib import ExitStack

import numpy as np
import concourse.bass as bass
from concourse import mybir

F32 = mybir.dt.float32
F32R = mybir.dt.float32r
U8 = mybir.dt.uint8
ALU = mybir.AluOpType
ACT = mybir.ActivationFunctionType
AX = mybir.AxisListType.X
ds = bass.ds

P = 128
T = 256
TT = T // P
D = 1024
KD = D // P
DFF, MLP = 2816, 4096
KFF, KMLP = DFF // P, MLP // P
HEADS = 4
LAYERS = 2
PANEL = 2048
COLS = PANEL // KD
ROWK = PANEL // D
SLOTS = 4
UNROLL = 4
LEVELS = (64, 32, 16, 8, 4, 2, 1)
EPS = 1e-6
EPS2 = 1e-5
L1_EPS = 1e-6
TWO_PI_HI, TWO_PI_MID = 6.28125, 0.0019350051879882812
TWO_PI_LO = 2 * math.pi - TWO_PI_HI - TWO_PI_MID
ROUND = 1.5 * 2.0 ** 23
PI_SAFE = 3.1415925

N_MOD, N_WIN = 9 * D // COLS, 6144 // COLS
N_UP, N_DOWN, N_BR, N_OUT = DFF // P, DFF // (P * ROWK), 512 // (P * ROWK), D // (P * ROWK)
G_MOD = 0
G_UP1 = G_MOD + N_MOD
G_DOWN1 = G_UP1 + N_UP
G_WIN = G_DOWN1 + N_DOWN
G_PA = G_WIN + N_WIN
G_PB = G_PA + N_BR
G_OUT1 = G_PB + N_BR
G_UP2 = G_OUT1 + N_OUT
G_DOWN2 = G_UP2 + N_UP
G_LAYER = G_DOWN2 + N_DOWN
N_PROJ, N_MIN, N_MOUT = 30, MLP // COLS, MLP // (P * ROWK)
O_BR = N_PROJ
O_OUT = O_BR + 3 * N_BR
O_MIN = O_OUT + N_OUT
O_MOUT = O_MIN + N_MIN
PER_LAYER = O_MOUT + N_MOUT
PANELS = G_LAYER + LAYERS * PER_LAYER
DVE_LINKS, ACT_LINKS = 65, 8
R_DOWN1 = 0
R_PA = R_DOWN1 + N_DOWN
R_PB = R_PA + N_BR
R_OUT1 = R_PB + N_BR
R_DOWN2 = R_OUT1 + N_OUT
R_LAYER = R_DOWN2 + N_DOWN
RO_BR = 0
RO_OUT = RO_BR + 3 * N_BR
RO_MOUT = RO_OUT + N_OUT
R_PER_LAYER = RO_MOUT + N_MOUT
assert PER_LAYER % UNROLL == 0 and R_PER_LAYER % 2 == 0

def columns(*sizes):
    out, at = {}, 0
    for name, n in sizes:
        out[name] = (at, n)
        at += n
    return out, at

VEC1, NV1 = columns(("c", 2 * KD), ("mod_b", 72), ("logit0", 8), ("logit1", 8), ("a_norm", 1), ("conv_w", 36),
                    ("conv_b", 12), ("hy_bias", 8), ("final", 8), ("b1", 1), ("fr1", 1), ("b2", 1), ("fr2", 1))
VEC2, NV2 = columns(("attn_norm", 8), ("mlp_norm", 8), ("dq_norm", 1), ("dk_norm", 1), ("gq_norm", 1), ("gk_norm", 1),
                    ("subln", 1), ("ret_gain", 4), ("decay", 8), ("lam_q", 2), ("lam_k", 2), ("lam_init", 1),
                    ("one_less", 1))
MATS, NMATS = columns(("ident", P), ("block64", P), ("after", P), ("before", P), ("rot_part", P), ("rot_axial", P),
                      ("rot_ret", P), ("fold", 2))
TABS, NTABS = columns(("cos_part", T), ("sin_part", T), ("cos_axial", T), ("sin_axial", T), ("cos_ret", T),
                      ("sin_ret", T), ("ahead", TT * T), ("behind", TT * T))
HYC, NHYC = columns(("dft", TT * 512), ("dft_back", TT * 512), ("idft", 4 * T))


def shape_constants():
    f4 = np.float32
    p = np.arange(P)
    mats = {n: np.zeros((P, k), f4) for n, (_, k) in MATS.items()}
    mats["ident"][:] = np.eye(P)
    mats["fold"][0:4] = np.tile(np.eye(2), (2, 1))
    mats["block64"][:] = (p[:, None] // 64 == p[None] // 64)
    mats["after"][:] = p[:, None] > p[None]
    mats["before"][:] = p[:, None] < p[None]

    def rotation(m, base, half):
        for i in range(half):
            m[base + half + i, base + i] = -1
            m[base + i, base + half + i] = 1

    for b in (0, 64):
        rotation(mats["rot_part"], b, 8)
        rotation(mats["rot_axial"], b, 16)
        rotation(mats["rot_axial"], b + 32, 16)
    rotation(mats["rot_ret"], 0, 64)

    pos = np.arange(T, dtype=f4)
    def angles(pos, dim, theta):
        inv = f4(theta) ** (-np.arange(0, dim, 2, dtype=f4) / f4(dim))
        return (pos[:, None] * inv[None, :]).astype(f4)

    tabs = {n: np.zeros((P, k), f4) for n, (_, k) in TABS.items()}
    a = angles(pos, 16, 500000.0)
    tabs["cos_part"][:] = 1
    for b in (0, 64):
        for h in (0, 8):
            tabs["cos_part"][b + h:b + h + 8] = np.cos(a).T
            tabs["sin_part"][b + h:b + h + 8] = np.sin(a).T
    for off, q in ((0, np.repeat(np.arange(T // 64), 64)), (32, np.tile(np.arange(64), T // 64))):
        a = angles(q.astype(f4), 32, 10000.0)
        for b in (0, 64):
            for h in (0, 16):
                tabs["cos_axial"][b + off + h:b + off + h + 16] = np.cos(a).T
                tabs["sin_axial"][b + off + h:b + off + h + 16] = np.sin(a).T
    a = angles(pos, 128, 10000.0)
    for h in (0, 64):
        tabs["cos_ret"][h:h + 64] = np.cos(a).T
        tabs["sin_ret"][h:h + 64] = np.sin(a).T
    j = (np.arange(TT)[None, :, None] * P + p[:, None, None])
    i = np.arange(T)[None, None, :]
    tabs["ahead"][:] = np.maximum(i - j, 0).reshape(P, -1)
    tabs["behind"][:] = np.maximum(j - i, 0).reshape(P, -1)

    masks = np.zeros((P, 2 * len(LEVELS) + 1, P), f4)
    for n, h in enumerate(LEVELS):
        same = (p[:, None] // (2 * h)) == (p[None] // (2 * h))
        first = (p // h) % 2 == 0
        masks[:, n] = same & first[:, None] & ~first[None]
        masks[:, len(LEVELS) + n] = same & ~first[:, None] & first[None]
    masks[:, -1] = np.eye(P)

    quarter = D // 4
    omega = (1.0 / (f4(10000.0) ** (np.arange(quarter, dtype=f4) / f4(quarter)))).astype(f4)
    rows = T // 64
    ar = np.arange(rows, dtype=f4)[:, None] * omega
    ac = np.arange(64, dtype=f4)[:, None] * omega
    er = np.concatenate([np.sin(ar), np.cos(ar)], -1)
    ec = np.concatenate([np.sin(ac), np.cos(ac)], -1)
    half = KD // 2
    posemb = np.concatenate([er.T.reshape(half, P, rows).transpose(1, 0, 2).reshape(P, -1),
                             ec.T.reshape(half, P, 64).transpose(1, 0, 2).reshape(P, -1)], 1).astype(f4)

    n = 2 * T
    f = np.arange(T)
    def dft(t):
        w = 2 * np.pi * ((t[:, None] * f[None]) % n) / n
        im = -np.sin(w)
        im[:, 0] = np.cos(np.pi * t)
        return np.concatenate([np.cos(w), im], 1)
    t = np.arange(T)
    hyc = {}
    hyc["dft"] = dft(t).reshape(TT, P, n).transpose(1, 0, 2)
    hyc["dft_back"] = dft(n - 1 - t).reshape(TT, P, n).transpose(1, 0, 2)
    inv = dft(t).T * (2.0 / n)
    inv[0] /= 2
    inv[T] /= 2
    hyc["idft"] = inv.reshape(4, P, T).transpose(1, 0, 2)
    tt = (np.arange(T, dtype=f4) / f4(T - 1)).astype(f4)
    lo, hi = math.log(1e-2) / 1.5, math.log(1e-2) / 0.3
    deltas = np.abs(np.linspace(lo, hi, 512, dtype=f4))
    window = (np.exp(-tt[:, None] * deltas[None]) + f4(0.05)).astype(f4)
    window = window.reshape(TT, P, 512).transpose(1, 0, 2)
    w = (2.0 * math.pi * np.arange(T, dtype=f4) / T).astype(f4)
    bands = np.linspace(1e-4, 15, 16, dtype=f4)
    ang = (w[:, None] * bands[None]).astype(f4)
    z = np.concatenate([tt[:, None], np.cos(ang), -np.sin(ang)], -1).astype(f4)
    zT = np.zeros((P, T), f4)
    zT[:33] = z.T

    def flat(x):
        return np.ascontiguousarray(np.asarray(x, f4).reshape(P, -1))
    return {
        "mats": np.concatenate([mats[k] for k in MATS], 1),
        "tabs": np.concatenate([tabs[k] for k in TABS], 1),
        "masks": np.ascontiguousarray(masks.reshape(P, -1)),
        "posemb": np.ascontiguousarray(posemb),
        "hyc": np.concatenate([flat(hyc[k]) for k in HYC], 1),
        "window": flat(window),
        "zT": zT,
    }


def build(nc, stream, xT, ctxT, vec1, vec2, lbrow, hyw, mats, tabs, masks, posemb, hyc, window, zT, spectra, out):
    with ExitStack() as ctx:
        def sb(name, shape, dt=F32):
            return ctx.enter_context(nc.sbuf_tensor(name, shape, dt))

        def sem(name):
            return ctx.enter_context(nc.semaphore(name))

        landing = sb("landing", [P, SLOTS, PANEL])
        whi, wlo = (sb(n, [P, 2, PANEL], F32R) for n in ("whi", "wlo"))
        xhi, xlo = (sb(n, [P, KD, 2 * T], F32R) for n in ("xhi", "xlo"))
        ahi, alo = (x[:, 0:2 * ROWK].rearrange("p (r k) t -> p r k t", k=ROWK) for x in (xhi, xlo))
        h = sb("h", [P, KD, T])
        big = sb("big", [P, 50, T])
        bigf = big[:].rearrange("p c t -> p (c t)")
        v1 = sb("v1", [P, NV1])
        v2 = sb("v2", [P, NV2])
        v2all = sb("v2all", [P, LAYERS, NV2])
        cst = sb("cst", [P, 4 * (KD - 1) + P], F32R)
        mat = sb("mat", [P, NMATS])
        msk = sb("msk", [P, 2 * len(LEVELS) + 1, P], U8)
        ones = sb("ones", [P, P])
        mcol = sb("mcol", [P, 72, 2])
        scol = sb("scol", [P, 64])
        gains = sb("gains", [P, 8, KD])
        eps = sb("eps", [P, 2])
        rstd = sb("rstd", [P, 2, T])
        ws = sb("ws", [P, 10880])
        ps = ctx.enter_context(nc.psum_tensor("ps", [P, 8, 512], F32))

        def W(at, *shape):
            n = int(np.prod(shape))
            v = ws[:, at:at + n]
            if len(shape) == 2:
                v = v.rearrange("p (a b) -> p a b", b=shape[1])
            if len(shape) == 3:
                v = v.rearrange("p (a b c) -> p a b c", b=shape[1], c=shape[2])
            if len(shape) == 4:
                v = v.rearrange("p (a b c d) -> p a b c d", b=shape[1], c=shape[2], d=shape[3])
            return v

        def chunks(a, n):
            return big[:, a:a + n, :]

        def flatc(a, n):
            return bigf[:, a * T:(a + n) * T]

        def m1(name, i=0, n=1):
            a = VEC1[name][0] + i
            return v1[:, a:a + n]

        def m2(name, i=0, n=1):
            a = VEC2[name][0] + i
            return v2[:, a:a + n]

        def mt(name):
            a = MATS[name][0]
            return mat[:, a:a + P]

        ident = mt("ident")

        hc = W(0, KD, T)
        POS = (KD // 2) * (T // 64 + 64)
        pos_row = W(2048, KD // 2, T // 64)
        pos_col = W(2048 + (KD // 2) * (T // 64), KD // 2, 64)
        mrow = W(4096, UNROLL, COLS)
        mask_in = W(6144, (2 * len(LEVELS) + 1) * P)
        Vx = W(0, TT, 512)
        Vc = W(1024, TT, 512)
        sc = [W(2048, TT, 512), W(3072, TT, 512)]
        lrow = W(4096, 2, 1024)
        lgc = W(6144, TT, 512)
        XC = [W(1024, HEADS * TT, P + 1), W(2056, HEADS * TT, P + 1)]
        S = W(3088, TT, HEADS, T)
        EM = [W(7168, HEADS * TT, P), W(8192, HEADS * TT, P)]
        EMf = [W(7168, HEADS * TT * P), W(8192, HEADS * TT * P)]
        Q0, KF, G0, HY, MG = 0, (4, 8), 12, 16, 28
        s0 = [bigf[:, 44 * T + d * 512:44 * T + (d + 1) * 512].rearrange("p (a b) -> p a b", b=P) for d in range(2)]
        FILT = 5120
        fdft = W(FILT, 2, TT, 512)
        hwindow = W(FILT + 2048, TT, 512)
        zfeat = W(FILT + 3072, T)
        h2 = W(FILT + 3072 + T, T)
        hyin = W(FILT + 3072 + 2 * T, 2176)
        hw1, hw2, hw3 = hyin[0:33, 0:64], hyin[0:64, 64:128], hyin[0:64, 128:2176]
        kern = bigf[:, 6144:8192].rearrange("p (u d c) -> p u d c", u=TT, d=2)
        absk = bigf[:, 8192:10240]
        Kst = bigf[:, 10240:12288].rearrange("p (m c) -> p m c", c=512)
        l1 = bigf[:, 12288:12800]
        ang = bigf[:, 12288:12800].rearrange("p (a b) -> p a b", b=T)
        F_MLP, F_ORDER, F_STEPS = 3, 7, 13
        idft = W(6144, 4, T)
        Kf = W(1024, 2, 4, 512)
        dft = W(9216, TT, 512)
        ZC = (4, 8, 16)
        uT = W(5120, TT, 512)
        ptmp = uT
        Pi = W(0, 2, 512)
        Pf = bigf[:, 44 * T:48 * T].rearrange("p (a b) -> p a b", b=512)
        DQ, DK, GQ, GK, RQ, RK, RG, GT = 0, 4, 8, 12, 14, 18, 22, 26
        tab = W(0, NTABS)
        def tb(name):
            a, n = TABS[name]
            return ws[:, a:a + n]
        VD = W(NTABS, TT, 512)
        VR = W(NTABS + 1024, TT, 512)
        VG = W(NTABS + 2048, TT, P)
        tmpA = NTABS + 2304
        nsq = W(tmpA, 4, T)
        nrs = W(tmpA + 1024, 4, T)
        nrot = W(tmpA + 2048, 4, T)
        ew = [W(tmpA, 2, T), W(tmpA + 512, 2, T)]
        wT = [W(tmpA + 3072, 2, TT, T), W(tmpA + 4096, 2, TT, T)]
        rtmp = [W(tmpA, 2 * T), W(tmpA + 512, 2 * T)]
        ROPES = ((DQ, 4, "dq_norm", "rot_part", "cos_part", "sin_part"), (DK, 4, "dk_norm", "rot_part", "cos_part", "sin_part"),
                 (GQ, 4, "gq_norm", "rot_axial", "cos_axial", "sin_axial"),
                 (GK, 2, "gk_norm", "rot_axial", "cos_axial", "sin_axial"),
                 (RQ, 4, None, "rot_ret", "cos_ret", "sin_ret"), (RK, 4, None, "rot_ret", "cos_ret", "sin_ret"))

        def hid_chunk(i, t):
            w = t // T
            return big[:, ds(i * w, w), :].rearrange("p c t -> p (c t)")

        def hid_src(t):
            if t == T:
                return lambda i: big[:, ds(i * ROWK, ROWK), :]
            return lambda i: big[:, ds(i * (2 * ROWK), 2 * ROWK), :].rearrange("p (k b) t -> p k (b t)", b=2)

        def chunk_src(c0):
            return lambda i: big[:, ds(i * ROWK + c0, ROWK), :]

        def halves(x, hh):
            b = x.rearrange("p (n u s) -> p n u s", u=2, s=hh)
            return b[:, :, 0], b[:, :, 1]

        NL = len(LEVELS) + 1
        levels = [(d, n) for d in range(2) for n in range(NL)] + [(2, 0)]
        smx = sb("smx", [P, 4, 8])
        Dm = [W(tmpA + 1024, TT, T), W(tmpA + 1536, TT, T)]
        sD = [W(tmpA + 2048, TT, T), W(tmpA + 2560, TT, T)]
        PLAIN = (DQ, DQ + 2, DK, DK + 2, GQ, GQ + 2, GK, RQ, RQ + 2, RK, RK + 2, RG, RG + 2) + tuple(range(GT, GT + 24, 2))
        N_VALUES, N_HEADS = 5, 18
        N_FIRST = 8
        beside_level = {2 * j: i for j, i in enumerate(range(N_FIRST + 7, N_WIN - 2))}
        SUM_AFTER = {7: 0, 9: 1, 11: 2, 12: 3}
        ROT_AFTER = {8: (0, 0), 10: (1, 0), 12: (2, 0), 13: (3, 0), 14: (4, 14), 16: (5, 16)}
        SQUARE_AFTER = {6: 0, 8: 1, 10: 2, 11: 3}
        RMS_AFTER = SUM_AFTER
        SCALE_IN = {8: 0, 10: 1, 12: 2, 13: 3}
        ROPE_IN = {9: 0, 11: 1, 13: 2, 14: 3, 15: 4, 17: 5}
        PAIRS = 16
        BRANCHES = ((GQ, 16), (DQ, 0), (RQ, 8))

        per = {}
        def lsem(name, n=0):
            s = sem(name)
            per[name] = n
            return s

        landed = [sem(f"landed{i}") for i in range(SLOTS)]
        hi_done = sem("hi_done")
        hi_act = sem("hi_act")
        lo_done = sem("lo_done")
        panel_used = sem("panel_used")
        act_hi = sem("act_hi")
        act_lo = sem("act_lo")
        vec_in = sem("vec_in")
        small_in = sem("small_in")
        mask_landed, mask_set = sem("mask_landed"), sem("mask_set")
        x_in = sem("x_in")
        lb_in = sem("lb_in")
        dft_in = sem("dft_in")
        idft_in = sem("idft_in")
        kf_in = [sem("kf0_in"), sem("kf1_in")]
        kf_out = sem("kf_out")
        hy_in = sem("hy_in")
        tab_in = sem("tab_in")
        v2_in = lsem("v2_in", 1)
        out_done = sem("out_done")
        const_set = sem("const_set")
        dve_chain, act_chain = sem("dve_chain"), sem("act_chain")
        dve_link = lsem("dve_link", DVE_LINKS)
        act_link = lsem("act_link", ACT_LINKS)
        c_silu, c_split, c_zero = sem("c_silu"), sem("c_split"), sem("c_zero")
        mod_copied, mod_turned, mod_added = sem("mod_copied"), sem("mod_turned"), sem("mod_added")
        cols_set = sem("cols_set")
        h_set = sem("h_set")
        sums_out = lsem("sums_out", 9)
        sq_done, sum_done, rstd_done = lsem("sq_done", 8), lsem("sum_done", 2), lsem("rstd_done", 2)
        norm_scaled, norm_hi, norm_lo = lsem("norm_scaled", 16), lsem("norm_hi", 16), lsem("norm_lo", 16)
        x_free = lsem("x_free", 1)
        silu_done, hid_done = sem("silu_done"), sem("hid_done")
        res_done = lsem("res_done", 4)
        xc_done = sem("xc_done")
        win_out = sem("win_out")
        lb_diff, lb_sig, lb_set = sem("lb_diff"), sem("lb_sig"), sem("lb_set")
        cf_done, cln_done, ck_done, csum_done, cdec_done, ckey_done, cst_done, cst_out = (
            sem(n) for n in ("cf_done", "cln_done", "ck_done", "csum_done", "cdec_done", "ckey_done", "cst_done",
                             "cst_out"))
        xf_done, xln_done = sem("xf_done"), sem("xln_done")
        lv_diff, lv_exp, lv_mul, lv_score, lv_sel = (sem("lv_" + n) for n in ("diff", "exp", "mul", "score", "sel"))
        qe_diff, qe_exp, qe_done, o_done, osq_done, osum_done, orstd_done, oa_done = (
            sem(n) for n in ("qe_diff", "qe_exp", "qe_done", "o_done", "osq_done", "osum_done", "orstd_done", "oa_done"))
        conv_done, fl_mm, fl_arg, fl_sin, h3_mm, win_mul, abs_done, l1_mm, kf_mm, kf_done = (
            sem(n) for n in ("conv_done", "fl_mm", "fl_arg", "fl_sin", "h3_mm", "win_mul", "abs_done", "l1_mm", "kf_mm",
                             "kf_done"))
        turn_done, uT_done, uf_mm, pf_done, y_mm, z_done = (
            sem(n) for n in ("turn_done", "uT_done", "uf_mm", "pf_done", "y_mm", "z_done"))
        gate_done = lsem("gate_done", 6)
        gate1_done = sem("gate1_done")
        gate1_on = sem("gate1_on")
        gate_on = lsem("gate_on", 4)
        proj_out = lsem("proj_out", N_PROJ)
        lam_mul, lam_mm, lam_exp, lam_set = (lsem("lam_" + n, 1) for n in ("mul", "mm", "exp", "set"))
        rp_sq, rp_sum, rp_rs = (lsem("rp_" + n, 4) for n in ("sq", "sum", "rs"))
        rp_n, rp_rot, rp_done = lsem("rp_n", 4), lsem("rp_rot", 6), lsem("rp_done", 6)
        sc_mm, sc_max, sc_exp, sc_w, sc_turn, sc_wT = (lsem("sc_" + n, 16) for n in ("mm", "max", "exp", "w", "turn", "wT"))
        pv_mm, pv_out = lsem("pv_mm", 8), lsem("pv_out", 8)
        rt_arg, rt_dec, rt_mm, rt_mul, rt_pv, rt_out = (lsem("rt_" + n, 4) for n in ("arg", "dec", "mm", "mul", "pv", "out"))
        sub_sq, sub_sum, sub_rs, sub_done = (lsem("sub_" + n, 1) for n in ("sq", "sum", "rs", "done"))
        gn_mean, gn_cen, gn_sq, gn_sum, gn_rs, gn_done = (
            lsem("gn_" + n, 1) for n in ("mean", "cen", "sq", "sum", "rs", "done"))
        relu_done, m_done = lsem("relu_done", N_MIN), lsem("m_done", N_MIN)
        layer_done = lsem("layer_done", 4)

        def following(s, l, c, base=0):
            return at(s, l, c + per[s.name], base)

        def at(s, l, c, base=0):
            return l * per[s.name] + (base + c)

        def panel_loop(eng, first, count, body):
            phase = first[1] if isinstance(first, tuple) else first
            g0 = first[0] if isinstance(first, tuple) else first
            if count >= 2 * UNROLL:
                with eng.Fori(0, count // UNROLL) as i:
                    for j in range(UNROLL):
                        body(i * UNROLL + j, g0 + (i * UNROLL + j), (phase + j) % UNROLL)
            else:
                for j in range(count - count % UNROLL):
                    body(j, g0 + j, (phase + j) % UNROLL)
            for j in range(count - count % UNROLL, count):
                body(j, g0 + j, (phase + j) % UNROLL)

        def layer_panel(l, off):
            return (l * PER_LAYER + (G_LAYER + off), G_LAYER + off)

        block = ctx.enter_context(nc.Block())

        @block.sync
        def _(sp):
            sp.dma_start(v1[:], vec1).then_inc(vec_in, 16)
            for g in range(SLOTS):
                sp.dma_start(landing[:, g], stream[g]).then_inc(landed[g], 16)

            def load(g, s):
                sp.wait_ge(lo_done, g - (SLOTS - 1))
                sp.dma_start(landing[:, s], stream[ds(g, 1)].rearrange("a p n -> p (a n)")).then_inc(landed[s], 16)

            with sp.Fori(1, PANELS // UNROLL) as i:
                for j in range(UNROLL):
                    load(i * UNROLL + j, j)
            for g in range(PANELS - PANELS % UNROLL, PANELS):
                load(g, g % SLOTS)
            sp.wait_ge(layer_done, 4 * (1 + LAYERS))
            sp.dma_start(out, h[:].rearrange("p k t -> p (k t)")).then_inc(out_done, 16)
            sp.wait_ge(out_done, 16)

        @block.gpsimd
        def _(pool):
            pool.wait_ge(const_set, 3)

            def high(g, s, turn, n=PANEL):
                pool.wait_ge(landed[s], (turn + 1) * 16)
                if not isinstance(g, int) or g >= 2:
                    pool.wait_ge(panel_used, g - 1)
                hi, panel = whi[:, s % 2], landing[:, s]
                pool.tensor_tensor(hi[:, 0:P], panel[:, 0:P], ones[:], ALU.mult)
                pool.tensor_scalar(hi[:, P:n], panel[:, P:n], 1.0, 0.0, ALU.mult, ALU.add).then_inc(hi_done, 1)

            for g in range(UNROLL):
                high(g, g, 0, PANEL // 2)
            with pool.Fori(1, N_MOD // UNROLL) as i:
                for j in range(UNROLL):
                    high(i * UNROLL + j, j, i, PANEL // 2)
            def diff(m):
                d, n = levels[m]
                if m < 2:
                    pool.wait_ge(xc_done, m + 1)
                em = EM[m % 2]
                if m >= 2:
                    pool.wait_ge(lv_score, m - 1)
                if d == 2:
                    pool.tensor_tensor(em, chunks(KF[0], 4).rearrange("p c (u s) -> p (c u) s", s=P),
                                    chunks(KF[1], 4).rearrange("p c (u s) -> p (c u) s", s=P), ALU.add
                                    ).then_inc(lv_diff, 1)
                    return
                o = 1 - d
                if n < len(LEVELS):
                    hh = LEVELS[n]
                    x = XC[d][:, :, o:o + P].rearrange("p n (b s) -> p n b s", s=2 * hh)
                    mid = XC[d][:, :, 0:P].rearrange("p n (b s) -> p n b s", s=2 * hh)[:, :, :, hh:hh + 1]
                    mid = mid.to_broadcast([P, HEADS * TT, P // (2 * hh), 2 * hh])
                    pool.tensor_tensor(em.rearrange("p n (b s) -> p n b s", s=2 * hh), x, mid, ALU.subtract
                                    ).then_inc(lv_diff, 1)
                else:
                    x = XC[d][:].rearrange("p (g u) s -> p g u s", u=TT)
                    tot = x[:, :, 0, P:P + 1].to_broadcast([P, HEADS, P])
                    pool.tensor_tensor(em.rearrange("p (g u) s -> p g u s", u=TT)[:, :, 0], tot, x[:, :, 0, o:o + P],
                                    ALU.subtract).then_inc(lv_diff, 1)
            begin, end = G_WIN + N_FIRST + 8, G_PA + 1
            whole = begin // UNROLL
            with pool.Fori(N_MOD // UNROLL, whole) as i:
                for j in range(UNROLL):
                    high(i * UNROLL + j, j, i)
            for g in range(whole * UNROLL, begin):
                high(g, g % SLOTS, g // SLOTS)
            diff(0)
            for j, g in enumerate(range(begin, end)):
                high(g, g % SLOTS, g // SLOTS)
                for m in (2 * j + 1, 2 * j + 2):
                    if m < len(levels):
                        diff(m)
            whole = -(-end // UNROLL)
            for g in range(end, whole * UNROLL):
                high(g, g % SLOTS, g // SLOTS)
            with pool.Fori(whole, PANELS // UNROLL) as i:
                for j in range(UNROLL):
                    high(i * UNROLL + j, j, i)
            for g in range(PANELS - PANELS % UNROLL, PANELS):
                high(g, g % SLOTS, g // SLOTS)

        @block.vector
        def _(dve):
            v = nc.vector
            count = [0]
            link = [0, 0]

            def step(ins):
                count[0] += 1
                ins.then_inc(dve_chain, 1)
                dve.wait_ge(dve_chain, count[0])

            def lstep(ins):
                link[1] += 1
                ins.then_inc(dve_link, 1)
                dve.wait_ge(dve_link, at(dve_link, link[0], link[1]))

            def low(g, s, halved=False):
                dve.wait_ge(hi_done, g + 1)
                if halved:
                    dve.wait_ge(hi_act, g + 1)
                if not isinstance(g, int) or g >= 2:
                    dve.wait_ge(panel_used, g - 1)
                v.tensor_tensor(wlo[:, s % 2], landing[:, s], whi[:, s % 2].bitcast(F32), ALU.subtract
                                ).then_inc(lo_done, 1)

            def low_stage(first, n, last=True):
                panel_loop(dve, first, n if last else n - 1, lambda i, g, s: low(g + 1, (s + 1) % SLOTS))

            def part_low(src, r, r_phase, t):
                dve.wait_ge(act_hi, r + 1)
                v.tensor_tensor(alo[:, r_phase % 2, :, 0:t], src, ahi[:, r_phase % 2, :, 0:t].bitcast(F32),
                                ALU.subtract).then_inc(act_lo, 1)

            def row_stage(first, n, src, r0, r_phase, t, last=True, begun=False):
                if not begun:
                    part_low(src(0), r0, r_phase, t)

                g0, phase = first if isinstance(first, tuple) else (first, first)

                def body(i, g, s):
                    low(g + 1, (s + 1) % SLOTS)
                    part_low(src(i + 1), r0 + (i + 1), r_phase + (s - phase) % UNROLL + 1, t)
                panel_loop(dve, first, n - 1, body)
                if last:
                    low(g0 + n, (phase + n) % SLOTS)
                return g0 + n

            def norm_step(k, n, src, gain, shift, dst0, l=None):
                val = (lambda c: at(norm_hi, l, c, base=5 * KD)) if l is not None else (lambda c: c)
                tmp = bigf[:, 4096:4096 + KD * T].rearrange("p (k t) -> p k t", t=T)
                if k == 0:
                    dve.wait_ge(rstd_done, n + 1 if l is None else at(rstd_done, l, n + 1, base=6))
                if k < KD:
                    v.scalar_tensor_tensor(tmp[:, k], src[:, k], gain(k), rstd[:, n % 2], ALU.mult, ALU.mult
                                           ).then_inc(norm_scaled, 1)
                if k >= 1:
                    j = k - 1
                    dve.wait_ge(norm_hi, val(n * KD + k))
                    hi = xhi[:, j, dst0:dst0 + T].bitcast(F32)
                    lo = xlo[:, j, dst0:dst0 + T]
                    if shift is None:
                        v.tensor_tensor(lo, tmp[:, j], hi, ALU.subtract).then_inc(norm_lo, 1)
                    else:
                        v.scalar_tensor_tensor(lo, tmp[:, j], shift(j), hi, ALU.add, ALU.subtract).then_inc(norm_lo, 1)

            def norm(*args):
                for k in range(KD + 1):
                    norm_step(k, *args)

            def residual(out0, end, add):
                for b in range(4):
                    if b < 3:
                        dve.wait_ge(sums_out, out0 + (b + 1))
                    else:
                        dve.wait_ge(panel_used, end)
                    add(b)

            v.memset(ones[:], 1.0).then_inc(const_set, 1)
            v.memset(eps[:, 0:1], EPS).then_inc(const_set, 1)
            v.memset(eps[:, 1:2], EPS2).then_inc(const_set, 1)
            v.memset(mcol[:], 0.0).then_inc(mod_added, 1)
            v.memset(cst[:].bitcast(F32), 0.0).then_inc(c_zero, 1)
            dve.wait_ge(c_silu, 2)
            cs = scol[:, 0:2 * KD].rearrange("p (k b) -> p k b", b=2)
            cparts = cst[:, 0:4 * KD].rearrange("p (k b) -> p k b", b=4)
            v.tensor_tensor(cparts[:, :, 2:4], cs, cparts[:, :, 0:2].bitcast(F32), ALU.subtract).then_inc(c_split, 1)

            def gcol(n):
                return lambda k: gains[:, n, k:k + 1]

            def mcolumn(n, who):
                return lambda k: mcol[:, 8 * n + k, who:who + 1]

            def mod(n, who):
                return mcol[:, 8 * n:8 * n + 8, who]

            def sine_argument(n):
                b, f = (("b1", "fr1"), ("b2", "fr2"))[n]
                x, k = ang[0:64, 0], ang[0:64, 1]
                dve.wait_ge(fl_mm, n + 1)
                step(v.tensor_scalar(x, ps[0:64, 5, 0:T], m1(b)[0:64], m1(f)[0:64], ALU.add, ALU.mult))
                step(v.tensor_scalar(k, x, 1 / (2 * math.pi), ROUND, ALU.mult, ALU.add))
                step(v.tensor_scalar(k, k, ROUND, None, ALU.subtract))
                for part in (TWO_PI_HI, TWO_PI_MID, TWO_PI_LO):
                    step(v.scalar_tensor_tensor(x, k, -part, x, ALU.mult, ALU.add))
                v.tensor_scalar(x, x, PI_SAFE, -PI_SAFE, ALU.min, ALU.max).then_inc(fl_arg, 1)

            def windowed(o, u):
                dve.wait_ge(h3_mm, 2 * o + u + 1)
                for d in range(2):
                    last = v.tensor_tensor(kern[:, u, d], ps[:, 6 + d], hwindow[:, u], ALU.mult)
                last.then_inc(win_mul, 1)

            def inverse_norm(o):
                dve.wait_ge(l1_mm, o + 1)
                step(v.tensor_scalar(l1, ps[:, 5], L1_EPS, None, ALU.add))
                step(v.reciprocal(l1, l1))

            def normed_spectrum(o, m):
                dve.wait_ge(kf_mm, 4 * o + m + 1)
                if o and m == 0:
                    dve.wait_ge(kf_out, 16)
                v.tensor_tensor(Kst[:, m], ps[:, 6 + m % 2], l1, ALU.mult).then_inc(kf_done, 1)

            def filter_step(q):
                if q in (F_MLP + 1, F_MLP + 3):
                    sine_argument((q - F_MLP) // 2)
                for o in range(2):
                    t = q - F_ORDER - o * F_STEPS
                    if t in (1, 2):
                        windowed(o, t - 1)
                    if t == 4:
                        inverse_norm(o)
                    if t in (6, 8, 10, 12):
                        normed_spectrum(o, t // 2 - 3)

            def mod_group(i, beside=lambda j: None):
                for j in range(UNROLL):
                    low(i * UNROLL + j + 1, (j + 1) % SLOTS, i * UNROLL + j + 1 < N_MOD)
                    beside(j)
                    filter_step(i * UNROLL + j)
                dve.wait_ge(mod_turned, i * UNROLL + UNROLL)
                v.tensor_tensor(mcol[:, ds(i * 8, 8), :], ps[:, 4, 0:16].rearrange("p (c b) -> p c b", b=2),
                                m1("mod_b", 0, 72)[:, ds(i * 8, 8)].unsqueeze(2).to_broadcast([P, 8, 2]), ALU.add
                                ).then_inc(mod_added, 1)
            low(0, 0, True)
            for i in range(3):
                mod_group(i)
            dve.wait_ge(x_in, 48)
            for b in range(4):
                for k in (2 * b, 2 * b + 1):
                    grid = h[:, k].rearrange("p (r c) -> p r c", c=64)
                    add = pos_row[:, k].unsqueeze(2) if k < KD // 2 else pos_col[:, k - KD // 2].unsqueeze(1)
                    last = v.tensor_tensor(grid, grid, add.to_broadcast([P, T // 64, 64]), ALU.add)
                last.then_inc(h_set, 1)
            dve.wait_ge(mod_added, 1 + 2)
            for n, (m, who) in enumerate(((1, 0), (1, 1))):
                v.tensor_scalar(gains[:, n], mod(m, who), 1.0, None, ALU.add).then_inc(cols_set, 1)
            mod_group(3)
            dve.wait_ge(cols_set, 2)
            for n, src, g0 in ((0, h, 4), (1, hc, 6)):
                for half in range(2):
                    def beside(j):
                        norm_step(4 * half + j, n, src, gcol(n), mcolumn(0, n), n * T)
                        if half and j == 3:
                            norm_step(KD, n, src, gcol(n), mcolumn(0, n), n * T)
                    mod_group(g0 + half, beside)
            mod_group(8)
            dve.wait_ge(mod_added, 1 + N_MOD // UNROLL)
            for n, (m, who) in ((2, (4, 0)), (3, (4, 1)), (4, (7, 0))):
                v.tensor_scalar(gains[:, n], mod(m, who), 1.0, None, ALU.add).then_inc(cols_set, 1)
            for n, (m, who) in enumerate(((2, 0), (2, 1), (8, 0))):
                v.tensor_scalar(gains[:, 5 + n], mod(m, who), 0.5, None, ALU.mult).then_inc(cols_set, 1)
            dve.wait_ge(cols_set, 8)

            def up_stage(g0, which, t, last=True):
                def body(i, g, s):
                    low(g + 1, (s + 1) % SLOTS)
                    if isinstance(i, int) and i == N_UP - 1:
                        r0 = (R_DOWN1, R_DOWN2)[which]
                        part_low(hid_src(t)(0), r0, r0, t)
                    dve.wait_ge(silu_done, which * KFF + i + 1)
                    hid = hid_chunk(i, t)
                    bank = 2 * ((s - g0) % UNROLL) + 1
                    v.tensor_tensor(hid, hid, ps[:, bank, 0:t], ALU.mult).then_inc(hid_done, 1)
                panel_loop(dve, g0, N_UP, body)

            up_stage(G_UP1, 0, 2 * T)
            dve.wait_ge(hid_done, KFF)
            row_stage(G_DOWN1, N_DOWN, hid_src(2 * T), R_DOWN1, R_DOWN1, 2 * T, begun=True)

            def down1(b):
                for k in (2 * b, 2 * b + 1):
                    v.scalar_tensor_tensor(h[:, k], ps[:, k, 0:T], gains[:, 5, k:k + 1], h[:, k], ALU.mult, ALU.add)
                    last = v.scalar_tensor_tensor(hc[:, k], ps[:, k, T:2 * T], gains[:, 6, k:k + 1], hc[:, k], ALU.mult,
                                                  ALU.add)
                last.then_inc(h_set, 1)
            residual(0, G_DOWN1 + N_DOWN, down1)
            norm(2, h, gcol(2), mcolumn(3, 0), 0)
            norm(3, hc, gcol(3), mcolumn(3, 1), T)

            low_stage(G_WIN, N_FIRST)

            def win(i):
                low(G_WIN + i + 1, (G_WIN + i + 1) % SLOTS)

            dve.wait_ge(norm_lo, 4 * KD)
            dve.wait_ge(mask_landed, 16)
            v.tensor_copy(msk[:].rearrange("p n s -> p (n s)"), mask_in).then_inc(mask_set, 1)
            dve.wait_ge(mask_set, 1)
            dve.wait_ge(lb_in, 16)
            v.tensor_tensor(scol[:, 16:24], m1("logit0", 0, 8), m1("logit1", 0, 8), ALU.subtract).then_inc(lb_diff, 1)
            v.tensor_tensor(lrow[:, 0], lrow[:, 0], lrow[:, 1], ALU.subtract).then_inc(lb_diff, 1)
            dve.wait_ge(lb_sig, 2)
            v.tensor_scalar(scol[:, 24:32], scol[:, 16:24], -1.0, 1.0, ALU.mult, ALU.add).then_inc(lb_set, 1)
            v.tensor_scalar(lrow[:, 1], lrow[:, 0], -1.0, 1.0, ALU.mult, ALU.add).then_inc(lb_set, 1)
            dve.wait_ge(lb_set, 2)

            dve.wait_ge(win_out, 6)
            for d in range(2):
                def row(n):
                    return lrow[:, n, 512 * d:512 * d + 512].unsqueeze(1).to_broadcast([P, TT, 512])
                step(v.tensor_tensor(sc[d], sc[d], row(1), ALU.mult))
                v.tensor_tensor(sc[d], sc[d], row(0), ALU.add).then_inc(cf_done, 1)
                win(N_FIRST + 2 * d)
                dve.wait_ge(cln_done, d + 1)
                v.tensor_scalar(sc[d], sc[d], -1.0, 1.0, ALU.mult, ALU.add).then_inc(ck_done, 1)
                win(N_FIRST + 2 * d + 1)
                dve.wait_ge(ck_done, d + 1)
                dve.wait_ge(cdec_done, d + 1)
                v.tensor_tensor(sc[d], sc[d], lgc, ALU.mult).then_inc(ckey_done, 1)

            for d in range(2):
                for c in range(HEADS):
                    n = 4 * d + c
                    last = v.tensor_scalar(big[:, KF[d] + c], big[:, KF[d] + c], scol[:, 24 + n:25 + n],
                                           scol[:, 16 + n:17 + n], ALU.mult, ALU.add)
                last.then_inc(xf_done, 1)
            win(N_FIRST + 4)
            dve.wait_ge(cst_out, 2)
            for d in range(2):
                last = v.memset(XC[d][:, :, 0:1], 0.0)
            step(last)
            for d in range(2):
                dve.wait_ge(xln_done, d + 1)
                v.tensor_scalar(flatc(KF[d], 4), flatc(KF[d], 4), -1.0, 1.0, ALU.mult, ALU.add)
                for n in range(HEADS * TT):
                    last = v.tensor_tensor_scan(XC[d][:, n, 1:P + 1], ones[:], EM[d][:, n], 0.0, ALU.mult, ALU.add)
                last.then_inc(xc_done, 1)
                win(N_FIRST + 5 + d)

            def q_of(c0):
                return flatc(c0, 4)
            def mul(m):
                d, n = levels[m]
                if d == 2:
                    return
                hh = (LEVELS + (P,))[n]
                dve.wait_ge(lv_exp, m + 1)
                e = halves(EMf[m % 2], hh)
                q, kk = halves(q_of(Q0), hh), halves(q_of(KF[d]), hh)
                a = (kk, q) if d == 0 else (q, kk)
                v.tensor_tensor(e[0], e[0], a[0][0], ALU.mult)
                v.tensor_tensor(e[1], e[1], a[1][1], ALU.mult).then_inc(lv_mul, 1)

            def select(m):
                d, n = levels[m]
                dve.wait_ge(lv_score, m + 1)
                if m:
                    dve.wait_ge(lv_sel, m)
                if d == 2 or n < len(LEVELS):
                    mk = msk[:, 2 * len(LEVELS) if d == 2 else d * len(LEVELS) + n].unsqueeze(1)
                    for u in range(TT):
                        last = v.copy_predicated(S[:, u, :, u * P:(u + 1) * P], mk.to_broadcast([P, HEADS, P]),
                                                 ps[:, 2 * (m % 2) + u].rearrange("p (g s) -> p g s", s=P))
                else:
                    last = v.tensor_copy(S[:, d, :, (1 - d) * P:(2 - d) * P],
                                         ps[:, 2 * (m % 2)].rearrange("p (g s) -> p g s", s=P))
                last.then_inc(lv_sel, 1)

            step(v.memset(S.rearrange("p u g t -> p (u g t)"), 0.0))
            for m in range(len(levels)):
                mul(m)
                if m >= 1:
                    select(m - 1)
                if m in beside_level:
                    win(beside_level[m])
            select(len(levels) - 1)
            dve.wait_ge(lv_score, len(levels))
            xs = [XC[d][:].rearrange("p (g u) s -> p g u s", u=TT) for d in range(2)]
            es = [EM[d].rearrange("p (g u) s -> p g u s", u=TT) for d in range(2)]
            def total(d, u):
                return xs[d][:, :, u, P:P + 1].to_broadcast([P, HEADS, P])
            v.tensor_copy(es[0][:, :, 0], xs[0][:, :, 0, 1:P + 1])
            v.tensor_tensor(es[0][:, :, 1], total(0, 0), xs[0][:, :, 1, 1:P + 1], ALU.add).then_inc(qe_diff, 1)
            v.tensor_tensor(es[1][:, :, 1], total(1, 1), xs[1][:, :, 1, 0:P], ALU.subtract)
            step(v.tensor_tensor(es[1][:, :, 0], total(1, 0), xs[1][:, :, 0, 0:P], ALU.subtract))
            v.tensor_tensor(es[1][:, :, 0], total(1, 1), es[1][:, :, 0], ALU.add).then_inc(qe_diff, 1)
            for d in range(2):
                dve.wait_ge(qe_exp, d + 1)
                last = v.tensor_tensor(EMf[d], EMf[d], q_of(Q0), ALU.mult)
            last.then_inc(qe_done, 1)
            win(N_WIN - 2)
            def convolve(c0, c1):
                for c in range(c0, c1):
                    src = big[:, HY + c]
                    dst = big[:, ZC[c // 4] + c % 4]
                    step(v.tensor_scalar(dst, src, m1("conv_w", 12 + c), m1("conv_b", c), ALU.mult, ALU.add))
                    step(v.scalar_tensor_tensor(dst[:, 1:T], src[:, 0:T - 1], m1("conv_w", c), dst[:, 1:T], ALU.mult, ALU.add))
                    last = v.scalar_tensor_tensor(dst[:, 0:T - 1], src[:, 1:T], m1("conv_w", 24 + c), dst[:, 0:T - 1],
                                                  ALU.mult, ALU.add)
                last.then_inc(conv_done, 1)
            dve.wait_ge(win_out, N_WIN - 2)
            convolve(0, 4)
            convolve(4, 8)
            dve.wait_ge(orstd_done, 1)
            for b in range(2):
                step(v.scalar_tensor_tensor(flatc(Q0 + 2 * b, 2), ps[:, 4 + b], m1("a_norm"),
                                            EMf[1][:, b * 512:(b + 1) * 512], ALU.mult, ALU.mult))
            dve.wait_ge(gate1_on, 1)
            v.tensor_tensor(flatc(Q0, 4), flatc(Q0, 4), flatc(G0, 4), ALU.mult).then_inc(oa_done, 1)

            for o in range(2):
                dve.wait_ge(uf_mm, o + 1)
                dve.wait_ge(oa_done, 1)
                dve.wait_ge(kf_in[o], 16)
                ur, ui = ps[:, 0:2], ps[:, 2:4]
                kr, ki = Kf[:, o, 0:2], Kf[:, o, 2:4]
                v.tensor_tensor(Pf, ur, kr, ALU.mult)
                step(v.tensor_tensor(ptmp, ui, ki, ALU.mult))
                step(v.tensor_tensor(Pf, Pf, ptmp, ALU.subtract))
                v.tensor_tensor(Pf[0:1, 0], ur[0:1, 0], kr[0:1, 0], ALU.mult).then_inc(pf_done, 1)
                v.tensor_tensor(Pi, ur, ki, ALU.mult)
                step(v.tensor_tensor(ptmp, ui, kr, ALU.mult))
                step(v.tensor_tensor(Pi, Pi, ptmp, ALU.add))
                v.tensor_tensor(Pi[0:1, 0], ui[0:1, 0], ki[0:1, 0], ALU.mult).then_inc(pf_done, 1)
                if o == 1:
                    part_low(chunk_src(Q0)(0), R_PA, R_PA, T)
                    low(G_PA + 1, (G_PA + 1) % SLOTS)
                    part_low(chunk_src(Q0)(1), R_PA + 1, R_PA + 1, T)
                dve.wait_ge(y_mm, o + 1)
                for c in range(4):
                    z, g = big[:, ZC[0] + c], big[:, ZC[1 + o] + c]
                    step(v.scalar_tensor_tensor(z, z, m1("hy_bias", 4 * o + c), ps[:, 6 + c // 2, (c % 2) * T:(c % 2 + 1) * T],
                                                ALU.mult, ALU.add))
                    last = v.tensor_tensor(z, z, g, ALU.mult)
                last.then_inc(z_done, 1)
                if o == 0:
                    win(N_WIN - 1)
                    convolve(8, 12)
                    dve.wait_ge(conv_done, 3)

            dve.wait_ge(z_done, 2)
            low(G_PB, G_PB % SLOTS)
            part_low(chunk_src(ZC[0])(0), R_PB, R_PB, T)
            dve.wait_ge(panel_used, G_PA + N_BR)
            dve.wait_ge(gate1_on, 3)
            for b in range(4):
                last = v.tensor_tensor(flatc(MG + 2 * b, 2), flatc(MG + 2 * b, 2), ps[:, b], ALU.mult)
            last.then_inc(gate1_done, 1)
            row_stage(G_PB, N_BR, chunk_src(ZC[0]), R_PB, R_PB, T, begun=True)
            dve.wait_ge(gate1_done, 1)

            def gated(b):
                one, two = flatc(MG + 2 * b, 2), flatc(MG + 8 + 2 * b, 2)
                step(v.tensor_tensor(two, two, ps[:, 4 + b], ALU.mult))
                v.tensor_tensor(one, one, two, ALU.add).then_inc(gate1_done, 1)
                if b == 1:
                    part_low(chunk_src(MG)(0), R_OUT1, R_OUT1, T)
            residual(3, G_PB + N_BR, gated)
            row_stage(G_OUT1, N_OUT, chunk_src(MG), R_OUT1, R_OUT1, T, begun=True)

            def scaled_add(col, b0):
                def add(b):
                    for k in (2 * b, 2 * b + 1):
                        last = v.scalar_tensor_tensor(h[:, k], ps[:, b0 + b, (k % 2) * T:(k % 2 + 1) * T], col(k), h[:, k],
                                                      ALU.mult, ALU.add)
                    last.then_inc(h_set, 1)
                return add
            residual(6, G_OUT1 + N_OUT, scaled_add(mcolumn(5, 0), 0))

            norm(4, h, gcol(4), mcolumn(6, 0), 0)
            up_stage(G_UP2, 1, T)
            dve.wait_ge(hid_done, 2 * KFF)
            row_stage(G_DOWN2, N_DOWN, hid_src(T), R_DOWN2, R_DOWN2, T, last=False, begun=True)
            residual(9, G_DOWN2 + N_DOWN, scaled_add(gcol(7), 4))
            dve.wait_ge(rstd_done, 6)
            for k in range(KD):
                last = v.scalar_tensor_tensor(h[:, k], h[:, k], m1("final", k), rstd[:, 1], ALU.mult, ALU.mult)
                if k % 2:
                    last.then_inc(layer_done, 1)

            with dve.Fori(0, LAYERS) as l:
                link[0], link[1] = l, 0
                first = layer_panel(l, 0)
                low(first[0], first[1] % SLOTS)
                dve.wait_ge(v2_in, at(v2_in, l, 1))
                v.tensor_tensor(scol[:, 32:34], m2("lam_q", 0, 2), m2("lam_k", 0, 2), ALU.mult).then_inc(lam_mul, 1)
                v.tensor_tensor(scol[:, 34:35], m2("subln"), m2("one_less"), ALU.mult)
                norm(0, h, lambda k: m2("attn_norm", k), None, 0, l)
                dve.wait_ge(lam_exp, at(lam_exp, l, 1))
                lstep(v.tensor_tensor(scol[:, 36:37], scol[:, 39:40], scol[:, 38:39], ALU.subtract))
                v.tensor_scalar(scol[:, 40:48], scol[:, 48:56], -1.0, None, ALU.mult)
                v.tensor_tensor(scol[:, 36:37], scol[:, 36:37], m2("lam_init"), ALU.subtract).then_inc(lam_set, 1)
                dve.wait_ge(lam_set, at(lam_set, l, 1))
                def low_next(i):
                    low(l * PER_LAYER + (G_LAYER + i + 1), (G_LAYER + i + 1) % SLOTS)

                def head_scale(n):
                    c, w, gain = ROPES[n][:3]
                    dve.wait_ge(rp_rs, at(rp_rs, l, n + 1))
                    v.scalar_tensor_tensor(flatc(c, w), flatc(c, w), m2(gain), nrs[:, 0:w].rearrange("p c t -> p (c t)"),
                                           ALU.mult, ALU.mult).then_inc(rp_n, 1)

                def head_rope(n):
                    c, w, _, _, cs_, sn = ROPES[n]
                    x = chunks(c, w)
                    dve.wait_ge(rp_rot, at(rp_rot, l, n + 1))
                    def wide(name):
                        return tb(name).unsqueeze(1).to_broadcast([P, w, T])
                    v.tensor_tensor(nrot[:, 0:w], ps[:, 4:6].rearrange("p b (c t) -> p (b c) t", t=T)[:, 0:w], wide(sn),
                                    ALU.mult)
                    lstep(v.tensor_tensor(x, x, wide(cs_), ALU.mult))
                    v.tensor_tensor(flatc(c, w), flatc(c, w), nrot[:, 0:w].rearrange("p c t -> p (c t)"), ALU.add
                                    ).then_inc(rp_done, 1)
                dve.wait_ge(tab_in, 16)
                for i in range(N_HEADS):
                    low_next(i)
                    if i in ROPE_IN:
                        head_rope(ROPE_IN[i])
                    if i in SCALE_IN:
                        head_scale(SCALE_IN[i])
                def stats(n):
                    return smx[:, n % 4]
                def top(n):
                    dve.wait_ge(sc_mm, at(sc_mm, l, n + 1))
                    st = stats(n)
                    lstep(v.tensor_reduce(st[:, 0:2], ps[:, 2 + 2 * (n % 2):4 + 2 * (n % 2), 0:T], AX, ALU.max,
                                          negate=True))
                    v.tensor_scalar(st[:, 2:4], st[:, 0:2], 0.125, None, ALU.mult).then_inc(sc_max, 1)
                def weights(n):
                    dve.wait_ge(sc_exp, at(sc_exp, l, n + 1))
                    st, e = stats(n), ew[n % 2]
                    lstep(v.reciprocal(st[:, 6:8], st[:, 4:6]))
                    if n < 8:
                        lstep(v.tensor_tensor(st[:, 7:8], st[:, 7:8], scol[:, 36:37], ALU.mult))
                        lstep(v.tensor_scalar(e[:, 0], e[:, 0], st[:, 6:7], None, ALU.mult))
                        v.scalar_tensor_tensor(e[:, 0], e[:, 1], st[:, 7:8], e[:, 0], ALU.mult, ALU.add).then_inc(sc_w, 1)
                    else:
                        v.tensor_scalar(e[:, 0], e[:, 0], st[:, 6:7], None, ALU.mult)
                        v.tensor_scalar(e[:, 1], e[:, 1], st[:, 7:8], None, ALU.mult).then_inc(sc_w, 1)
                def decay(g):
                    lstep(v.tensor_scalar(Dm[g % 2].rearrange("p u t -> p (u t)"), tb("ahead"), scol[:, 40 + g:41 + g],
                                          None, ALU.mult))
                    v.scalar_tensor_tensor(Dm[g % 2].rearrange("p u t -> p (u t)"), tb("behind"), scol[:, 44 + g:45 + g],
                                           Dm[g % 2].rearrange("p u t -> p (u t)"), ALU.mult, ALU.add).then_inc(rt_arg, 1)

                def decayed(g):
                    dve.wait_ge(rt_dec, at(rt_dec, l, g + 1))
                    dve.wait_ge(rt_mm, at(rt_mm, l, g + 1))
                    if g >= 2:
                        dve.wait_ge(rt_pv, at(rt_pv, l, g - 1))
                    v.scalar_tensor_tensor(sD[g % 2].rearrange("p u t -> p (u t)"), ps[:, 0], P ** -0.5,
                                           Dm[g % 2].rearrange("p u t -> p (u t)"), ALU.mult, ALU.mult
                                           ).then_inc(rt_mul, 1)
                top(0)
                for n in range(PAIRS):
                    if n + 1 < PAIRS:
                        top(n + 1)
                    weights(n)
                    if N_HEADS + n < N_PROJ:
                        low_next(N_HEADS + n)
                    g = n - (PAIRS - HEADS)
                    if g >= 0:
                        decayed(g)
                    if -1 <= g < HEADS - 1:
                        if g >= 1:
                            dve.wait_ge(rt_mul, at(rt_mul, l, g))
                        decay(g + 1)
                rl = l * R_PER_LAYER + R_LAYER

                def branch_low(n, i):
                    g = O_BR + n * N_BR + i
                    low(layer_panel(l, g)[0], (G_LAYER + g) % SLOTS)

                def branch_part(n, i):
                    j = RO_BR + n * N_BR + i
                    part_low(chunk_src(BRANCHES[n][0])(i), rl + j, R_LAYER + j, T)

                def branch_end(n):
                    return layer_panel(l, O_BR + (n + 1) * N_BR)[0]

                def gated(n, b):
                    gt = GT + BRANCHES[n][1] + 2 * b
                    return v.tensor_tensor(flatc(gt, 2), flatc(gt, 2), ps[:, 4 * (n % 2) + b], ALU.mult)
                dve.wait_ge(pv_out, at(pv_out, l, 8))
                branch_part(0, 0)
                dve.wait_ge(gn_mean, at(gn_mean, l, 1))
                for b in range(2):
                    last = v.scalar_tensor_tensor(flatc(RQ + 2 * b, 2), ps[:, 6 + b], -1.0 / P, flatc(RQ + 2 * b, 2),
                                                  ALU.mult, ALU.add)
                last.then_inc(gn_cen, 1)
                branch_low(0, 1)
                branch_part(0, 1)
                dve.wait_ge(sub_rs, at(sub_rs, l, 1))
                v.scalar_tensor_tensor(flatc(DQ, 4), flatc(DQ, 4), scol[:, 34:35], nrs.rearrange("p c t -> p (c t)"),
                                       ALU.mult, ALU.mult).then_inc(sub_done, 1)
                dve.wait_ge(sub_done, at(sub_done, l, 1))
                branch_low(1, 0)
                branch_part(1, 0)
                branch_low(1, 1)
                branch_part(1, 1)
                dve.wait_ge(gn_rs, at(gn_rs, l, 1))
                for g in range(HEADS):
                    last = v.scalar_tensor_tensor(big[:, RQ + g], big[:, RQ + g], m2("ret_gain", g), nrot[:, g], ALU.mult,
                                                  ALU.mult)
                lstep(last)
                dve.wait_ge(gate_on, at(gate_on, l, 1))
                v.tensor_tensor(flatc(RQ, 4), flatc(RQ, 4), flatc(RG, 4), ALU.mult).then_inc(gn_done, 1)
                dve.wait_ge(panel_used, branch_end(0))
                dve.wait_ge(gate_on, at(gate_on, l, 2))
                for b in range(4):
                    last = gated(0, b)
                last.then_inc(gate_done, 1)
                dve.wait_ge(gn_done, at(gn_done, l, 1))
                branch_low(2, 0)
                branch_part(2, 0)
                branch_low(2, 1)
                branch_part(2, 1)
                dve.wait_ge(panel_used, branch_end(1))
                dve.wait_ge(gate_on, at(gate_on, l, 4))
                dve.wait_ge(gate_done, at(gate_done, l, 1))
                for b in range(4):
                    last = gated(1, b)
                lstep(last)
                v.tensor_tensor(flatc(GT, 8), flatc(GT, 8), flatc(GT + 16, 8), ALU.add).then_inc(gate_done, 1)
                dve.wait_ge(gate_done, at(gate_done, l, 2))
                branch_low(2, 2)

                def gated_last(b):
                    lstep(gated(2, b))
                    v.tensor_tensor(flatc(GT + 2 * b, 2), flatc(GT + 2 * b, 2), flatc(GT + 8 + 2 * b, 2), ALU.add
                                    ).then_inc(gate_done, 1)
                    if b == 1:
                        part_low(chunk_src(GT)(0), rl + RO_OUT, R_LAYER + RO_OUT, T)
                residual(at(sums_out, l, 0, base=12), branch_end(2), gated_last)
                end = row_stage(layer_panel(l, O_OUT), N_OUT, chunk_src(GT), rl + RO_OUT, R_LAYER + RO_OUT, T, begun=True)

                def add_res_done(b):
                    two = h[:, 2 * b:2 * b + 2].rearrange("p c t -> p (c t)")
                    v.tensor_tensor(two, two, ps[:, 4 + b], ALU.add).then_inc(res_done, 1)
                residual(at(sums_out, l, 3, base=12), end, add_res_done)
                norm(1, h, lambda k: m2("mlp_norm", k), None, 0, l)
                low_stage(layer_panel(l, O_MIN), N_MIN)
                part_low(chunk_src(0)(0), rl + RO_MOUT, R_LAYER + RO_MOUT, T)
                end = row_stage(layer_panel(l, O_MOUT), N_MOUT, chunk_src(0), rl + RO_MOUT, R_LAYER + RO_MOUT, T, last=False,
                                begun=True)
                def add_layer_done(b):
                    two = h[:, 2 * b:2 * b + 2].rearrange("p c t -> p (c t)")
                    v.tensor_tensor(two, two, ps[:, 4 + b], ALU.add).then_inc(layer_done, 1)
                residual(at(sums_out, l, 6, base=12), end, add_layer_done)
            assert link[1] == per["dve_link"], link[1]

        @block.scalar
        def _(act):
            a = nc.scalar
            count = [0]
            link = [0, 0]

            def step(ins):
                count[0] += 1
                ins.then_inc(act_chain, 1)
                act.wait_ge(act_chain, count[0])

            def lstep(ins):
                link[1] += 1
                ins.then_inc(act_link, 1)
                act.wait_ge(act_link, at(act_link, link[0], link[1]))

            def log_exp():
                a.preload_act_table_set("natural_log_exp_and_others")

            def rms(dst, src, n, e, st):
                st(a.activation(dst, src, ACT.Ln, bias=eps[:, e:e + 1], scale=1.0 / n))
                return a.activation(dst, dst, ACT.Exp, scale=-0.5)

            def squares(n, src, b):
                sq = bigf[:, (n % 2) * 2048:(n % 2) * 2048 + 2048].rearrange("p (k t) -> p k t", t=T)
                a.activation(sq[:, 2 * b:2 * b + 2], src[:, 2 * b:2 * b + 2], ACT.Square).then_inc(sq_done, 1)

            def norm_rms(n, bank, l=None):
                act.wait_ge(sum_done, n + 1 if l is None else at(sum_done, l, n + 1, base=6))
                rms(rstd[:, n % 2], ps[:, bank, 0:T], D, 0, step if l is None else lstep).then_inc(rstd_done, 1)

            def norm_high(k, n, shift, dst0, l=None):
                tmp = bigf[:, 4096:4096 + KD * T].rearrange("p (k t) -> p k t", t=T)
                c = n * KD + k + 1
                act.wait_ge(norm_scaled, at(norm_scaled, l, c, base=5 * KD) if l is not None else c)
                bias = {} if shift is None else {"bias": shift(k)}
                a.activation(xhi[:, k, dst0:dst0 + T], tmp[:, k], ACT.Identity, **bias).then_inc(norm_hi, 1)

            def norm_parts(n, shift, dst0, l=None):
                for k in range(KD):
                    norm_high(k, n, shift, dst0, l)

            def mcolumn(n, who):
                return lambda k: mcol[:, 8 * n + k, who:who + 1]

            def first_high(src, r_phase, t, free):
                act.wait_ge(x_free, free)
                a.activation(ahi[:, r_phase % 2, :, 0:t], src(0), ACT.Identity).then_inc(act_hi, 1)

            def up_stage(g0, which, t):
                def body(i, g, s):
                    if isinstance(i, int) and i == N_UP - 1:
                        act.wait_ge(hid_done, which * KFF + ROWK)
                        first_high(hid_src(t), (R_DOWN1, R_DOWN2)[which], t, which + 1)
                    act.wait_ge(panel_used, g + 1)
                    a.activation(hid_chunk(i, t), ps[:, 2 * ((s - g0) % UNROLL), 0:t], ACT.Silu).then_inc(silu_done, 1)
                panel_loop(act, g0, N_UP, body)

            def row_stage(first, n, src, r_phase, t, ready=None, begun=False):
                g0, phase = first if isinstance(first, tuple) else (first, first)
                skip = 1 if begun else 0

                def body(i, g, s):
                    if ready is not None:
                        ready(i + skip)
                    act.wait_ge(panel_used, g - 1)
                    j = (r_phase + (s - phase) % UNROLL) % 2
                    a.activation(ahi[:, j, :, 0:t], src(i + skip), ACT.Identity).then_inc(act_hi, 1)
                rest = (g0 + skip, phase + skip) if isinstance(first, tuple) else first + skip
                panel_loop(act, rest, n - skip, body)

            def hid_ready(which):
                return lambda i: act.wait_ge(hid_done, i * ROWK + (which * KFF + ROWK))

            act.dma_start(mat[:], mats).then_inc(small_in, 16)
            act.dma_start(hyin[0:64], hyw).then_inc(hy_in, 16)
            act.dma_start(zfeat, zT).then_inc(hy_in, 16)
            act.dma_start(hwindow.rearrange("p u c -> p (u c)"), window).then_inc(hy_in, 16)
            act.dma_start(ws[:, FILT:FILT + 2048], hyc[:, 0:2048]).then_inc(hy_in, 16)
            act.dma_start(h[:].rearrange("p k t -> p (k t)"), xT).then_inc(x_in, 16)
            act.dma_start(ws[:, 2048:2048 + POS], posemb).then_inc(x_in, 16)
            act.dma_start(ws[:, 0:2048], ctxT).then_inc(x_in, 16)
            act.dma_start(v2all[:], vec2.rearrange("l p n -> p l n")).then_inc(small_in, 16)
            act.wait_ge(vec_in, 16)
            a.activation(scol[:, 0:2 * KD], m1("c", 0, 2 * KD), ACT.Silu).then_inc(c_silu, 1)
            act.wait_ge(c_silu, 1)
            act.wait_ge(c_zero, 1)
            a.activation(cst[:, 0:4 * KD].rearrange("p (k b) -> p k b", b=4)[:, :, 0:2],
                         scol[:, 0:2 * KD].rearrange("p (k b) -> p k b", b=2), ACT.Identity).then_inc(c_silu, 1)
            def spill(o):
                act.wait_ge(kf_done, 4 * (o + 1))
                act.dma_start(spectra[o], Kst.rearrange("p m c -> p (m c)")).then_inc(kf_out, 16)

            def filter_step(q):
                if q in (F_MLP + 1, F_MLP + 3):
                    n = (q - F_MLP) // 2
                    act.wait_ge(fl_arg, n + 1)
                    a.activation(h2[0:64], ang[0:64, 0], ACT.Sin).then_inc(fl_sin, 1)
                for o in range(2):
                    t = q - F_ORDER - o * F_STEPS
                    if t == 2:
                        act.wait_ge(win_mul, 2 * (o + 1))
                        a.activation(absk, kern.rearrange("p u d c -> p (u d c)"), ACT.Abs).then_inc(abs_done, 1)
                    if t == 13 and o == 0:
                        spill(o)

            def high(g, s, turn):
                act.wait_ge(landed[s], (turn + 1) * 16)
                if not isinstance(g, int) or g >= 2:
                    act.wait_ge(panel_used, g - 1)
                a.activation(whi[:, s % 2, PANEL // 2:], landing[:, s, PANEL // 2:], ACT.Identity).then_inc(hi_act, 1)

            def mod_group(i, beside=lambda j: None):
                for j in range(UNROLL):
                    act.wait_ge(panel_used, i * UNROLL + (G_MOD + j + 1))
                    a.activation(mrow[0:4, j], ps[0:4, j % 2, 0:COLS], ACT.Identity).then_inc(mod_copied, 1)
                    if i * UNROLL + j + 2 < N_MOD:
                        high(i * UNROLL + j + 2, (j + 2) % SLOTS, i + (j + 2) // SLOTS)
                    beside(j)
                    filter_step(i * UNROLL + j)
            high(0, 0, 0)
            high(1, 1, 0)
            for i in range(3):
                mod_group(i)
            act.wait_ge(x_in, 48)
            act.wait_ge(const_set, 3)
            for b in range(4):
                act.wait_ge(h_set, b + 1)
                squares(0, h, b)
            for b in range(4):
                squares(1, hc, b)
            mod_group(3)
            log_exp()
            norm_rms(0, 2)
            norm_rms(1, 3)
            act.wait_ge(mod_added, 1 + 2)
            for n, g0 in ((0, 4), (1, 6)):
                for half in range(2):
                    mod_group(g0 + half, lambda j: norm_high(4 * half + j, n, mcolumn(0, n), n * T))
            mod_group(8)
            spill(1)
            act.wait_ge(mod_turned, N_MOD)
            act.dma_start(ws[:, 4096:6144], lbrow).then_inc(lb_in, 16)
            act.dma_start(mask_in, masks).then_inc(mask_landed, 16)
            act.dma_start(dft.rearrange("p u f -> p (u f)"), hyc[:, 0:1024]).then_inc(dft_in, 16)
            act.wait_ge(kf_out, 32)
            up_stage(G_UP1, 0, 2 * T)
            row_stage(G_DOWN1, N_DOWN, hid_src(2 * T), R_DOWN1, 2 * T, hid_ready(0), begun=True)
            log_exp()
            for b in range(4):
                act.wait_ge(h_set, 4 + b + 1)
                squares(2, h, b)
                squares(3, hc, b)
            norm_rms(2, 0)
            norm_rms(3, 1)
            norm_parts(2, mcolumn(3, 0), 0)
            norm_parts(3, mcolumn(3, 1), T)
            def win(i):
                act.wait_ge(panel_used, G_WIN + i + 1)
                two = ps[:, i % 4 if i < N_FIRST else 4 + i % 2].rearrange("p (u n) -> p u n", n=COLS)
                ctx_two = ps[:, 4 + i % 2].rearrange("p (u n) -> p u n", n=COLS)
                if i < 2:
                    a.activation(Vx[:, :, i * COLS:(i + 1) * COLS], two, ACT.Identity)
                    last = a.activation(Vc[:, :, i * COLS:(i + 1) * COLS], ctx_two, ACT.Identity)
                elif i < 6:
                    d, half = divmod(i - 2, 2)
                    a.activation(chunks(KF[d] + 2 * half, 2), two, ACT.Sigmoid)
                    last = a.activation(sc[d][:, :, half * COLS:(half + 1) * COLS], ctx_two, ACT.Sigmoid)
                else:
                    c = Q0 if i < 8 else G0 - 4 if i < 10 else HY - 8 if i < 16 else MG - 20
                    last = a.activation(chunks(c + 2 * (i - 6), 2), two, ACT.Silu if i < 8 else ACT.Identity)
                last.then_inc(win_out, 1)
            for i in range(N_FIRST):
                win(i)
            act.wait_ge(lb_diff, 2)
            a.activation(scol[:, 16:24], scol[:, 16:24], ACT.Sigmoid).then_inc(lb_sig, 1)
            a.activation(lrow[:, 0], lrow[:, 0], ACT.Sigmoid).then_inc(lb_sig, 1)
            log_exp()
            for d in range(2):
                act.wait_ge(cf_done, d + 1)
                if d:
                    act.wait_ge(ckey_done, d)
                a.activation(lgc, sc[d], ACT.Ln).then_inc(cln_done, 1)
                win(N_FIRST + 2 * d)
                act.wait_ge(csum_done, d + 1)
                a.activation(lgc, ps[:, 0:2], ACT.Exp).then_inc(cdec_done, 1)
                win(N_FIRST + 2 * d + 1)
                act.wait_ge(cst_done, d + 1)
                a.activation(s0[d], ps[:, 2 + d].rearrange("p (g e) -> p g e", e=P), ACT.Identity).then_inc(cst_out, 1)
            act.dma_start(idft.rearrange("p m t -> p (m t)"), hyc[:, 2048:3072]).then_inc(idft_in, 16)
            for d in range(2):
                act.wait_ge(xf_done, d + 1)
                a.activation(EMf[d], flatc(KF[d], 4), ACT.Ln).then_inc(xln_done, 1)
            for i in range(4, 7):
                win(N_FIRST + i)
            for m, (d, n) in enumerate(levels[:-1]):
                act.wait_ge(lv_diff, m + 1)
                if n < len(LEVELS):
                    first, second = halves(EMf[m % 2], LEVELS[n])
                    a.activation(second, second, ACT.Exp)
                    a.activation(first, first, ACT.Exp, scale=-1.0).then_inc(lv_exp, 1)
                else:
                    e = EM[m % 2].rearrange("p (g u) s -> p g u s", u=TT)
                    x = XC[d].rearrange("p (g u) s -> p g u s", u=TT)
                    a.activation(e[:, :, 0], e[:, :, 0], ACT.Exp)
                    a.activation(e[:, :, 1], x[:, :, 1, 1 - d:1 - d + P], ACT.Exp).then_inc(lv_exp, 1)
                if m - 2 in beside_level:
                    win(beside_level[m - 2])
            for d in range(2):
                act.wait_ge(qe_diff, d + 1)
                a.activation(EMf[d], EMf[d], ACT.Exp).then_inc(qe_exp, 1)
            act.dma_start(Kf[:, 0].rearrange("p m c -> p (m c)"), spectra[0]).then_inc(kf_in[0], 16)
            act.wait_ge(win_out, N_WIN - 2)
            a.activation(chunks(G0, 4), chunks(G0, 4), ACT.Silu).then_inc(gate1_on, 1)
            log_exp()
            act.wait_ge(o_done, 1)
            a.activation(EMf[0], ps[:, 4:6].rearrange("p b t -> p (b t)"), ACT.Square).then_inc(osq_done, 1)
            act.wait_ge(turn_done, 1)
            a.activation(uT, ps[:, 0:2], ACT.Identity).then_inc(uT_done, 1)
            act.dma_start(Kf[:, 1].rearrange("p m c -> p (m c)"), spectra[1]).then_inc(kf_in[1], 16)
            act.wait_ge(osum_done, 1)
            rms(EMf[1], ps[:, 6:8].rearrange("p b t -> p (b t)"), P, 0, step).then_inc(orstd_done, 1)
            win(N_WIN - 2)
            act.wait_ge(win_out, N_WIN - 1)
            a.activation(chunks(MG, 14), chunks(MG, 14), ACT.Sigmoid).then_inc(gate1_on, 1)
            act.wait_ge(turn_done, 2)
            a.activation(uT, ps[:, 0:2], ACT.Identity).then_inc(uT_done, 1)
            win(N_WIN - 1)
            act.wait_ge(win_out, N_WIN)
            a.activation(chunks(MG + 14, 2), chunks(MG + 14, 2), ACT.Sigmoid).then_inc(gate1_on, 1)
            act.wait_ge(oa_done, 1)
            row_stage(G_PA, N_BR, chunk_src(Q0), R_PA, T)
            act.wait_ge(z_done, 2)
            act.dma_start(tab, tabs).then_inc(tab_in, 16)
            row_stage(G_PB, N_BR, chunk_src(ZC[0]), R_PB, T)
            row_stage(G_OUT1, N_OUT, chunk_src(MG), R_OUT1, T, lambda i: act.wait_ge(gate1_done, 1 + i + 1))
            log_exp()
            for b in range(4):
                act.wait_ge(h_set, 8 + b + 1)
                squares(4, h, b)
            norm_rms(4, 6)
            norm_parts(4, mcolumn(6, 0), 0)
            up_stage(G_UP2, 1, T)
            row_stage(G_DOWN2, N_DOWN, hid_src(T), R_DOWN2, T, hid_ready(1), begun=True)
            log_exp()
            for b in range(4):
                act.wait_ge(h_set, 12 + b + 1)
                squares(5, h, b)
            norm_rms(5, 0)
            for b in range(4):
                act.wait_ge(layer_done, b + 1)
                squares(0, h, b)

            with act.Fori(0, LAYERS) as l:
                link[0], link[1] = l, 0
                log_exp()
                a.activation(v2[:].unsqueeze(1), v2all[:, ds(l, 1), :], ACT.Identity).then_inc(v2_in, 1)
                norm_rms(0, 1, l)
                norm_parts(0, None, 0, l)
                act.wait_ge(v2_in, at(v2_in, l, 1))
                a.activation(scol[:, 48:56], m2("decay", 0, 8), ACT.Exp)
                act.wait_ge(lam_mm, at(lam_mm, l, 1))
                a.activation(scol[:, 38:40], ps[:, 5, 0:2], ACT.Exp).then_inc(lam_exp, 1)
                act.wait_ge(tab_in, 16)
                dests = ((VD, 0), (VD, 1), (VR, 0), (VR, 1), (VG, 0))

                def projected(i):
                    act.wait_ge(panel_used, l * PER_LAYER + (G_LAYER + i + 1))
                    two = ps[:, i % 2].rearrange("p (u n) -> p u n", n=COLS)
                    if i < N_VALUES:
                        dst, k = dests[i]
                        if dst is VG:
                            ins = a.activation(VG, two[:, :, 0:P], ACT.Identity)
                        else:
                            ins = a.activation(dst[:, :, k * COLS:(k + 1) * COLS], two, ACT.Identity)
                    else:
                        ins = a.activation(chunks(PLAIN[i - N_VALUES], 2), two, ACT.Identity)
                    ins.then_inc(proj_out, 1)

                def head_square(n):
                    act.wait_ge(proj_out, at(proj_out, l, (7, 9, 11, 12)[n]))
                    c, w = ROPES[n][:2]
                    a.activation(nsq[:, 0:w], chunks(c, w), ACT.Square).then_inc(rp_sq, 1)

                def head_rms(n):
                    w = ROPES[n][1]
                    act.wait_ge(rp_sum, at(rp_sum, l, n + 1))
                    if n:
                        act.wait_ge(rp_n, at(rp_n, l, n))
                    rms(nrs[:, 0:w], ps[:, 2:4].rearrange("p b (c t) -> p (b c) t", t=T)[:, 0:w], 64, 0, lstep
                        ).then_inc(rp_rs, 1)
                for i in range(N_HEADS):
                    projected(i)
                    if i in RMS_AFTER:
                        head_rms(RMS_AFTER[i])
                    if i in SQUARE_AFTER:
                        head_square(SQUARE_AFTER[i])

                def expo(n):
                    act.wait_ge(sc_max, at(sc_max, l, n + 1))
                    if n >= 2:
                        act.wait_ge(sc_turn, at(sc_turn, l, n - 1))
                    st = smx[:, n % 4]
                    for m in range(2):
                        last = a.activation(ew[n % 2][:, m], ps[:, 2 + 2 * (n % 2) + m, 0:T], ACT.Exp, bias=st[:, 2 + m:3 + m],
                                            scale=0.125, accum_out=st[:, 4 + m:5 + m])
                    last.then_inc(sc_exp, 1)

                def turned(n):
                    act.wait_ge(sc_turn, at(sc_turn, l, n + 1))
                    p, u = divmod(n, 2)
                    if p >= 2:
                        act.wait_ge(pv_mm, at(pv_mm, l, p - 1))
                    k = 1 if n < 8 else 2
                    for m in range(k):
                        last = a.activation(wT[p % 2][:, m, :, u * P:(u + 1) * P],
                                            ps[:, 6, m * T:(m + 1) * T].rearrange("p (k q) -> p k q", q=P),
                                            ACT.Identity)
                    last.then_inc(sc_wT, 1)

                def attended(p):
                    act.wait_ge(pv_mm, at(pv_mm, l, p + 1))
                    a.activation(big[:, DQ + p if p < 4 else GQ + p - 4], ps[:, 7, 0:T], ACT.Identity
                                 ).then_inc(pv_out, 1)

                def retained(f):
                    act.wait_ge(rt_pv, at(rt_pv, l, f + 1))
                    a.activation(big[:, RQ + f], ps[:, 1, 0:T], ACT.Identity).then_inc(rt_out, 1)
                expo(0)
                for n in range(PAIRS):
                    if n + 1 < PAIRS:
                        expo(n + 1)
                    if N_HEADS + n < N_PROJ:
                        projected(N_HEADS + n)
                    g = n - (PAIRS - HEADS)
                    if g >= 0:
                        act.wait_ge(rt_arg, at(rt_arg, l, g + 1))
                        a.activation(Dm[g % 2], Dm[g % 2], ACT.Exp).then_inc(rt_dec, 1)
                    turned(n)
                    if g >= 1:
                        retained(g - 1)
                    if n % 2 and n > 1:
                        attended(n // 2 - 1)
                attended(7)
                retained(HEADS - 1)
                act.wait_ge(pv_out, at(pv_out, l, 8))
                act.wait_ge(rt_out, at(rt_out, l, HEADS))
                a.activation(nsq, chunks(DQ, 4), ACT.Square).then_inc(sub_sq, 1)

                def branch_high(n, i):
                    g, j = O_BR + n * N_BR + i, R_LAYER + RO_BR + n * N_BR + i
                    act.wait_ge(panel_used, layer_panel(l, g)[0] - 1)
                    a.activation(ahi[:, j % 2, :, 0:T], chunk_src(BRANCHES[n][0])(i), ACT.Identity).then_inc(act_hi, 1)
                branch_high(0, 0)
                branch_high(0, 1)
                act.wait_ge(sub_sum, at(sub_sum, l, 1))
                act.wait_ge(rt_mul, at(rt_mul, l, HEADS))
                rms(nrs, ps[:, 4:6].rearrange("p b (c t) -> p (b c) t", t=T), P, 1, lstep).then_inc(sub_rs, 1)
                act.wait_ge(gn_cen, at(gn_cen, l, 1))
                a.activation(nsq, chunks(RQ, 4), ACT.Square).then_inc(gn_sq, 1)
                act.wait_ge(sub_done, at(sub_done, l, 1))
                branch_high(1, 0)
                act.wait_ge(gn_sum, at(gn_sum, l, 1))
                rms(nrot, ps[:, 4:6].rearrange("p b (c t) -> p (b c) t", t=T), P, 1, lstep).then_inc(gn_rs, 1)
                act.wait_ge(proj_out, at(proj_out, l, N_PROJ))
                a.activation(chunks(RG, 4), chunks(RG, 4), ACT.Silu).then_inc(gate_on, 1)
                branch_high(1, 1)
                for _, gt in BRANCHES:
                    a.activation(chunks(GT + gt, 8), chunks(GT + gt, 8), ACT.Sigmoid).then_inc(gate_on, 1)
                act.wait_ge(gn_done, at(gn_done, l, 1))
                branch_high(2, 0)
                branch_high(2, 1)
                row_stage(layer_panel(l, O_OUT), N_OUT, chunk_src(GT), R_LAYER + RO_OUT, T,
                          lambda i: act.wait_ge(gate_done, at(gate_done, l, 2 + i + 1)))
                log_exp()
                for b in range(4):
                    act.wait_ge(res_done, at(res_done, l, b + 1))
                    squares(1, h, b)
                norm_rms(1, 0, l)
                norm_parts(1, None, 0, l)
                mfirst = layer_panel(l, O_MIN)

                def relu2(i, g, s):
                    j = (s - mfirst[1]) % UNROLL
                    act.wait_ge(panel_used, g + 1)
                    a.activation(rtmp[j % 2], ps[:, j], ACT.Relu).then_inc(relu_done, 1)
                    act.wait_ge(relu_done, at(relu_done, l, 1) + i)
                    a.activation(big[:, ds(i * 2, 2), :].rearrange("p c t -> p (c t)"), rtmp[j % 2], ACT.Square
                                 ).then_inc(m_done, 1)
                panel_loop(act, mfirst, N_MIN - UNROLL, relu2)
                for i in range(N_MIN - UNROLL, N_MIN):
                    if i == N_MIN - 1:
                        act.wait_ge(m_done, at(m_done, l, 1))
                        first_high(chunk_src(0), R_LAYER + RO_MOUT, T, at(x_free, l, 1, base=2))
                    relu2(i, layer_panel(l, O_MIN + i)[0], (mfirst[1] + i) % UNROLL)
                row_stage(layer_panel(l, O_MOUT), N_MOUT, chunk_src(0), R_LAYER + RO_MOUT, T,
                          lambda i: act.wait_ge(m_done, at(m_done, l, 1) + i), begun=True)
                for b in range(4):
                    act.wait_ge(layer_done, following(layer_done, l, b + 1))
                    squares(0, h, b)
            assert link[1] == per["act_link"], link[1]

        @block.tensor
        def _(pe):
            mm = nc.tensor.matmul

            def product(out, w_hi, w_lo, x_hi, x_lo, first, last):
                mm(out, w_hi, x_hi, start=first, stop=False, skip_group_check=True)
                mm(out, w_hi, x_lo, start=False, stop=False, skip_group_check=True)
                return mm(out, w_lo, x_hi, start=False, stop=last, skip_group_check=True)

            def feature_panel(s, outs, x0, t):
                for c, out in enumerate(outs):
                    for k in range(KD):
                        at_ = k * COLS + c * P
                        last = product(out, whi[:, s % 2, at_:at_ + P], wlo[:, s % 2, at_:at_ + P], xhi[:, k, x0:x0 + t],
                                       xlo[:, k, x0:x0 + t], k == 0, k == KD - 1)
                return last

            def token_panel(s, outs, x0, n):
                for u, out in enumerate(outs):
                    for k in range(KD):
                        x = slice(x0 + u * P, x0 + (u + 1) * P)
                        c = slice(k * COLS, k * COLS + n)
                        last = product(out, xhi[:, k, x], xlo[:, k, x], whi[:, s % 2, c], wlo[:, s % 2, c], k == 0, k == KD - 1)
                return last

            def row_panel(s, r, outs, t, first, last, by_banks=False, beside=None):
                for j, (out, opens) in enumerate(outs):
                    for k in range(ROWK):
                        w = slice(k * D + j * P, k * D + (j + 1) * P)
                        ins = product(out, whi[:, s % 2, w], wlo[:, s % 2, w], ahi[:, r % 2, k, 0:t], alo[:, r % 2, k, 0:t],
                                      first and opens and k == 0, last and k == ROWK - 1)
                    if by_banks and j % 2 and j < KD - 1:
                        ins.then_inc(sums_out, 1)
                    if beside is not None and j in (5, 6):
                        beside(j - 5)
                return ins

            def streamed(s, outs, x0, t, base, token=False):
                for k in range(KD):
                    pe.wait_ge(norm_lo, base + (k + 1))
                    for c, (out, opens) in enumerate(outs):
                        w = slice(k * COLS, (k + 1) * COLS) if token else slice(k * COLS + c * P, k * COLS + (c + 1) * P)
                        x = slice(x0 + c * P, x0 + (c + 1) * P) if token else slice(x0, x0 + t)
                        a = whi[:, s % 2, w], wlo[:, s % 2, w]
                        b = xhi[:, k, x], xlo[:, k, x]
                        last = product(out, *(b + a if token else a + b), k == 0 and opens, k == KD - 1)
                return last

            def last_panel(s, outs, t):
                for k in range(KD):
                    for c, (out, opens) in enumerate(outs):
                        w = slice(k * COLS + c * P, k * COLS + (c + 1) * P)
                        last = product(out, whi[:, s % 2, w], wlo[:, s % 2, w], xhi[:, k, 0:t], xlo[:, k, 0:t],
                                       k == 0 and opens, k == KD - 1)
                    if k == KD // 2 - 1:
                        last.then_inc(x_free, 1)
                return last

            def opened(outs):
                return [(out, c == 0) for c, out in enumerate(outs)]

            def sums(b0, t=T):
                if t == T:
                    return [(ps[:, b0 + j // 2, (j % 2) * T:(j % 2 + 1) * T], j % 2 == 0) for j in range(KD)]
                return [(ps[:, j, 0:t], True) for j in range(KD)]

            def row_stage(first, n, r0, r_phase, outs, t, by_banks=False, between=lambda: None, beside=None):
                g0, phase = first if isinstance(first, tuple) else (first, first)

                def one(i, g, s, begins, ends):
                    pe.wait_ge(lo_done, g + 1)
                    pe.wait_ge(act_lo, r0 + i + 1)
                    row_panel(s, r_phase + (s - phase) % UNROLL, outs, t, begins, ends, by_banks and ends,
                              beside if ends else None).then_inc(panel_used, 1)
                one(0, g0, phase % UNROLL, True, False)
                between()
                nxt = (g0 + 1, phase + 1) if isinstance(first, tuple) else g0 + 1
                panel_loop(pe, nxt, n - 2, lambda i, g, s: one(i + 1, g, s, False, False))
                one(n - 1, g0 + (n - 1), (phase + n - 1) % UNROLL, False, True)

            def norm_sum(n, bank, b, sq):
                pe.wait_ge(sq_done, sq)
                for k in (2 * b, 2 * b + 1):
                    x = bigf[:, (n % 2) * 2048 + k * T:(n % 2) * 2048 + (k + 1) * T]
                    last = mm(ps[:, bank, 0:T], ones[:], x, start=k == 0, stop=k == KD - 1, skip_group_check=True)
                if b == 3:
                    last.then_inc(sum_done, 1)

            def up_stage(g0, which, t, base=None):
                def one(i, g, s, reused):
                    j = (s - g0) % UNROLL
                    pe.wait_ge(lo_done, g + 1)
                    if reused:
                        pe.wait_ge(hid_done, i + (which * KFF - UNROLL + 1))
                    outs = [ps[:, 2 * j, 0:t], ps[:, 2 * j + 1, 0:t]]
                    if isinstance(i, int) and i == N_UP - 1:
                        last = last_panel(s, [(o, True) for o in outs], t)
                    elif isinstance(i, int) and i == 0 and base is not None:
                        last = streamed(s, [(o, True) for o in outs], 0, t, base)
                    else:
                        last = feature_panel(s, outs, 0, t)
                    last.then_inc(panel_used, 1)
                for i in range(UNROLL):
                    one(i, g0 + i, (g0 + i) % UNROLL, False)
                panel_loop(pe, g0 + UNROLL, N_UP - UNROLL, lambda i, g, s: one(i + UNROLL, g, s, True))

            def halves_of(b):
                return [ps[:, b, 0:T], ps[:, b, T:2 * T]]

            pe.wait_ge(c_split, 1)

            def turn(i, j):
                pe.wait_ge(mod_copied, i * UNROLL + (j + 1))
                if j == 0:
                    pe.wait_ge(mod_added, i + 1)
                pe.wait_ge(small_in, 32)
                fold = mat[0:4, MATS["fold"][0]:MATS["fold"][0] + 2]
                for c in range(2):
                    last = mm(ps[:, 4, 4 * j + 2 * c:4 * j + 2 * c + 2], mrow[0:4, j, c * P:(c + 1) * P], fold, start=True,
                              stop=True)
                last.then_inc(mod_turned, 1)

            def filter_step(q):
                if q == F_MLP:
                    pe.wait_ge(hy_in, 64)
                    mm(ps[0:64, 5, 0:T], hw1, zfeat[0:33], start=True, stop=True).then_inc(fl_mm, 1)
                if q == F_MLP + 2:
                    pe.wait_ge(fl_sin, 1)
                    mm(ps[0:64, 5, 0:T], hw2, h2[0:64], start=True, stop=True).then_inc(fl_mm, 1)
                for o in range(2):
                    t = q - F_ORDER - o * F_STEPS
                    if t in (0, 1):
                        if t:
                            pe.wait_ge(win_mul, 2 * o + 1)
                        elif o:
                            pe.wait_ge(kf_done, 4)
                        else:
                            pe.wait_ge(fl_sin, 2)
                        for d in range(2):
                            last = mm(ps[:, 6 + d], h2[0:64, t * P:(t + 1) * P], hw3[:, (2 * o + d) * 512:(2 * o + d + 1) * 512],
                                      start=True, stop=True)
                        last.then_inc(h3_mm, 1)
                    if t == 3:
                        pe.wait_ge(abs_done, o + 1)
                        for x in range(4):
                            last = mm(ps[:, 5], ones[:], absk[:, x * 512:(x + 1) * 512], start=x == 0, stop=x == 3)
                        last.then_inc(l1_mm, 1)
                    if 4 <= t < 12:
                        m, u = divmod(t - 4, 2)
                        if u == 0:
                            pe.wait_ge(win_mul, 2 * (o + 1))
                            if m >= 2:
                                pe.wait_ge(kf_done, 4 * o + m - 1)
                        for d in range(2):
                            last = mm(ps[:, 6 + m % 2], fdft[:, d, u, m * P:(m + 1) * P], kern[:, u, d], start=u + d == 0,
                                      stop=u + d == 2)
                        if u:
                            last.then_inc(kf_mm, 1)

            def mod_group(i):
                for j in range(UNROLL):
                    pe.wait_ge(lo_done, i * UNROLL + (G_MOD + j + 1))
                    for k in range(KD):
                        c, w = cst[:, 4 * k:4 * k + P], slice(k * COLS, (k + 1) * COLS)
                        out_ = ps[:, j % 2, 0:COLS]
                        mm(out_, c, whi[:, j % 2, w], start=k == 0, stop=False)
                        last = mm(out_, c, wlo[:, j % 2, w], start=False, stop=k == KD - 1)
                    last.then_inc(panel_used, 1)
                    if j:
                        turn(i, j - 1)
                    filter_step(i * UNROLL + j)
                turn(i, UNROLL - 1)

            for i in range(4):
                mod_group(i)
            pe.wait_ge(const_set, 3)
            for n in range(2):
                for b in range(4):
                    norm_sum(n, 2 + n, b, 4 * n + b + 1)
            for i in range(4, N_MOD // UNROLL):
                mod_group(i)

            pe.wait_ge(norm_lo, 2 * KD)
            up_stage(G_UP1, 0, 2 * T)
            pe.wait_ge(hid_done, KFF)
            def both_sums(b):
                for n in range(2):
                    norm_sum(n, n, b, 8 + 2 * b + 2)
            row_stage(G_DOWN1, N_DOWN, R_DOWN1, R_DOWN1, sums(0, 2 * T), 2 * T, by_banks=True, beside=both_sums)
            both_sums(2)
            both_sums(3)

            def win(i):
                g, s = G_WIN + i, (G_WIN + i) % UNROLL
                pe.wait_ge(lo_done, g + 1)
                if i >= 4:
                    pe.wait_ge(win_out, i - 3 if i < N_FIRST else i - 1)
                bank = i % 4 if i < N_FIRST else 4 + i % 2
                if i >= 6:
                    last = feature_panel(s, halves_of(bank), 0, T)
                else:
                    if i >= 2:
                        pe.wait_ge(win_out, i - 1)
                    both = [ps[:, 4 + i % 2, 0:COLS], ps[:, 4 + i % 2, COLS:2 * COLS]]
                    if i == 0:
                        streamed(s, opened([ps[:, bank, 0:COLS], ps[:, bank, COLS:2 * COLS]]), 0, COLS, 2 * KD, token=True)
                        streamed(s, opened(both), T, COLS, 3 * KD, token=True).then_inc(panel_used, 1)
                        return
                    token_panel(s, both, T, COLS)
                    if i < 2:
                        last = token_panel(s, [ps[:, bank, 0:COLS], ps[:, bank, COLS:2 * COLS]], 0, COLS)
                    else:
                        last = feature_panel(s, halves_of(bank), 0, T)
                last.then_inc(panel_used, 1)
            for i in range(N_FIRST):
                win(i)
            pe.wait_ge(win_out, N_FIRST)
            for d, order in enumerate(("after", "before")):
                win(N_FIRST + 2 * d)
                pe.wait_ge(cln_done, d + 1)
                if d:
                    pe.wait_ge(cdec_done, d)
                near, far = d, 1 - d
                mm(ps[:, far], mt(order), lgc[:, far], start=True, stop=True)
                mm(ps[:, near], mt(order), lgc[:, near], start=True, stop=False)
                mm(ps[:, near], ones[:], lgc[:, far], start=False, stop=True).then_inc(csum_done, 1)
                win(N_FIRST + 2 * d + 1)
                pe.wait_ge(ckey_done, d + 1)
                for g in range(HEADS):
                    for u in range(TT):
                        last = mm(ps[:, 2 + d, g * P:(g + 1) * P], sc[d][:, u, g * P:(g + 1) * P], Vc[:, u, g * P:(g + 1) * P],
                                  start=u == 0, stop=u == TT - 1)
                last.then_inc(cst_done, 1)
            q = flatc(Q0, 4)
            for i in range(4, 7):
                win(N_FIRST + i)
            pe.wait_ge(cst_out, 2)
            for m, (d, n) in enumerate(levels):
                if d == 2:
                    pe.wait_ge(lv_diff, m + 1)
                else:
                    pe.wait_ge(lv_mul, m + 1)
                if m >= 2:
                    pe.wait_ge(lv_sel, m - 1)
                e, b = EM[m % 2], 2 * (m % 2)
                for x in range(HEADS * TT):
                    g, u = divmod(x, TT)
                    o = slice(g * P, (g + 1) * P)
                    if d == 2:
                        last = mm(ps[:, b + u, o], e[:, x], q[:, x * P:(x + 1) * P], start=True, stop=True)
                    elif n < len(LEVELS):
                        last = mm(ps[:, b + u, o], e[:, x], e[:, x], start=True, stop=True)
                    elif u == d:
                        last = mm(ps[:, b, o], e[:, x], e[:, 2 * g + 1 - d], start=True, stop=True)
                last.then_inc(lv_score, 1)
                if m in beside_level:
                    win(beside_level[m])
            pe.wait_ge(win_out, N_WIN - 2)
            pe.wait_ge(lv_sel, len(levels))
            for g in range(HEADS):
                for u in range(TT):
                    mm(halves_of(4 + g // 2)[g % 2], Vx[:, u, g * P:(g + 1) * P], S[:, u, g], start=u == 0 and g % 2 == 0,
                       stop=False, skip_group_check=True)
            pe.wait_ge(qe_done, 1)
            for g in range(HEADS):
                for d in range(2):
                    last = mm(halves_of(4 + g // 2)[g % 2], s0[d][:, g], EMf[d][:, g * T:(g + 1) * T], start=False,
                              stop=d == 1, skip_group_check=True)
            last.then_inc(o_done, 1)
            pe.wait_ge(dft_in, 16)
            for o in range(2):
                if o == 0:
                    pe.wait_ge(conv_done, 1)
                else:
                    pe.wait_ge(z_done, 1)
                for c in range(4):
                    for u in range(TT):
                        last = nc.tensor.transpose(ps[:, u, c * P:(c + 1) * P], big[:, ZC[0] + c, u * P:(u + 1) * P], ident)
                last.then_inc(turn_done, 1)
                if o == 0:
                    pe.wait_ge(osq_done, 1)
                    for g in range(HEADS):
                        last = mm(halves_of(6 + g // 2)[g % 2], ones[:], EMf[0][:, g * T:(g + 1) * T], start=True, stop=True)
                    last.then_inc(osum_done, 1)
                pe.wait_ge(uT_done, o + 1)
                for m in range(4):
                    for u in range(TT):
                        last = mm(ps[:, m], dft[:, u, m * P:(m + 1) * P], uT[:, u], start=u == 0, stop=u == 1)
                last.then_inc(uf_mm, 1)
                pe.wait_ge(oa_done, 1)
                win(N_WIN - 2 + o)
                pe.wait_ge(idft_in, 16)
                for m in range(4):
                    if m % 2 == 0:
                        pe.wait_ge(pf_done, 2 * o + m // 2 + 1)
                    for c in range(4):
                        f = (Pf, Pi)[m // 2][:, m % 2, c * P:(c + 1) * P]
                        last = mm(halves_of(6 + c // 2)[c % 2], f, idft[:, m], start=m == 0 and c % 2 == 0, stop=m == 3,
                                  skip_group_check=True)
                last.then_inc(y_mm, 1)
            row_stage(G_PA, N_BR, R_PA, R_PA, sums(0), T)
            row_stage(G_PB, N_BR, R_PB, R_PB, sums(4), T, by_banks=True)
            row_stage(G_OUT1, N_OUT, R_OUT1, R_OUT1, sums(0), T, by_banks=True,
                      beside=lambda b: norm_sum(4, 6, b, 16 + b + 1))
            for b in (2, 3):
                norm_sum(4, 6, b, 16 + b + 1)
            up_stage(G_UP2, 1, T, base=4 * KD)
            pe.wait_ge(hid_done, KFF + 20)
            row_stage(G_DOWN2, N_DOWN, R_DOWN2, R_DOWN2, sums(4), T, by_banks=True,
                      beside=lambda b: norm_sum(5, 0, b, 20 + b + 1))
            for b in (2, 3):
                norm_sum(5, 0, b, 20 + b + 1)
            for b in range(4):
                norm_sum(0, 1, b, 24 + b + 1)

            with pe.Fori(0, LAYERS) as l:
                pe.wait_ge(lam_mul, at(lam_mul, l, 1))
                mm(ps[:, 5, 0:2], ones[:], scol[:, 32:34], start=True, stop=True).then_inc(lam_mm, 1)
                def proj(i):
                    pe.wait_ge(lo_done, l * PER_LAYER + (G_LAYER + i + 1))
                    if i >= 2:
                        pe.wait_ge(proj_out, at(proj_out, l, i - 1))
                    s, j = (G_LAYER + i) % UNROLL, i % 2
                    if i == 0:
                        last = streamed(s, opened(halves_of(j)), 0, COLS, at(norm_lo, l, 0, base=5 * KD), token=True)
                    elif i < N_VALUES:
                        n = COLS if i < 4 else P
                        last = token_panel(s, [ps[:, j, 0:n], ps[:, j, COLS:COLS + n]], 0, n)
                    else:
                        last = feature_panel(s, halves_of(j), 0, T)
                    last.then_inc(panel_used, 1)

                def head_sums(n):
                    c, w = ROPES[n][:2]
                    pe.wait_ge(rp_sq, at(rp_sq, l, n + 1))
                    for x in range(w):
                        last = mm(halves_of(2 + x // 2)[x % 2], mt("block64"), nsq[:, x], start=True, stop=True)
                    last.then_inc(rp_sum, 1)

                def head_rotate(n, out):
                    c, w, gain, rot = ROPES[n][:4]
                    if gain:
                        pe.wait_ge(rp_n, at(rp_n, l, n + 1))
                    else:
                        pe.wait_ge(proj_out, at(proj_out, l, out))
                    if n:
                        pe.wait_ge(rp_done, at(rp_done, l, n))
                    for x in range(w):
                        last = mm(halves_of(4 + x // 2)[x % 2], mt(rot), big[:, c + x], start=True, stop=True)
                    last.then_inc(rp_rot, 1)
                for i in range(N_HEADS):
                    proj(i)
                    if i in ROT_AFTER:
                        head_rotate(*ROT_AFTER[i])
                    if i in SUM_AFTER:
                        head_sums(SUM_AFTER[i])

                def scores(n):
                    if n >= 2:
                        pe.wait_ge(sc_exp, at(sc_exp, l, n - 1))
                    hd, u = divmod(n, 2)
                    qc, kc = (DQ + hd, DK + hd) if n < 8 else (GQ + hd - 4, GK + (hd - 4) // 2)
                    for m in range(2):
                        r = slice(64 * m, 64 * m + 64)
                        last = mm(ps[:, 2 + 2 * (n % 2) + m, 0:T], big[r, qc, u * P:(u + 1) * P], big[r, kc], start=True,
                                  stop=True)
                    last.then_inc(sc_mm, 1)

                def turn_weights(n):
                    pe.wait_ge(sc_w, at(sc_w, l, n + 1))
                    if n >= 1:
                        pe.wait_ge(sc_wT, at(sc_wT, l, n))
                    for x in range(2 if n < 8 else 4):
                        m, k = divmod(x, 2)
                        last = nc.tensor.transpose(ps[:, 6, x * P:(x + 1) * P], ew[n % 2][:, m, k * P:(k + 1) * P], ident)
                    last.then_inc(sc_turn, 1)

                def attend(p):
                    pe.wait_ge(sc_wT, at(sc_wT, l, 2 * p + 2))
                    if p >= 1:
                        pe.wait_ge(pv_out, at(pv_out, l, p))
                    for m in range(1 if p < 4 else 2):
                        for k in range(TT):
                            if p < 4:
                                out_, val = ps[:, 7, 0:T], VD[:, k, p * P:(p + 1) * P]
                            else:
                                kv = (p - 4) // 2
                                out_, val = ps[64 * m:64 * m + 64, 7, 0:T], VG[:, k, kv * 64:kv * 64 + 64]
                            last = mm(out_, val, wT[p % 2][:, m, k], start=k == 0, stop=k == TT - 1)
                    last.then_inc(pv_mm, 1)

                def retention_scores(g):
                    if g == 0:
                        pe.wait_ge(proj_out, at(proj_out, l, N_PROJ))
                    else:
                        pe.wait_ge(rt_mul, at(rt_mul, l, g))
                    for u in range(TT):
                        last = mm(halves_of(0)[u], big[:, RK + g, u * P:(u + 1) * P], big[:, RQ + g], start=True, stop=True)
                    last.then_inc(rt_mm, 1)

                def retain(f):
                    pe.wait_ge(rt_mul, at(rt_mul, l, f + 1))
                    if f >= 1:
                        pe.wait_ge(rt_out, at(rt_out, l, f))
                    for u in range(TT):
                        last = mm(ps[:, 1, 0:T], VR[:, u, f * P:(f + 1) * P], sD[f % 2][:, u], start=u == 0, stop=u == TT - 1)
                    last.then_inc(rt_pv, 1)
                pe.wait_ge(rp_done, at(rp_done, l, len(ROPES)))
                scores(0)
                for n in range(PAIRS):
                    if n + 1 < PAIRS:
                        scores(n + 1)
                    if N_HEADS + n < N_PROJ:
                        proj(N_HEADS + n)
                    g = n - (PAIRS - HEADS)
                    if g >= 0:
                        retention_scores(g)
                    turn_weights(n)
                    if g >= 1:
                        retain(g - 1)
                    if n % 2 and n > 1:
                        attend(n // 2 - 1)
                attend(7)
                retain(HEADS - 1)
                pe.wait_ge(sub_sq, at(sub_sq, l, 1))
                for x in range(4):
                    last = mm(halves_of(4 + x // 2)[x % 2], ones[:], nsq[:, x], start=True, stop=True)
                last.then_inc(sub_sum, 1)
                pe.wait_ge(rt_out, at(rt_out, l, HEADS))
                for x in range(4):
                    last = mm(halves_of(6 + x // 2)[x % 2], ones[:], big[:, RQ + x], start=True, stop=True)
                last.then_inc(gn_mean, 1)
                rl = l * R_PER_LAYER + R_LAYER

                def branch_stage(n, **how):
                    row_stage(layer_panel(l, O_BR + n * N_BR), N_BR, rl + RO_BR + n * N_BR, R_LAYER + RO_BR + n * N_BR,
                              sums(4 * (n % 2)), T, **how)

                def retention_squares():
                    pe.wait_ge(gn_sq, at(gn_sq, l, 1))
                    for x in range(4):
                        last = mm(halves_of(4 + x // 2)[x % 2], ones[:], nsq[:, x], start=True, stop=True)
                    last.then_inc(gn_sum, 1)
                branch_stage(0, between=retention_squares)
                pe.wait_ge(gn_rs, at(gn_rs, l, 1))
                branch_stage(1)
                branch_stage(2, by_banks=True)
                row_stage(layer_panel(l, O_OUT), N_OUT, rl + RO_OUT, R_LAYER + RO_OUT, sums(4), T, by_banks=True,
                          beside=lambda b: norm_sum(1, 0, b, at(sq_done, l, 4 + b + 1, base=24)))
                for b in (2, 3):
                    norm_sum(1, 0, b, at(sq_done, l, 4 + b + 1, base=24))
                mfirst = layer_panel(l, O_MIN)

                def up(i, g, s):
                    pe.wait_ge(lo_done, g + 1)
                    if not isinstance(i, int) or i >= 4:
                        pe.wait_ge(relu_done, at(relu_done, l, 0) + (i - 3))
                    outs = halves_of((s - mfirst[1]) % 4)
                    if isinstance(i, int) and i == 0:
                        last = streamed(s, opened(outs), 0, T, at(norm_lo, l, KD, base=5 * KD))
                    elif isinstance(i, int) and i == N_MIN - 1:
                        last = last_panel(s, opened(outs), T)
                    else:
                        last = feature_panel(s, outs, 0, T)
                    last.then_inc(panel_used, 1)
                for i in range(4):
                    up(i, mfirst[0] + i, (mfirst[1] + i) % UNROLL)
                panel_loop(pe, layer_panel(l, O_MIN + 4), N_MIN - 8, lambda i, g, s: up(i + 4, g, s))
                for i in range(N_MIN - 4, N_MIN):
                    up(i, mfirst[0] + i, (mfirst[1] + i) % UNROLL)
                row_stage(layer_panel(l, O_MOUT), N_MOUT, rl + RO_MOUT, R_LAYER + RO_MOUT, sums(4), T, by_banks=True,
                          beside=lambda b: norm_sum(0, 1, b, following(sq_done, l, b + 1, base=24)))
                for b in (2, 3):
                    norm_sum(0, 1, b, following(sq_done, l, b + 1, base=24))


def _column_panels(w, cols):
    w = w[:, cols] if cols is not None else w
    n = w.shape[1] // COLS
    return w.reshape(KD, P, n, COLS).transpose(2, 1, 0, 3).reshape(n, P, PANEL)


def _row_panels(w):
    n = w.shape[0] // (P * ROWK)
    return w.reshape(n, ROWK, P, D).transpose(0, 2, 1, 3).reshape(n, P, PANEL)


def _cols(x):
    x = np.asarray(x).reshape(-1)
    return x.reshape(-1, P).T


def _pad(x):
    out = np.zeros((P, 1), np.float32)
    out[:x.size, 0] = x.reshape(-1)
    return out


def _up_panels(gate, up):
    both = np.stack([gate.reshape(D, KFF, P), up.reshape(D, KFF, P)], 2).reshape(D, KFF * 2 * P)
    return _column_panels(both, None)


def kernel(**inputs):
    import concourse.bacc as _bacc
    from concourse import mybir as _mybir
    from concourse.bass_utils import run_bass_kernel_spmd as _run

    x = {k: np.asarray(v) for k, v in inputs.items()}
    def first(name):
        return x[name][0]

    panels = [_column_panels(first("mod_w"), None)]
    ffn = [[_up_panels(first("ffn_w_gate")[i], first("ffn_w_up")[i]), _row_panels(first("ffn_w_down")[i])] for i in range(2)]
    panels += ffn[0] + [_column_panels(first("w_in"), None), _row_panels(first("w_proj_a")), _row_panels(first("w_proj_b")),
                        _row_panels(first("w_out"))] + ffn[1]
    at = np.cumsum([0, 512, 512, 512, 512, 512, 512, 512, 512, 128, 128, 3072])
    dq, dk, dv, rq, rk, rv, rg, gq, gk, gv, gates = (np.arange(at[i], at[i + 1]) for i in range(11))
    order = np.concatenate([dv, rv, gv, gv, dq, dk, gq, gk[:64], gk[:64], gk[64:], gk[64:], rq, rk, rg, gates])
    for l in range(LAYERS):
        panels += [_column_panels(x["w_in_2"][l], order)] + [_row_panels(x["w_branch_2"][l][b]) for b in (2, 0, 1)]
        panels += [_row_panels(x["w_out_2"][l]), _column_panels(x["w_mlp_in_2"][l], None), _row_panels(x["w_mlp_out_2"][l])]

    c = np.stack([_cols(x["c"]), _cols(x["c_ctx"])], 2).reshape(P, -1)
    logits = x["hgrn_lb_logits"]
    vec1 = np.concatenate([
        c, _cols(first("mod_b")), _cols(logits[0]), _cols(logits[1]), _cols(first("hgrn_norm_w")), _cols(first("hyena_conv_w")),
        _cols(first("hyena_conv_b")), _cols(first("hyena_bias")), _cols(x["final_norm_w"]), _pad(first("hyena_b1")),
        _pad(first("hyena_freq1")), _pad(first("hyena_b2")), _pad(first("hyena_freq2"))], 1)
    vec2 = []
    for l in range(LAYERS):
        twice = [_cols(np.concatenate([x[n][l], x[n][l]])) for n in ("diff_q_norm_2", "diff_k_norm_2", "gqa_q_norm_2",
                                                                     "gqa_k_norm_2")]
        decay = np.concatenate([x["ret_decay_fwd_2"][l], x["ret_decay_bwd_2"][l]])
        start = 0.8 - 0.6 * math.exp(-0.3 * l)
        vec2.append(np.concatenate(
            [_cols(x["attn_norm_2"][l]), _cols(x["mlp_norm_2"][l])] + twice
            + [_cols(x["diff_subln_2"][l]), _cols(x["ret_group_norm_2"][l]), np.broadcast_to(decay, (P, 8))]
            + [_pad(x[f"diff_lam_{n}_2"][l]) for n in ("q1", "q2", "k1", "k2")]
            + [np.full((P, 1), start, np.float32), np.full((P, 1), 1.0 - start, np.float32)], 1))
    hyw = np.zeros((64, 2176), np.float32)
    hyw[:33, 0:64] = first("hyena_w1")
    hyw[:, 64:128] = first("hyena_w2")
    hyw[:, 128:] = first("hyena_w3")

    def tokens(a):
        return a[0].T.reshape(KD, P, T).transpose(1, 0, 2).reshape(P, KD * T)

    arrays = {
        "stream": np.concatenate(panels, 0), "xT": tokens(x["x"]), "ctxT": tokens(x["ctx"]), "vec1": vec1,
        "vec2": np.stack(vec2), "lbrow": np.broadcast_to(logits.reshape(1, 2048), (P, 2048)), "hyw": hyw,
        **shape_constants(),
    }
    arrays = {f"in_{k}": np.ascontiguousarray(v) for k, v in arrays.items()}
    nc = _bacc.Bacc("TRN2", target_bir_lowering=False, num_devices=1)
    args = {k[3:]: nc.dram_tensor(k, v.shape, _mybir.dt.from_np(v.dtype), kind="ExternalInput").ap()
            for k, v in arrays.items()}
    args["out"] = nc.dram_tensor("out_0", (P, KD * T), _mybir.dt.float32, kind="ExternalOutput").ap()
    args["spectra"] = nc.dram_tensor("spectra", (2, P, 4 * 512), _mybir.dt.float32).ap()
    build(nc, **args)
    r = _run(nc, [arrays], core_ids=[0])
    got = r.results[0]["out_0"]
    return got.reshape(P, KD, T).transpose(2, 1, 0).reshape(1, T, D)
```
